# Optimizing a Trainium2 kernel written in Bass

```python
import math
import jax, jax.numpy as jnp
from jax import lax
import numpy as np
import jax
import jax.numpy as jnp

D_MODEL = 1024
BATCH = 1
SEQ = 256
DEPTH = 1

BRANCH_WIDTH = D_MODEL
N_BRANCH = 3
EPS = 1e-6
NEG_INF = -1e30
FORCED = 1e4

LRU_WIDTH = BRANCH_WIDTH
LRU_BLOCKS = 8
LRU_BLOCK = LRU_WIDTH // LRU_BLOCKS
CONV_WIDTH = 4
LRU_C = 8.0

NSA_HEADS = 16
NSA_KV_HEADS = 4
NSA_GROUP = NSA_HEADS // NSA_KV_HEADS
NSA_HEAD_DIM = BRANCH_WIDTH // NSA_HEADS
NSA_WIDTH = NSA_HEADS * NSA_HEAD_DIM
CMP_BLOCK = 32
CMP_STRIDE = 16
CMP_HIDDEN = 256
SLC_BLOCK = 64
SLC_TOP_N = 8
SLC_Q_BLOCK = 64
WINDOW = 256
Q_BLOCK = 128

GLA_HEADS = 4
GLA_KEY_WIDTH = D_MODEL // 2
GLA_VALUE_WIDTH = BRANCH_WIDTH
GLA_DK = GLA_KEY_WIDTH // GLA_HEADS
GLA_DV = GLA_VALUE_WIDTH // GLA_HEADS
GLA_GATE_RANK = 16
GLA_TAU = 16.0
GLA_CHUNK = 32

REL_BUCKETS = 32
REL_MAX_EXACT = 16
REL_MAX_DIST = 128

D_FF = -(-8 * D_MODEL // (3 * 256)) * 256

IN_SIZES = (
    LRU_WIDTH,
    LRU_WIDTH,
    NSA_WIDTH,
    6 * NSA_KV_HEADS * NSA_HEAD_DIM,
    3 * NSA_HEADS,
    GLA_KEY_WIDTH,
    GLA_KEY_WIDTH,
    GLA_VALUE_WIDTH,
    GLA_VALUE_WIDTH,
    GLA_GATE_RANK,
    N_BRANCH * D_MODEL,
)
IN_WIDTH = sum(IN_SIZES)


def rms_norm(x, g):
    xf = x.astype(jnp.float32)
    y = xf * lax.rsqrt(jnp.mean(xf * xf, axis=-1, keepdims=True) + EPS)
    return (y * g.astype(jnp.float32)).astype(x.dtype)

def rel_bucket(dist):
    n = jnp.maximum(dist, 0)
    nf = jnp.maximum(n, REL_MAX_EXACT).astype(jnp.float32)
    large = REL_MAX_EXACT + (jnp.log(nf / REL_MAX_EXACT) / math.log(REL_MAX_DIST / REL_MAX_EXACT)
                             * (REL_BUCKETS - REL_MAX_EXACT)).astype(jnp.int32)
    large = jnp.minimum(large, REL_BUCKETS - 1)
    return jnp.where(n < REL_MAX_EXACT, n, large)

def rglru_mixer(xa, ga, conv_w, conv_b, w_gates, b_gates, lam):
    B_, S_, _ = xa.shape
    f32 = jnp.float32
    xc = lax.conv_general_dilated(
        xa, conv_w[:, None, :].astype(xa.dtype), window_strides=(1,),
        padding=[(CONV_WIDTH - 1, 0)], dimension_numbers=("NWC", "WIO", "NWC"),
        feature_group_count=LRU_WIDTH) + conv_b
    xb = xc.reshape(B_, S_, LRU_BLOCKS, LRU_BLOCK)
    gates = jnp.einsum("bsnc,knce->kbsne", xb, w_gates).reshape(2, B_, S_, LRU_WIDTH) + b_gates[:, None, None, :]
    r = jax.nn.sigmoid(gates[0].astype(f32))
    i = jax.nn.sigmoid(gates[1].astype(f32))
    log_a = -LRU_C * r * jax.nn.softplus(-lam.astype(f32))
    a = jnp.exp(log_a)
    u = jnp.sqrt(-jnp.expm1(2.0 * log_a)) * (i * xc.astype(f32))

    def combine(left, right):
        a1, b1 = left
        a2, b2 = right
        return a1 * a2, a2 * b1 + b2

    _, h = lax.associative_scan(combine, (a, u), axis=1)
    return h.astype(xa.dtype) * jax.nn.gelu(ga)

def compress_blocks(t, pos_emb, w1, w2):
    B_, G_, S_, hd = t.shape
    r = CMP_BLOCK // CMP_STRIDE
    n_cmp = S_ // CMP_STRIDE - r + 1
    ch = t.reshape(B_, G_, S_ // CMP_STRIDE, CMP_STRIDE, hd)
    blocks = jnp.concatenate([ch[:, :, j:j + n_cmp] for j in range(r)], axis=3) + pos_emb
    return jax.nn.gelu(blocks.reshape(B_, G_, n_cmp, CMP_BLOCK * hd) @ w1) @ w2

def nsa_mixer(q, kv, gate, rel_table, cmp_pos, cmp_w1, cmp_w2):
    B_, S_, _ = q.shape
    G, R, hd = NSA_KV_HEADS, NSA_GROUP, NSA_HEAD_DIM
    f32 = jnp.float32
    q = q.reshape(B_, S_, G, R, hd).transpose(0, 2, 3, 1, 4) * (hd ** -0.5)
    kv = kv.reshape(B_, S_, 6, G, hd).transpose(2, 0, 3, 1, 4)
    k_cmp, v_cmp, k_slc, v_slc, k_win, v_win = kv[0], kv[1], kv[2], kv[3], kv[4], kv[5]
    tbl = rel_table.reshape(REL_BUCKETS, G, R)
    pos = jnp.arange(S_)

    kc = compress_blocks(k_cmp, cmp_pos[0], cmp_w1[0], cmp_w2[0])
    vc = compress_blocks(v_cmp, cmp_pos[1], cmp_w1[1], cmp_w2[1])
    n_cmp = kc.shape[2]
    cmp_end = jnp.arange(n_cmp) * CMP_STRIDE + CMP_BLOCK - 1
    valid_c = cmp_end[None, :] <= pos[:, None]
    bias_c = tbl[rel_bucket(pos[:, None] - cmp_end[None, :])].transpose(2, 3, 0, 1)
    logit_c = jnp.einsum("bgrsd,bgcd->bgrsc", q, kc).astype(f32) + bias_c
    p_c = jax.nn.softmax(jnp.where(valid_c, logit_c, NEG_INF), axis=-1) * valid_c
    o_cmp = jnp.einsum("bgrsc,bgcd->bgrsd", p_c.astype(q.dtype), vc)

    n_slc = S_ // SLC_BLOCK
    top_n = min(SLC_TOP_N, n_slc)
    slc_start = jnp.arange(n_slc) * SLC_BLOCK
    cmp_start = cmp_end - (CMP_BLOCK - 1)
    overlap = jnp.clip(jnp.minimum(cmp_start[:, None] + CMP_BLOCK, slc_start[None, :] + SLC_BLOCK)
                       - jnp.maximum(cmp_start[:, None], slc_start[None, :]), 0).astype(f32) / CMP_BLOCK
    imp = jnp.einsum("bgrsc,cj->bgsj", p_c, overlap)
    blk = jnp.arange(n_slc)[None, :]
    cur = (pos // SLC_BLOCK)[:, None]
    forced = (blk == 0) | (blk == cur) | (blk == cur - 1)
    score = jnp.where(forced, FORCED, jnp.where(blk <= cur, imp, -FORCED))
    _, sel = lax.top_k(score, top_n)

    kb = k_slc.reshape(B_, G, n_slc, SLC_BLOCK, hd)
    vb = v_slc.reshape(B_, G, n_slc, SLC_BLOCK, hd)
    nqs = S_ // SLC_Q_BLOCK
    q_blk = q.reshape(B_, G, R, nqs, SLC_Q_BLOCK, hd).transpose(3, 0, 1, 2, 4, 5)
    sel_blk = sel.reshape(B_, G, nqs, SLC_Q_BLOCK, top_n).transpose(2, 0, 1, 3, 4)
    bi = jnp.arange(B_)[:, None, None, None]
    gi = jnp.arange(G)[None, :, None, None]
    gi5 = jnp.arange(G)[None, :, None, None, None]
    tbl_g = tbl.transpose(1, 0, 2)

    def slc_block(args):
        qb, sb, start = args
        ks = kb[bi, gi, sb]
        vs = vb[bi, gi, sb]
        tq = start + jnp.arange(SLC_Q_BLOCK)
        tk = sb[..., None] * SLC_BLOCK + jnp.arange(SLC_BLOCK)
        dist = tq[:, None, None] - tk
        bias = tbl_g[gi5, rel_bucket(dist)].transpose(0, 1, 5, 2, 3, 4)
        logit = jnp.einsum("bgrqd,bgqnld->bgrqnl", qb, ks).astype(f32) + bias
        logit = jnp.where((dist >= 0)[:, :, None], logit, NEG_INF)
        p = jax.nn.softmax(logit.reshape(B_, G, R, SLC_Q_BLOCK, top_n * SLC_BLOCK), axis=-1)
        p = p.reshape(B_, G, R, SLC_Q_BLOCK, top_n, SLC_BLOCK)
        return jnp.einsum("bgrqnl,bgqnld->bgrqd", p.astype(qb.dtype), vs)

    o_slc = lax.map(slc_block, (q_blk, sel_blk, jnp.arange(nqs) * SLC_Q_BLOCK))
    o_slc = o_slc.transpose(1, 2, 3, 0, 4, 5).reshape(B_, G, R, S_, hd)

    nqb = S_ // Q_BLOCK
    nband = WINDOW // Q_BLOCK + 1

    def band(t):
        tp = jnp.pad(t, ((0, 0), (0, 0), ((nband - 1) * Q_BLOCK, 0), (0, 0)))
        tb = tp.reshape(B_, G, nqb + nband - 1, Q_BLOCK, hd)
        return jnp.concatenate([tb[:, :, j:j + nqb] for j in range(nband)], axis=3)

    kw, vw = band(k_win), band(v_win)
    qi = jnp.arange(Q_BLOCK)
    kj = jnp.arange(nband * Q_BLOCK)
    dist_w = (nband - 1) * Q_BLOCK + qi[:, None] - kj[None, :]
    key_pos = jnp.arange(nqb)[:, None] * Q_BLOCK - (nband - 1) * Q_BLOCK + kj[None, :]
    mask_w = ((dist_w >= 0) & (dist_w < WINDOW))[None] & (key_pos >= 0)[:, None, :]
    bias_w = tbl[rel_bucket(dist_w)].transpose(2, 3, 0, 1)[:, :, None]
    qw = q.reshape(B_, G, R, nqb, Q_BLOCK, hd)
    logit_w = jnp.einsum("bgrnqd,bgnkd->bgrnqk", qw, kw).astype(f32) + bias_w
    p_w = jax.nn.softmax(jnp.where(mask_w, logit_w, NEG_INF), axis=-1)
    o_win = jnp.einsum("bgrnqk,bgnkd->bgrnqd", p_w.astype(q.dtype), vw).reshape(B_, G, R, S_, hd)

    g = jax.nn.sigmoid(gate).reshape(B_, S_, 3, G, R).transpose(2, 0, 3, 4, 1)[..., None]
    o = g[0] * o_cmp + g[1] * o_slc + g[2] * o_win
    return o.transpose(0, 3, 1, 2, 4).reshape(B_, S_, NSA_WIDTH)

def gla_mixer(q, k, v, og, lr, wa2, ba, norm_g):
    B_, S_, _ = q.shape
    f32 = jnp.float32
    nc = S_ // GLA_CHUNK
    log_alpha = jax.nn.log_sigmoid((lr @ wa2 + ba).astype(f32)) / GLA_TAU

    def heads(t, d):
        return t.reshape(B_, nc, GLA_CHUNK, GLA_HEADS, d).transpose(1, 0, 3, 2, 4).astype(f32)

    qh = heads(q, GLA_DK) * (GLA_DK ** -0.5)
    kh = heads(k, GLA_DK)
    vh = heads(v, GLA_DV)
    b = jnp.cumsum(heads(log_alpha, GLA_DK), axis=3)
    q_t = qh * jnp.exp(b)
    k_t = kh * jnp.exp(-b)
    b_last = b[:, :, :, -1:]
    k_end = kh * jnp.exp(b_last - b)
    decay = jnp.exp(b_last[:, :, :, 0])
    causal = jnp.tril(jnp.ones((GLA_CHUNK, GLA_CHUNK), bool))
    att = jnp.where(causal, jnp.einsum("nbhcd,nbhsd->nbhcs", q_t, k_t), 0.0)
    o_intra = jnp.einsum("nbhcs,nbhse->nbhce", att, vh)

    def step(state, xs):
        q_c, ke_c, v_c, dec_c = xs
        o = jnp.einsum("bhcd,bhde->bhce", q_c, state)
        state = state * dec_c[..., None] + jnp.einsum("bhcd,bhce->bhde", ke_c, v_c)
        return state, o

    s0 = jnp.zeros((B_, GLA_HEADS, GLA_DK, GLA_DV), f32)
    _, o_inter = lax.scan(step, s0, (q_t, k_end, vh, decay))
    o = rms_norm(o_intra + o_inter, norm_g)
    o = o.transpose(1, 0, 3, 2, 4).reshape(B_, S_, GLA_VALUE_WIDTH)
    return o.astype(og.dtype) * jax.nn.silu(og)

def hybrid_layer(x, rel_table, norm_g, w_in, conv_w, conv_b, lru_w_gates, lru_b_gates, lru_lambda,
                 cmp_pos, cmp_w1, cmp_w2, gla_wa2, gla_ba, gla_norm, w_branch, w_out, w_ffn_in, w_ffn_out):
    B_, S_, D_ = x.shape
    h = rms_norm(x, norm_g[0])
    proj = h @ w_in
    cuts, acc = [], 0
    for size in IN_SIZES[:-1]:
        acc += size
        cuts.append(acc)
    (lru_x, lru_g, nsa_q, nsa_kv, nsa_gate, gla_q, gla_k, gla_v, gla_og, gla_lr,
     merge_logit) = jnp.split(proj, cuts, axis=-1)
    y_a = rglru_mixer(lru_x, lru_g, conv_w, conv_b, lru_w_gates, lru_b_gates, lru_lambda)
    y_b = nsa_mixer(nsa_q, nsa_kv, nsa_gate, rel_table, cmp_pos, cmp_w1, cmp_w2)
    y_c = gla_mixer(gla_q, gla_k, gla_v, gla_og, gla_lr, gla_wa2, gla_ba, gla_norm)
    gates = jax.nn.sigmoid(merge_logit.reshape(B_, S_, N_BRANCH, D_))
    merged = (gates[:, :, 0] * (y_a @ w_branch[0])
              + gates[:, :, 1] * (y_b @ w_branch[1])
              + gates[:, :, 2] * (y_c @ w_branch[2]))
    x = x + rms_norm(merged @ w_out, norm_g[1])
    h = rms_norm(x, norm_g[2])
    gt, up = jnp.split(h @ w_ffn_in, 2, axis=-1)
    x = x + rms_norm((jax.nn.silu(gt) * up) @ w_ffn_out, norm_g[3])
    return x

def first_inputs(seed: int = 0) -> dict:
    key = jax.random.key(seed)
    ks = jax.random.split(key, 20)
    f32 = jnp.float32

    def nrm(k, shape, scale):
        return jax.random.normal(k, shape, f32) * scale

    u = jax.random.uniform(ks[8], (DEPTH, LRU_WIDTH), f32, 0.9, 0.999)
    s = u ** (1.0 / LRU_C)
    return {
        "x": nrm(ks[0], (BATCH, SEQ, D_MODEL), 1.0),
        "rel_table": nrm(ks[1], (REL_BUCKETS, NSA_HEADS), 0.5),
        "norm_g": 1.0 + nrm(ks[2], (DEPTH, 4, D_MODEL), 0.05),
        "w_in": nrm(ks[3], (DEPTH, D_MODEL, IN_WIDTH), D_MODEL ** -0.5),
        "conv_w": nrm(ks[4], (DEPTH, CONV_WIDTH, LRU_WIDTH), CONV_WIDTH ** -0.5),
        "conv_b": nrm(ks[5], (DEPTH, LRU_WIDTH), 0.01),
        "lru_w_gates": nrm(ks[6], (DEPTH, 2, LRU_BLOCKS, LRU_BLOCK, LRU_BLOCK), LRU_BLOCK ** -0.5),
        "lru_b_gates": nrm(ks[7], (DEPTH, 2, LRU_WIDTH), 0.01),
        "lru_lambda": jnp.log(s) - jnp.log1p(-s),
        "cmp_pos": nrm(ks[9], (DEPTH, 2, CMP_BLOCK, NSA_HEAD_DIM), 0.1),
        "cmp_w1": nrm(ks[10], (DEPTH, 2, CMP_BLOCK * NSA_HEAD_DIM, CMP_HIDDEN), (CMP_BLOCK * NSA_HEAD_DIM) ** -0.5),
        "cmp_w2": nrm(ks[11], (DEPTH, 2, CMP_HIDDEN, NSA_HEAD_DIM), CMP_HIDDEN ** -0.5),
        "gla_wa2": nrm(ks[12], (DEPTH, GLA_GATE_RANK, GLA_KEY_WIDTH), GLA_GATE_RANK ** -0.5),
        "gla_ba": 1.0 + nrm(ks[13], (DEPTH, GLA_KEY_WIDTH), 0.5),
        "gla_norm": 1.0 + nrm(ks[14], (DEPTH, GLA_DV), 0.05),
        "w_branch": nrm(ks[15], (DEPTH, N_BRANCH, BRANCH_WIDTH, D_MODEL), BRANCH_WIDTH ** -0.5),
        "w_out": nrm(ks[16], (DEPTH, D_MODEL, D_MODEL), D_MODEL ** -0.5),
        "w_ffn_in": nrm(ks[17], (DEPTH, D_MODEL, 2 * D_FF), D_MODEL ** -0.5),
        "w_ffn_out": nrm(ks[18], (DEPTH, D_FF, D_MODEL), D_FF ** -0.5),
    }

def first_block(x, rel_table, norm_g, w_in, conv_w, conv_b, lru_w_gates, lru_b_gates, lru_lambda,
              cmp_pos, cmp_w1, cmp_w2, gla_wa2, gla_ba, gla_norm, w_branch, w_out, w_ffn_in, w_ffn_out):
    for l in range(DEPTH):
        x = hybrid_layer(x, rel_table, norm_g[l], w_in[l], conv_w[l], conv_b[l], lru_w_gates[l],
                         lru_b_gates[l], lru_lambda[l], cmp_pos[l], cmp_w1[l], cmp_w2[l],
                         gla_wa2[l], gla_ba[l], gla_norm[l], w_branch[l], w_out[l],
                         w_ffn_in[l], w_ffn_out[l])
    return x


DEPTH_2 = 2

GRID_W = 64
CTX_LEN = 256
HEAD_DIM = 64
MIX_HALF = D_MODEL // 2
N_MOD = 9
D_FF_2 = ((8 * D_MODEL // 3 + 127) // 128) * 128
ROPE_THETA = 10000.0
NEG = -1e30
N_EVEN = (DEPTH_2 + 1) // 2
N_ODD = DEPTH_2 // 2
A_HEADS = MIX_HALF // HEAD_DIM
A_KV_HEADS = A_HEADS // 4
WINDOW_2 = 128
A_BLOCK = 128
A_W = A_HEADS * HEAD_DIM
A_KV = A_KV_HEADS * HEAD_DIM
B_GROUPS = MIX_HALF // HEAD_DIM
B_CHUNK = 128
B_W = B_GROUPS * HEAD_DIM
EVEN_SPLIT = [A_W, A_W + A_KV, A_W + 2 * A_KV, A_W + 2 * A_KV + B_W]
EVEN_IN = A_W + 2 * A_KV + 2 * B_W
EVEN_MIX = A_W + B_W
POOL_WINDOWS = (2, 4, 8, 16)
C_GROUPS = len(POOL_WINDOWS)
C_W = MIX_HALF
C_GROUP_W = C_W // C_GROUPS
D_HEADS = MIX_HALF // HEAD_DIM
D_W = D_HEADS * HEAD_DIM
NA_ROWS = 8
NA_COLS = 16
ODD_SPLIT = [C_W, C_W + D_W, C_W + 2 * D_W]
ODD_IN = C_W + 3 * D_W
ODD_MIX = C_W + D_W


def rms_norm_2(x, g):
    xf = x.astype(jnp.float32)
    y = xf * lax.rsqrt(jnp.mean(xf * xf, axis=-1, keepdims=True) + EPS)
    return (y * g.astype(jnp.float32)).astype(x.dtype)

def norm_mod(h, g, shift, scale):
    return rms_norm_2(h, g) * (1.0 + scale) + shift

def swiglu(x, w_gu, w_down):
    gt, up = jnp.split(x @ w_gu, 2, axis=-1)
    return (jax.nn.silu(gt) * up) @ w_down

def half_ffn(h, g, shift, scale, gate, w_gu, w_down):
    return h + 0.5 * gate * swiglu(norm_mod(h, g, shift, scale), w_gu, w_down)

def axial_rope_angles(s):
    t = jnp.arange(s)
    row = (t // GRID_W).astype(jnp.float32)
    col = (t % GRID_W).astype(jnp.float32)
    m = HEAD_DIM // 4
    inv = 1.0 / (ROPE_THETA ** (jnp.arange(m, dtype=jnp.float32) / m))
    return row[:, None] * inv[None, :], col[:, None] * inv[None, :]

def rotate(x, ang):
    x1, x2 = jnp.split(x, 2, axis=-1)
    cos = jnp.cos(ang)[None, :, None, :]
    sin = jnp.sin(ang)[None, :, None, :]
    return jnp.concatenate([x1 * cos - x2 * sin, x2 * cos + x1 * sin], axis=-1)

def apply_rope_2d(x, ang_r, ang_c):
    half = HEAD_DIM // 2
    return jnp.concatenate([rotate(x[..., :half], ang_r), rotate(x[..., half:], ang_c)], axis=-1).astype(x.dtype)

def ctx_attention(q, k, v, sink):
    b, l, nq, dh = q.shape
    nkv = k.shape[2]
    g = nq // nkv
    qg = q.reshape(b, l, nkv, g, dh)
    sc = jnp.einsum('bqkgd,bskd->bkgqs', qg, k).astype(jnp.float32) * dh ** -0.5
    if sink is not None:
        s_sink = jnp.broadcast_to(sink.astype(jnp.float32).reshape(nkv, g)[None, :, :, None, None], sc.shape[:-1] + (1,))
        sc = jnp.concatenate([sc, s_sink], axis=-1)
    p = jax.nn.softmax(sc, axis=-1)[..., :l].astype(v.dtype)
    o = jnp.einsum('bkgqs,bskd->bqkgd', p, v)
    return o.reshape(b, l, nq * dh)

def window_gqa(q, k, v, k_ctx, v_ctx, sink):
    b, s, nq, dh = q.shape
    nkv = k.shape[2]
    g = nq // nkv
    nb = s // A_BLOCK
    lc = k_ctx.shape[1]
    nloc = 3 * A_BLOCK
    qb = q.reshape(b, nb, A_BLOCK, nkv, g, dh)

    def band(t):
        tb = t.reshape(b, nb, A_BLOCK, nkv, dh)
        pad = jnp.zeros_like(tb[:, :1])
        prev = jnp.concatenate([pad, tb[:, :-1]], axis=1)
        nxt = jnp.concatenate([tb[:, 1:], pad], axis=1)
        return jnp.concatenate([prev, tb, nxt], axis=2)

    kb, vb = band(k), band(v)
    scale = dh ** -0.5
    qpos = jnp.arange(nb)[:, None, None] * A_BLOCK + jnp.arange(A_BLOCK)[None, :, None]
    kpos = (jnp.arange(nb)[:, None, None] - 1) * A_BLOCK + jnp.arange(nloc)[None, None, :]
    valid = (jnp.abs(qpos - kpos) <= WINDOW_2) & (kpos >= 0) & (kpos < s)
    s_loc = jnp.einsum('bnqkgd,bnskd->bnkgqs', qb, kb).astype(jnp.float32) * scale
    s_loc = jnp.where(valid[None, :, None, None], s_loc, NEG)
    s_ctx = jnp.einsum('bnqkgd,bckd->bnkgqc', qb, k_ctx).astype(jnp.float32) * scale
    s_sink = jnp.broadcast_to(sink.astype(jnp.float32).reshape(nkv, g)[None, None, :, :, None, None], s_loc.shape[:-1] + (1,))
    p = jax.nn.softmax(jnp.concatenate([s_loc, s_ctx, s_sink], axis=-1), axis=-1).astype(v.dtype)
    o = (jnp.einsum('bnkgqs,bnskd->bnqkgd', p[..., :nloc], vb)
         + jnp.einsum('bnkgqc,bckd->bnqkgd', p[..., nloc:nloc + lc], v_ctx))
    return o.reshape(b, s, nq * dh)

def chunk_gmlp(bu, bv, v_gain, ws, bias):
    b, s, _ = bu.shape
    u = jax.nn.gelu(bu)
    vv = jax.nn.gelu(bv).reshape(b, s // B_CHUNK, B_CHUNK, B_GROUPS, HEAD_DIM)
    vv = rms_norm_2(vv, v_gain.reshape(B_GROUPS, HEAD_DIM))
    mixed = jnp.einsum('gij,bnjgd->bnigd', ws, vv) + bias.T[None, None, :, :, None]
    return u * mixed.reshape(b, s, B_W)

def multiscale_pool(xp, w_pool, c_scale):
    b, s, _ = xp.shape
    xf = xp.astype(jnp.float32)
    cs = jnp.concatenate([jnp.zeros_like(xf[:, :1]), jnp.cumsum(xf, axis=1)], axis=1)
    t = jnp.arange(s)
    outs = []
    for gi, w in enumerate(POOL_WINDOWS):
        lo = jnp.clip(t - w // 2, 0, s)
        hi = jnp.clip(t + w - w // 2, 0, s)
        csg = cs[..., gi * C_GROUP_W:(gi + 1) * C_GROUP_W]
        mean = (csg[:, hi] - csg[:, lo]) / (hi - lo).astype(jnp.float32)[None, :, None]
        outs.append(mean - xf[..., gi * C_GROUP_W:(gi + 1) * C_GROUP_W])
    pooled = jnp.stack(outs, axis=2).astype(xp.dtype)
    y = jnp.einsum('bsgc,gcd->bsgd', pooled, w_pool).reshape(b, s, C_W)
    return y * c_scale

def neighbourhood_attn(q, k, v, k_ctx, v_ctx, rpb):
    b, s, nh, dh = q.shape
    rows = s // GRID_W
    kr = min(NA_ROWS, rows)
    nqb = GRID_W // NA_COLS
    kbw = 2 * NA_COLS
    q5 = q.reshape(b, rows, GRID_W, nh, dh)
    k5 = k.reshape(b, rows, GRID_W, nh, dh)
    v5 = v.reshape(b, rows, GRID_W, nh, dh)
    qcol = np.arange(GRID_W).reshape(nqb, NA_COLS)
    qstart = np.clip(qcol - NA_COLS // 2, 0, GRID_W - NA_COLS)
    kstart = np.clip(np.arange(nqb) * NA_COLS - NA_COLS // 2, 0, GRID_W - kbw)
    kcol = kstart[:, None] + np.arange(kbw)[None, :]
    col_valid = (kcol[:, None, :] >= qstart[:, :, None]) & (kcol[:, None, :] < qstart[:, :, None] + NA_COLS)
    col_idx = np.clip(kcol[:, None, :] - qcol[:, :, None], 1 - NA_COLS, NA_COLS - 1) + NA_COLS - 1
    scale = dh ** -0.5
    nloc = kr * kbw

    def row_block(r):
        r0 = jnp.clip(r - kr // 2, 0, rows - kr)
        qr = lax.dynamic_index_in_dim(q5, r, axis=1, keepdims=False).reshape(b, nqb, NA_COLS, nh, dh)
        kblk = lax.dynamic_slice_in_dim(k5, r0, kr, axis=1)[:, :, kcol]
        vblk = lax.dynamic_slice_in_dim(v5, r0, kr, axis=1)[:, :, kcol]
        row_idx = r0 + jnp.arange(kr) - r + NA_ROWS - 1
        bias = jnp.transpose(rpb[:, row_idx][:, :, col_idx], (0, 2, 3, 1, 4))
        s_loc = jnp.einsum('bmqhd,brmkhd->bhmqrk', qr, kblk).astype(jnp.float32) * scale + bias[None].astype(jnp.float32)
        s_loc = jnp.where(col_valid[None, None, :, :, None, :], s_loc, NEG)
        s_ctx = jnp.einsum('bmqhd,bchd->bhmqc', qr, k_ctx).astype(jnp.float32) * scale
        p = jax.nn.softmax(jnp.concatenate([s_loc.reshape(b, nh, nqb, NA_COLS, nloc), s_ctx], axis=-1), axis=-1).astype(v.dtype)
        o = (jnp.einsum('bhmqrk,brmkhd->bmqhd', p[..., :nloc].reshape(s_loc.shape), vblk)
             + jnp.einsum('bhmqc,bchd->bmqhd', p[..., nloc:], v_ctx))
        return o.reshape(b, GRID_W, nh, dh)

    out = lax.map(row_block, jnp.arange(rows))
    return jnp.moveaxis(out, 0, 1).reshape(b, s, nh * dh)

def even_mixer(z, zc, w_in, w_out, q_gain, k_gain, sink, v_gain, ws, bias, ang_r, ang_c, need_ctx):
    b, s, _ = z.shape
    l = zc.shape[1]
    q, k, v, bu, bv = jnp.split(z @ w_in, EVEN_SPLIT, axis=-1)
    q = apply_rope_2d(rms_norm_2(q.reshape(b, s, A_HEADS, HEAD_DIM), q_gain), ang_r, ang_c)
    k = apply_rope_2d(rms_norm_2(k.reshape(b, s, A_KV_HEADS, HEAD_DIM), k_gain), ang_r, ang_c)
    v = v.reshape(b, s, A_KV_HEADS, HEAD_DIM)
    if need_ctx:
        qc, kc, vc, buc, bvc = jnp.split(zc @ w_in, EVEN_SPLIT, axis=-1)
    else:
        kc, vc = jnp.split(zc @ w_in[:, A_W:A_W + 2 * A_KV], 2, axis=-1)
    kc = rms_norm_2(kc.reshape(b, l, A_KV_HEADS, HEAD_DIM), k_gain)
    vc = vc.reshape(b, l, A_KV_HEADS, HEAD_DIM)
    y = jnp.concatenate([window_gqa(q, k, v, kc, vc, sink), chunk_gmlp(bu, bv, v_gain, ws, bias)], axis=-1) @ w_out
    yc = None
    if need_ctx:
        qc = rms_norm_2(qc.reshape(b, l, A_HEADS, HEAD_DIM), q_gain)
        yc = jnp.concatenate([ctx_attention(qc, kc, vc, sink), chunk_gmlp(buc, bvc, v_gain, ws, bias)], axis=-1) @ w_out
    return y, yc

def odd_mixer(z, zc, w_in, w_out, w_pool, c_scale, q_gain, k_gain, rpb, need_ctx):
    b, s, _ = z.shape
    l = zc.shape[1]
    xp, q, k, v = jnp.split(z @ w_in, ODD_SPLIT, axis=-1)
    q = rms_norm_2(q.reshape(b, s, D_HEADS, HEAD_DIM), q_gain)
    k = rms_norm_2(k.reshape(b, s, D_HEADS, HEAD_DIM), k_gain)
    v = v.reshape(b, s, D_HEADS, HEAD_DIM)
    if need_ctx:
        xpc, qc, kc, vc = jnp.split(zc @ w_in, ODD_SPLIT, axis=-1)
    else:
        kc, vc = jnp.split(zc @ w_in[:, C_W + D_W:], 2, axis=-1)
    kc = rms_norm_2(kc.reshape(b, l, D_HEADS, HEAD_DIM), k_gain)
    vc = vc.reshape(b, l, D_HEADS, HEAD_DIM)
    y = jnp.concatenate([multiscale_pool(xp, w_pool, c_scale), neighbourhood_attn(q, k, v, kc, vc, rpb)], axis=-1) @ w_out
    yc = None
    if need_ctx:
        qc = rms_norm_2(qc.reshape(b, l, D_HEADS, HEAD_DIM), q_gain)
        yc = jnp.concatenate([multiscale_pool(xpc, w_pool, c_scale), ctx_attention(qc, kc, vc, None)], axis=-1) @ w_out
    return y, yc

def second_inputs(seed: int = 0) -> dict:
    key = jax.random.key(seed)
    ks = jax.random.split(key, 24)
    f32 = jnp.float32

    def nrm(k, shape, sd):
        return jax.random.normal(k, shape, f32) * sd

    d = D_MODEL
    return {
        'x': nrm(ks[0], (BATCH, SEQ, d), 1.0),
        'c': nrm(ks[1], (BATCH, d), 1.0),
        'ctx': nrm(ks[2], (BATCH, CTX_LEN, d), 1.0),
        'c_ctx': nrm(ks[3], (d,), 1.0),
        'ada_w': nrm(ks[4], (DEPTH_2, d, N_MOD * d), 0.5 * d ** -0.5),
        'ada_b': nrm(ks[5], (DEPTH_2, N_MOD * d), 0.02),
        'norm_g': 1.0 + nrm(ks[6], (DEPTH_2, 3, d), 0.05),
        'ffn_w_gu': nrm(ks[7], (DEPTH_2, 2, d, 2 * D_FF_2), d ** -0.5),
        'ffn_w_down': nrm(ks[8], (DEPTH_2, 2, D_FF_2, d), D_FF_2 ** -0.5),
        'ev_w_in': nrm(ks[9], (N_EVEN, d, EVEN_IN), d ** -0.5),
        'ev_w_out': nrm(ks[10], (N_EVEN, EVEN_MIX, d), EVEN_MIX ** -0.5),
        'a_q_gain': 1.0 + nrm(ks[11], (N_EVEN, HEAD_DIM), 0.05),
        'a_k_gain': 1.0 + nrm(ks[12], (N_EVEN, HEAD_DIM), 0.05),
        'a_sink': nrm(ks[13], (N_EVEN, A_HEADS), 0.5),
        'b_v_gain': 1.0 + nrm(ks[14], (N_EVEN, B_W), 0.05),
        'b_ws': nrm(ks[15], (N_EVEN, B_GROUPS, B_CHUNK, B_CHUNK), B_CHUNK ** -0.5),
        'b_bias': 1.0 + nrm(ks[16], (N_EVEN, B_GROUPS, B_CHUNK), 0.1),
        'od_w_in': nrm(ks[17], (N_ODD, d, ODD_IN), d ** -0.5),
        'od_w_out': nrm(ks[18], (N_ODD, ODD_MIX, d), ODD_MIX ** -0.5),
        'c_w_pool': nrm(ks[19], (N_ODD, C_GROUPS, C_GROUP_W, C_GROUP_W), C_GROUP_W ** -0.5),
        'c_scale': 1.0 + nrm(ks[20], (N_ODD, C_W), 0.1),
        'd_q_gain': 1.0 + nrm(ks[21], (N_ODD, HEAD_DIM), 0.05),
        'd_k_gain': 1.0 + nrm(ks[22], (N_ODD, HEAD_DIM), 0.05),
        'd_rpb': nrm(ks[23], (N_ODD, D_HEADS, 2 * NA_ROWS - 1, 2 * NA_COLS - 1), 0.5),
    }

def second_block(x, c, ctx, c_ctx, ada_w, ada_b, norm_g, ffn_w_gu, ffn_w_down,
              ev_w_in, ev_w_out, a_q_gain, a_k_gain, a_sink, b_v_gain, b_ws, b_bias,
              od_w_in, od_w_out, c_w_pool, c_scale, d_q_gain, d_k_gain, d_rpb):
    ang_r, ang_c = axial_rope_angles(x.shape[1])
    sc = jax.nn.silu(c)
    scc = jax.nn.silu(c_ctx)
    h, hc = x, ctx
    for li in range(DEPTH_2):
        need_ctx = li < DEPTH_2 - 1
        m = jnp.split((sc @ ada_w[li] + ada_b[li])[:, None, :], N_MOD, axis=-1)
        mc = jnp.split(scc @ ada_w[li] + ada_b[li], N_MOD, axis=-1)
        h = half_ffn(h, norm_g[li, 0], m[0], m[1], m[2], ffn_w_gu[li, 0], ffn_w_down[li, 0])
        hc = half_ffn(hc, norm_g[li, 0], mc[0], mc[1], mc[2], ffn_w_gu[li, 0], ffn_w_down[li, 0])
        z = norm_mod(h, norm_g[li, 1], m[3], m[4])
        zc = norm_mod(hc, norm_g[li, 1], mc[3], mc[4])
        if li % 2 == 0:
            e = li // 2
            y, yc = even_mixer(z, zc, ev_w_in[e], ev_w_out[e], a_q_gain[e], a_k_gain[e], a_sink[e],
                               b_v_gain[e], b_ws[e], b_bias[e], ang_r, ang_c, need_ctx)
        else:
            o = li // 2
            y, yc = odd_mixer(z, zc, od_w_in[o], od_w_out[o], c_w_pool[o], c_scale[o],
                              d_q_gain[o], d_k_gain[o], d_rpb[o], need_ctx)
        h = h + m[5] * y
        h = half_ffn(h, norm_g[li, 2], m[6], m[7], m[8], ffn_w_gu[li, 1], ffn_w_down[li, 1])
        if need_ctx:
            hc = hc + mc[5] * yc
            hc = half_ffn(hc, norm_g[li, 2], mc[6], mc[7], mc[8], ffn_w_gu[li, 1], ffn_w_down[li, 1])
    return h


def setup_inputs(seed=0):
    out = dict(first_inputs(seed))
    for name, value in second_inputs(seed + 1).items():
        if name != "x":
            out[name + "_2"] = value
    return out


def reference(
    x, rel_table, norm_g, w_in, conv_w, conv_b, lru_w_gates, lru_b_gates, lru_lambda, cmp_pos,
    cmp_w1, cmp_w2, gla_wa2, gla_ba, gla_norm, w_branch, w_out, w_ffn_in, w_ffn_out, c_2, ctx_2,
    c_ctx_2, ada_w_2, ada_b_2, norm_g_2, ffn_w_gu_2, ffn_w_down_2, ev_w_in_2, ev_w_out_2,
    a_q_gain_2, a_k_gain_2, a_sink_2, b_v_gain_2, b_ws_2, b_bias_2, od_w_in_2, od_w_out_2,
    c_w_pool_2, c_scale_2, d_q_gain_2, d_k_gain_2, d_rpb_2,
):
    x = first_block(
        x, rel_table, norm_g, w_in, conv_w, conv_b, lru_w_gates, lru_b_gates, lru_lambda,
        cmp_pos, cmp_w1, cmp_w2, gla_wa2, gla_ba, gla_norm, w_branch, w_out, w_ffn_in,
        w_ffn_out,
    )
    return second_block(
        x, c_2, ctx_2, c_ctx_2, ada_w_2, ada_b_2, norm_g_2, ffn_w_gu_2, ffn_w_down_2, ev_w_in_2,
        ev_w_out_2, a_q_gain_2, a_k_gain_2, a_sink_2, b_v_gain_2, b_ws_2, b_bias_2, od_w_in_2,
        od_w_out_2, c_w_pool_2, c_scale_2, d_q_gain_2, d_k_gain_2, d_rpb_2,
    )


_drawn_inputs = setup_inputs


def setup_inputs(seed=0):
    import zlib

    import numpy as np

    out = dict(_drawn_inputs(seed))
    spreads = {}
    factors = {'lru_b_gates': 8.0,
     'ctx_2': 4.587,
     'ada_b_2': 3.563,
     'norm_g_2': 4.291,
     'a_q_gain_2': 8.0,
     'a_k_gain_2': 8.0,
     'a_sink_2': 8.0,
     'b_v_gain_2': 8.0,
     'b_bias_2': 6.082,
     'c_scale_2': 4.91,
     'd_q_gain_2': 8.0,
     'd_k_gain_2': 8.0,
     'd_rpb_2': 26.713}
    for name, (base, spread) in spreads.items():
        noise = np.random.default_rng([zlib.crc32(name.encode()), seed]).standard_normal(out[name].shape)
        drawn = base * np.exp(spread * noise) if base else spread * noise
        out[name] = jnp.asarray(drawn.astype(out[name].dtype))
    for name, factor in factors.items():
        out[name] = (out[name] * factor).astype(out[name].dtype)
    return out
```

```python
import math
from contextlib import ExitStack

import numpy as np
import concourse.bass as bass
from concourse import mybir

P = 128
D = 1024
KT = D // P
S = 256
CL = 256
TOK = S + CL
FF = 2816
FT = FF // P
FFC = FT // 2
LRU, NSAW, GKW, GVW = 1024, 1024, 512, 1024
HD = 64
CMP_N = S // 16 - 1
NEG = -1e30
EPS = 1e-6
NSLOT = 3
SLOT = FT * 256
W8 = KT * 512
BANK = 512
NG = 4

VEC = [("norm_g", 32), ("conv_w", 32), ("conv_b", 8), ("b_gates", 16), ("lam", 8), ("gla_ba", 4),
       ("gla_norm", 2), ("c", 16), ("ada_b", 144), ("norm_g2", 48), ("qg_ev", 1), ("kg_ev", 1),
       ("qg_od", 1), ("kg_od", 1), ("c_scale", 4), ("sink", 8), ("pos_k", 16), ("pos_v", 16),
       ("w2k", 256), ("w2v", 128), ("w_small", 512), ("wa2", 512), ("tbl", 16)]
CST = [("ident", 128), ("ones", 128), ("blk64", 128), ("flip", 128), ("rope_r", 128),
       ("oh_fwd", 512), ("oh_rev", 384), ("valid_c", 2 * CMP_N), ("gla_mask", 128), ("scan_mask", S),
       ("win_mask", 2 * S), ("na_mask", 2 * S), ("rope_c", S), ("rope_s", S), ("inv_count", 4 * S),
       ("eps", 1), ("one", 1)]


def offsets(table):
    at, out = 0, {}
    for name, n in table:
        out[name] = (at, n)
        at += n
    return out, at


VOFF, VN = offsets(VEC)
COFF, CN = offsets(CST)


def constants():
    c = np.zeros((P, CN), np.float32)

    def put(name, a):
        at, n = COFF[name]
        a = np.asarray(a, np.float32)
        c[:a.shape[0], at:at + n] = a.reshape(a.shape[0], n)

    put("ident", np.eye(P))
    put("ones", np.ones((P, P)))
    put("blk64", np.kron(np.eye(2), np.ones((64, 64))))
    put("flip", np.eye(P)[::-1])
    r = np.zeros((P, P))
    for i in range(P):
        if i % 32 < 16:
            r[i + 16, i] = -1.0
        else:
            r[i - 16, i] = 1.0
    put("rope_r", r)
    n = np.arange(0, 512)
    nf = np.maximum(n, 16).astype(np.float32)
    large = 16 + (np.log(nf / np.float32(16)) / np.float32(math.log(128 / 16)) * np.float32(16)).astype(np.int32)
    bucket = np.where(n < 16, n, np.minimum(large, 31))

    def onehot(dist):
        out = np.zeros((33, len(dist)), np.float32)
        for i, d in enumerate(dist):
            out[bucket[d] if d >= 0 else 32, i] = 1.0
        return out

    put("oh_fwd", onehot(np.arange(512) - 271))
    put("oh_rev", onehot(255 - np.arange(384)))
    t = np.arange(S)
    valid = (16 * np.arange(CMP_N) + 31)[None, :] <= t[:, None]
    put("valid_c", valid.reshape(2, P, CMP_N).transpose(1, 0, 2))
    s_, c_ = np.arange(P)[:, None], np.arange(P)[None, :]
    put("gla_mask", (s_ // 32 == c_ // 32) & (s_ <= c_))
    put("scan_mask", np.broadcast_to((t % 32 != 0), (P, S)))
    win = np.where(np.abs(t[:, None] - t[None, :]) <= 128, 0.0, NEG)
    put("win_mask", win.reshape(2, P, S).transpose(1, 0, 2))
    qc, kc = t[:, None] % 64, t[None, :] % 64
    start = np.clip(qc - 8, 0, 48)
    na = np.where((kc >= start) & (kc < start + 16), 0.0, NEG)
    put("na_mask", na.reshape(2, P, S).transpose(1, 0, 2))
    inv = (1.0 / (np.float32(10000.0) ** (np.arange(16, dtype=np.float32) / np.float32(16)))).astype(np.float32)
    row, col = (t // 64).astype(np.float32), (t % 64).astype(np.float32)
    f = np.arange(P)
    ang = np.where((f % 64 < 32)[:, None], row[None, :], col[None, :]) * inv[f % 16][:, None]
    put("rope_c", np.cos(ang.astype(np.float32)))
    put("rope_s", np.sin(ang.astype(np.float32)))
    cnt = np.stack([np.clip(t + w - w // 2, 0, S) - np.clip(t - w // 2, 0, S) for w in (2, 4, 8, 16)])
    put("inv_count", np.broadcast_to((1.0 / cnt).reshape(1, -1), (P, 4 * S)))
    put("eps", np.full((P, 1), EPS))
    put("one", np.ones((P, 1)))
    return c


def w8(i):
    return ("w8", i, W8)


W8_LRU_X, W8_LRU_G, W8_MERGE_A, W8_GQK, W8_GV, W8_OG, W8_MERGE_C = 0, 2, 4, 8, 10, 12, 14
W8_NQ, W8_KVC, W8_KSW, W8_VSW, W8_CW1, W8_MERGE_B, W8_OUT = 18, 20, 21, 22, 23, 25, 29
W8_FFN = 31
W8_ADA = W8_FFN + 5 * FFC
W8_EQ = W8_ADA + 36
W8_EO = W8_EQ + 3
W8_OD = W8_EO + 2
W8_OO = W8_OD + 4
W8_N = W8_OO + 2


def make_plan():
    plan = []

    def add(stage, chunk, who):
        plan.append((stage, chunk, who))

    def ada(li, a, b):
        for c in range(a, b):
            add(f"ada{li}_{c}", w8(W8_ADA + 18 * li + c), "V")

    def ffn(f):
        for c in range(FFC):
            add(f"ffn{f}_in{c}", w8(W8_FFN + FFC * f + c), "AVAV")
        for c in range(4):
            add(f"ffn{f}_out{c}", ("w22", 4 * f + c, SLOT), "AA" if f == 0 else "VV")

    add("norm0", None, "A")
    for c in range(2):
        add(f"lru_x{c}", w8(W8_LRU_X + c), "AAAA")
    for c in range(2):
        add(f"lru_g{c}", w8(W8_LRU_G + c), "AAAA")
    add("strip", None, "V")
    add("cbias", None, "V")
    add("lru_gates", ("w4", 0, 2048), "A" * 16)
    ada(0, 0, 6)
    for c in range(4):
        add(f"mergeA{c}", w8(W8_MERGE_A + c), "AVAV")
    add("gla_q", w8(W8_GQK), "AAAA")
    add("gla_k", w8(W8_GQK + 1), "AAAA")
    add("gla_lr", None, "A")
    add("gla_al", None, "AAAA")
    for c in range(2):
        add(f"gla_v{c}", w8(W8_GV + c), "VV")
    for c in range(2):
        add(f"gla_og{c}", w8(W8_OG + c), "AAAA")
    ada(0, 6, 12)
    add("gla_t", None, "AA")
    add("gla_att", None, "VV")
    add("gla_o", None, "A" * 8)
    add("gla_n", None, "AAAA")
    for c in range(4):
        add(f"mergeC{c}", w8(W8_MERGE_C + c), "AVAV")
    add("flip", None, "V" * 8)
    for c in range(2):
        add(f"nsa_q{c}", w8(W8_NQ + c), "AAAA")
    add("nsa_kvc", w8(W8_KVC), "AAAA")
    add("nsa_ksw", w8(W8_KSW), "AAAA")
    add("nsa_vsw", w8(W8_VSW), "VV")
    add("nsa_gate", None, "AA")
    for i in range(2):
        add(f"cmp_hid{i}", w8(W8_CW1 + i), "AA")
    add("cmp_kv", None, "VV")
    ada(0, 12, 18)
    for c in range(4):
        add(f"mergeB{c}", w8(W8_MERGE_B + c), "AVAV")
    for c in range(2):
        add(f"w_out{c}", w8(W8_OUT + c), "AAAA")
    add("norm1", None, "A")
    add("norm2", None, "A")
    ffn(0)
    add("norm3", None, "A")
    add("norm4", None, "A")
    ffn(1)
    add("norm5", None, "A")
    add("ev_q", w8(W8_EQ), "AAAA")
    add("ev_k", ("w4", 1, 2048), "A")
    add("ev_v", None, "VVVV")
    add("ev_bv", w8(W8_EQ + 1), "AAAA")
    add("ev_bu", w8(W8_EQ + 2), "AAAA")
    add("ev_qn", None, "A" * 5)
    add("ev_rope", None, "V" * 5)
    add("ev_mix", None, "V" * 4)
    for c in range(2):
        add(f"ev_out{c}", w8(W8_EO + c), "VVVV")
    add("norm6", None, "A")
    ffn(2)
    ada(1, 0, 18)
    add("norm7", None, "A")
    ffn(3)
    add("norm8", None, "A")
    add("od_q", w8(W8_OD), "AAAA")
    add("od_k", w8(W8_OD + 1), "AAAA")
    add("od_v", w8(W8_OD + 2), "VVVV")
    add("od_xp", w8(W8_OD + 3), "AAAA")
    add("od_qn", None, "A" * 8)
    add("od_flip", None, "V" * 8)
    add("od_pool", None, "A" * 4)
    for c in range(2):
        add(f"od_out{c}", w8(W8_OO + c), "VVVV")
    add("norm9", None, "A")
    ffn(4)
    return plan


PLAN = make_plan()
TILE, WHO, CHUNKS, CHUNK_OF = {}, "", [], {}
for _stage, _chunk, _who in PLAN:
    TILE[_stage] = len(WHO)
    WHO += _who
    if _chunk is not None:
        CHUNK_OF[_stage] = len(CHUNKS)
        CHUNKS.append((_chunk, len(WHO) - 1 + (4 if _stage == "ev_k" else 0)))
NTILES = len(WHO)


def emptied(n):
    return WHO[:n + 1].count(WHO[n])


UNITS = ([("nsa", g, t) for g in range(4) for t in range(2)]
         + [("ev", g, t) for g in range(2) for t in range(4)]
         + [("od", g, t) for g in range(2) for t in range(2)])
NSA_U, EV_U, OD_U = (0, 8), (8, 16), (16, 20)


def batches(u):
    kind, _, t = UNITS[u]
    if kind == "nsa":
        return [(seg, b) for seg in range(2) for b in range(t + 1)] + [(2, 0)]
    if kind == "ev" and t >= 2:
        return [(0, 2), (0, 3)]
    return [(0, b) for b in range(4)]


def place(seg, r):
    return 4 * (r % 2) + 2 * seg + r // 2


def batches_before(u):
    return sum(len(batches(v)) for v in range(u))


def build(nc, d, out_x):
    f32 = mybir.dt.float32
    ACT = mybir.ActivationFunctionType
    ALU = mybir.AluOpType
    AX = mybir.AxisListType.X
    ctx = ExitStack()
    with ctx:
        def sb(name, width):
            return ctx.enter_context(nc.sbuf_tensor(name, [P, width], f32))

        xT_ = sb("xT", KT * TOK)
        zT_ = sb("zT", KT * TOK)
        cst = sb("cst", CN)
        vec = sb("vec", VN)
        ring = sb("ring", NSLOT * SLOT)
        rt = sb("rt", TOK)
        rr = sb("rr", TOK)
        mod = sb("mod", 144)
        modA = sb("modA", 48)
        gates_h = sb("gates_h", 32)
        cs = sb("cs", 16)
        small = sb("small", 160)
        ARENA = 20400
        arena = sb("arena", ARENA)
        psum = ctx.enter_context(nc.psum_tensor("psum", [P, 8 * BANK], f32))
        strip_dram = nc.dram_tensor("strip_scratch", (16, 384), f32, kind="Internal").ap()
        rpb_dram = nc.dram_tensor("rpb_scratch", (120, 128), f32, kind="Internal").ap()

        xT = xT_[:, :].rearrange("p (k t) -> p k t", k=KT)
        zT = zT_[:, :].rearrange("p (k t) -> p k t", k=KT)

        def V(name, a=0, n=None):
            at, w = VOFF[name]
            return vec[:, at + a:at + (w if n is None else a + n)]

        def C(name):
            at, w = COFF[name]
            return cst[:, at:at + w]

        def area(at, *shape):
            n = int(np.prod(shape))
            assert at + n <= ARENA, (at, shape)
            v = arena[:, at:at + n]
            if len(shape) == 2:
                return v.rearrange("p (a b) -> p a b", a=shape[0])
            if len(shape) == 3:
                return v.rearrange("p (a b c) -> p a b c", a=shape[0], b=shape[1])
            return v

        def bank(n, width=BANK):
            return psum[:, (n % NG) * BANK:(n % NG) * BANK + width]

        def b3(ap, n, width):
            return ap.unsqueeze(1).to_broadcast([ap.shape[0], n, width])

        def rep(ap, n):
            return ap.unsqueeze(2).to_broadcast([ap.shape[0], ap.shape[1], n])

        sems = {}

        def sig(name):
            if name not in sems:
                sems[name] = ctx.enter_context(nc.semaphore(name))
            return sems[name]

        landed = [sig(f"weights_landed{i}") for i in range(NSLOT)]
        filled = sig("tiles_filled")
        evac = {"A": sig("tiles_emptied_by_act"), "V": sig("tiles_emptied_by_dve")}

        def wait_evac(eng, n):
            eng.wait_ge(evac[WHO[n]], emptied(n))

        def fence(eng, name, others, k):
            eng.drain().then_inc(sig(f"fence_{name}"), 1)
            for o in others:
                eng.wait_ge(sig(f"fence_{o}"), k)

        A_xp = area(0, KT, S + 3)
        A_xc = area(2072, KT, S)
        A_g = area(4120, KT, S)
        A_r = area(6168, KT, S)
        A_i = area(8216, KT, S)
        A_a = area(10264, KT, S)
        A_t = area(12312, KT, S)
        A_y = area(14360, KT, S)
        mg_t = area(16408, 2, S)
        C_q = area(0, 4, S)
        C_k = area(1024, 4, S)
        C_Y = area(2048, 4, S)
        C_e = area(3072, 4, S)
        C_b = area(4096, 4, S)
        C_v = area(5120, 2, GVW)
        C_og = area(7168, KT, S)
        C_kt = area(9216, 8, P)
        C_at = area(10240, 8, P)
        C_st = area(11264, 4, 7 * S)
        C_o = area(2048, KT, S)
        mgC_t = area(9216, 2, S)
        C_lr = area(18432, S)
        B_q = area(0, KT, S)
        B_kk = area(2048, 4, S)
        B_ks = area(3072, 4, S)
        B_kc = area(4096, 4, S)
        B_st = area(5120, 2, 4, S)
        B_bl = area(7168, 2, 16, 60)
        B_hid = area(9088, 2, 2, 60)
        B_stage = area(4096, 16, S)
        B_P = area(4096, 2108)
        B_PT = area(6204, 3, BANK)
        B_T = area(9328, 16, S)
        B_C = area(13424, 2, 16, CMP_N)
        B_v = area(13904, 2, BANK)
        B_y = area(14928, KT, S)
        B_kcT = area(16976, 60)
        B_vc = area(17036, 4, HD)
        B_gate = area(17292, 2, 48)
        mgB_t = area(17400, 2, S)
        K_strip = area(18900, 384)
        K_C = area(19300, 480)
        K_tbl = area(19800, 16)
        Y_y = area(11264, KT, S)
        F_a = area(0, FT, TOK)
        E_qk = area(0, 5, TOK)
        E_ks = area(2560, TOK)
        E_u = area(3072, 4, TOK)
        E_v = area(5120, 4, P)
        E_bv = area(5632, 4, BANK)
        E_y = area(7680, KT, TOK)
        E_P = area(11776, 4 * BANK)
        E_sq = area(11776, 4, BANK)
        E_PT = area(13824, 3, BANK)
        E_w = area(15360, 2048)
        E_rt = area(17408, 5, TOK)
        O_q = area(0, 4, S)
        O_k = area(1024, 4, TOK)
        O_v = area(3072, 4, BANK)
        O_xp = area(5120, 4, S + 16)
        O_s1 = area(6208, 4, S + 16)
        O_s2 = area(7296, 4, S + 16)
        O_y = area(8384, KT, S)
        O_P = area(10432, 4 * BANK)
        O_stage = area(8384, 2 * 8, S)
        O_PT = area(12480, 3, BANK)
        O_nb = area(14016, 2 * 8, S)
        O_wp = area(18112, 4 * P)
        O_tmp = area(18624, 2, TOK)
        PAD = area(19900, 128)

        MODN = {4: (0, TOK), 5: (1, TOK), 6: (2, TOK), 7: (0, TOK), 8: (1, TOK), 9: (2, S)}

        def norm_xr_before(q):
            return KT * sum(1 for p in MODN if p < q)

        def norm_zc_before(q):
            return KT * sum(1 for p, (_, n) in MODN.items() if p < q and n == TOK)

        block = ctx.enter_context(nc.Block())

        @block.sync
        def _(sp):
            for i, ((arr, idx, size), last) in enumerate(CHUNKS):
                if i >= NSLOT:
                    sp.wait_ge(filled, CHUNKS[i - NSLOT][1] + 1)
                slot = i % NSLOT
                sp.dma_start(ring[:, slot * SLOT:slot * SLOT + size], d[arr][idx, :, :])\
                    .then_inc(landed[slot], 16)
            wait_evac(sp, NTILES - 1)
            sp.dma_start(out_x.rearrange("k p t -> p k t"), xT[:, :, 0:S]).then_inc(sig("out_written"), 16)
            sp.wait_ge(sig("out_written"), 16)

        @block.gpsimd
        def _(pool):
            pool.dma_start(xT[:, :, 0:S], d["x"].rearrange("k p t -> p k t")).then_inc(sig("x_in"), 16)
            pool.dma_start(vec[:, :], d["vec"]).then_inc(sig("vec_in"), 16)
            pool.dma_start(cst[:, :], d["cst"]).then_inc(sig("cst_in"), 16)
            pool.dma_start(xT[:, :, S:TOK], d["ctx"].rearrange("k p t -> p k t")).then_inc(sig("ctx_in"), 16)
            pool.memset(K_tbl[32:33, :], NEG).then_inc(sig("tbl_row"), 1)
            pool.dma_start(K_tbl[0:32, :], d["tbl"]).then_inc(sig("tbl_in"), 16)
            wait_evac(pool, TILE["strip"])
            pool.dma_start(strip_dram, K_strip[0:16, :]).then_inc(sig("strip_out"), 16)
            pool.wait_ge(sig("strip_out"), 16)
            fence(pool, "pool", ("pe", "act", "dve"), 1)
            fence(pool, "pool", ("pe", "act", "dve"), 2)
            src = bass.AP(tensor=strip_dram.tensor, offset=0, ap=[[1, P], [384, 16], [1, S]])
            pool.dma_start(B_stage, src).then_inc(sig("stage_in"), 16)
            for c in range(2):
                n = TILE["nsa_kvc"] + 2 * c + 1
                wait_evac(pool, n)
                for g in range(4):
                    half = slice(64 * (g % 2), 64 * (g % 2) + 64)
                    src = B_kc[half, 2 * c + g // 2, :]
                    pool.dma_start(B_st[0:64, c, g, :], src).then_inc(sig("stack_in"), 16)
                    pool.dma_start(B_st[64:128, c, g, 0:S - 1], src[:, 1:S]).then_inc(sig("stack_in"), 16)
            wait_evac(pool, TILE["nsa_ksw"] + 3)
            pool.dma_start(B_ks[0:64, :, :], B_kk[64:128, :, :]).then_inc(sig("kswap_in"), 16)
            pool.dma_start(B_ks[64:128, :, :], B_kk[0:64, :, :]).then_inc(sig("kswap_in"), 16)
            for k in range(3, 5):
                fence(pool, "pool", ("pe", "act", "dve"), k)

            def norm_ctx(q, j):
                for k in range(KT):
                    pool.wait_ge(sig("norm_xr"), norm_xr_before(q) + k + 1)
                    pool.tensor_scalar(out=zT[:, k, S:TOK], in0=zT[:, k, S:TOK],
                                       scalar1=modA[:, 2 * (8 * j + k) + 1:2 * (8 * j + k) + 2],
                                       scalar2=mod[:, 2 * (24 * j + k) + 1:2 * (24 * j + k) + 2],
                                       op0=ALU.mult, op1=ALU.add).then_inc(sig("norm_zc"), 1)

            norm_ctx(4, 0)
            norm_ctx(5, 1)
            fence(pool, "pool", ("pe", "act", "dve"), 5)
            pool.dma_start(E_w, d["ev_small"]).then_inc(sig("ev_small_in"), 16)
            wait_evac(pool, TILE["ev_rope"] + 4)
            pool.dma_start(E_ks[0:64, :], E_qk[64:128, 4, :]).then_inc(sig("ekswap_in"), 16)
            pool.dma_start(E_ks[64:128, :], E_qk[0:64, 4, :]).then_inc(sig("ekswap_in"), 16)
            fence(pool, "pool", ("pe", "act", "dve"), 6)
            norm_ctx(6, 2)
            norm_ctx(7, 0)
            norm_ctx(8, 1)
            fence(pool, "pool", ("pe", "act", "dve"), 7)
            pool.memset(PAD[0:120, :], NEG).then_inc(sig("pad_set"), 1)
            pool.wait_ge(sig("pad_set"), 1)
            pool.dma_start(PAD[0:120, 48:79], d["rpb"]).then_inc(sig("rpb_in"), 16)
            pool.wait_ge(sig("rpb_in"), 16)
            pool.dma_start(rpb_dram, PAD[0:120, :]).then_inc(sig("rpb_out"), 16)
            pool.wait_ge(sig("rpb_out"), 16)
            for t in range(2):
                for r in range(2):
                    for kr in range(4):
                        row = kr - (2 * t + 1 - r) + 7
                        src = bass.AP(tensor=rpb_dram.tensor, offset=row * 128,
                                      ap=[[1, 64], [15 * 128, 8], [1, 64]])
                        pool.dma_start(O_stage[64 * r:64 * r + 64, 8 * t:8 * t + 8, 64 * kr:64 * kr + 64], src)\
                            .then_inc(sig("rpb_stage"), 16)
            pool.dma_start(O_wp, d["pool_w"]).then_inc(sig("pool_w_in"), 16)
            fence(pool, "pool", ("pe", "act", "dve"), 8)

        @block.tensor
        def _(pe):
            mm = nc.tensor.matmul

            def get(stage):
                i = CHUNK_OF[stage]
                pe.wait_ge(landed[i % NSLOT], 16 * (i // NSLOT + 1))
                size = CHUNKS[i][0][2]
                return ring[:, (i % NSLOT) * SLOT:(i % NSLOT) * SLOT + size]

            def open_tile(n):
                if n >= NG:
                    wait_evac(pe, n - NG)
                return bank(n)

            def feature_tiles(stage, w, cols, rhs, nt, nk=KT, first=None):
                for j, c in enumerate(cols):
                    n = TILE[stage] + j
                    b = open_tile(n)
                    for k in range(nk):
                        if j == 0 and first is not None:
                            first(k)
                        last = mm(b[:, 0:nt], w[:, k, c:c + P], rhs(k), start=(k == 0), stop=(k == nk - 1))
                    last.then_inc(filled, 1)

            def token_tiles(stage, w, lhs, ntt, c0, width, nk=KT):
                for j in range(ntt):
                    n = TILE[stage] + j
                    b = open_tile(n)
                    for k in range(nk):
                        last = mm(b[:, 0:width], lhs(k, j), w[:, k, c0:c0 + width],
                                  start=(k == 0), stop=(k == nk - 1))
                    last.then_inc(filled, 1)

            def w3(stage, nk=KT):
                return get(stage).rearrange("p (k n) -> p k n", k=nk)

            def norm(q, nt):
                n = TILE[f"norm{q}"]
                b = open_tile(n)
                for k in range(KT):
                    pe.wait_ge(sig("norm_sq"), KT * q + k + 1)
                    last = mm(b[:, 0:nt], C("ones"), zT[:, k, 0:nt], start=(k == 0), stop=(k == KT - 1))
                last.then_inc(filled, 1)

            def normed(q):
                def first(k):
                    if q in (0, 2):
                        pe.wait_ge(sig("norm_z"), (KT if q == 2 else 0) + k + 1)
                    else:
                        pe.wait_ge(sig("norm_zm"), norm_xr_before(q) + k + 1)
                        if MODN[q][1] == TOK:
                            pe.wait_ge(sig("norm_zc"), norm_zc_before(q) + k + 1)
                return first

            def ada(li, a, b_):
                for c in range(a, b_):
                    stage = f"ada{li}_{c}"
                    w = w3(stage)
                    n = TILE[stage]
                    b = open_tile(n)
                    for j in range(4):
                        for k in range(KT):
                            last = mm(b[:, 2 * j:2 * j + 2], w[:, k, j * P:(j + 1) * P], cs[:, 2 * k:2 * k + 2],
                                      start=(k == 0), stop=(k == KT - 1))
                    last.then_inc(filled, 1)

            def ffn(f, nt, q):
                for c in range(FFC):
                    w = w3(f"ffn{f}_in{c}")
                    feature_tiles(f"ffn{f}_in{c}", w, (0, 256, 128, 384), lambda k: zT[:, k, 0:nt], nt,
                                  first=normed(q) if c == 0 else None)
                for c in range(4):
                    w = w3(f"ffn{f}_out{c}", FT)

                    def first(k):
                        wait_evac(pe, TILE[f"ffn{f}_in{k // 2}"] + 1 + 2 * (k % 2))

                    feature_tiles(f"ffn{f}_out{c}", w, (0, 128), lambda k: F_a[:, k, 0:nt], nt, nk=FT,
                                  first=first if c == 0 else None)

            def merge(br, y, ready):
                for c in range(4):
                    stage = f"merge{br}{c}"
                    w = w3(stage)
                    for j in range(2):
                        for half in range(2):
                            n = TILE[stage] + 2 * j + half
                            b = open_tile(n)
                            if half and c == 0 and j == 0:
                                ready()
                            for k in range(KT):
                                last = mm(b[:, 0:S], w[:, k, 256 * half + P * j:256 * half + P * j + P],
                                          y[:, k, :] if half else zT[:, k, 0:S], start=(k == 0), stop=(k == KT - 1))
                            last.then_inc(filled, 1)

            hrhs = lambda k: zT[:, k, 0:S]

            pe.wait_ge(sig("cst_in"), 16)
            pe.wait_ge(sig("vec_in"), 16)
            norm(0, S)
            for c in range(2):
                feature_tiles(f"lru_x{c}", w3(f"lru_x{c}"), range(0, 512, P), hrhs, S,
                              first=normed(0) if c == 0 else None)
            for c in range(2):
                feature_tiles(f"lru_g{c}", w3(f"lru_g{c}"), range(0, 512, P), hrhs, S)
            pe.wait_ge(sig("tbl_in"), 16)
            pe.wait_ge(sig("tbl_row"), 1)
            oh = C("oh_rev")
            b = open_tile(TILE["strip"])
            mm(b[0:16, 0:384], K_tbl[0:33, :], oh[0:33, :], start=True, stop=True).then_inc(filled, 1)
            oh = C("oh_fwd")
            b = open_tile(TILE["cbias"])
            for t in range(2):
                for c in range(CMP_N):
                    at = P * t - 16 * c - 31 + 271
                    col = (t * CMP_N + c) * 16
                    last = mm(b[:, col:col + 16], oh[0:33, at:at + P], K_tbl[0:33, :], start=True, stop=True)
            last.then_inc(filled, 1)
            w = get("lru_gates").rearrange("p (g n e) -> p g n e", g=2, n=8)
            for k in range(KT):
                pe.wait_ge(sig("lru_xc"), k + 1)
                for g in range(2):
                    n = TILE["lru_gates"] + 2 * k + g
                    b = open_tile(n)
                    mm(b[:, 0:S], w[:, g, k, :], A_xc[:, k, :], start=True, stop=True).then_inc(filled, 1)
            pe.wait_ge(sig("cs_ready"), 1)
            ada(0, 0, 6)
            merge("A", A_y, lambda: pe.wait_ge(sig("lru_y"), KT))
            fence(pe, "pe", ("act", "dve", "pool"), 1)

            feature_tiles("gla_q", w3("gla_q"), range(0, 512, P), hrhs, S)
            feature_tiles("gla_k", w3("gla_k"), range(0, 512, P), hrhs, S)
            wsm = V("w_small").rearrange("p (k n) -> p k n", k=KT)
            b = open_tile(TILE["gla_lr"])
            for k in range(KT):
                last = mm(b[0:16, 0:S], wsm[:, k, 48:64], zT[:, k, 0:S], start=(k == 0), stop=(k == KT - 1))
            last.then_inc(filled, 1)
            wait_evac(pe, TILE["gla_lr"])
            for h in range(4):
                b = open_tile(TILE["gla_al"] + h)
                mm(b[:, 0:S], V("wa2", h * P, P)[0:16, :], C_lr[0:16, :], start=True, stop=True).then_inc(filled, 1)
            for c in range(2):
                token_tiles(f"gla_v{c}", w3(f"gla_v{c}"), lambda k, j: zT[:, k, j * P:(j + 1) * P], 2, 0, 512)
            for c in range(2):
                feature_tiles(f"gla_og{c}", w3(f"gla_og{c}"), range(0, 512, P), hrhs, S)
            ada(0, 6, 12)
            pe.wait_ge(sig("gla_kend"), 1)
            for t in range(2):
                b = open_tile(TILE["gla_t"] + t)
                for h in range(4):
                    last = nc.tensor.transpose(b[:, h * P:(h + 1) * P], C_e[:, h, t * P:(t + 1) * P], C("ident"))
                last.then_inc(filled, 1)
            for t in range(2):
                b = open_tile(TILE["gla_att"] + t)
                for h in range(4):
                    last = mm(b[:, h * P:(h + 1) * P], C_k[:, h, t * P:(t + 1) * P], C_q[:, h, t * P:(t + 1) * P],
                              start=True, stop=True)
                last.then_inc(filled, 1)
            wait_evac(pe, TILE["gla_t"] + 1)
            wait_evac(pe, TILE["gla_v1"] + 1)
            for c in range(7):
                for h in range(4):
                    if c >= 1:
                        pe.wait_ge(sig("gla_state"), 4 * (c - 1) + h + 1)
                    rows = slice(32 * (c % 4), 32 * (c % 4) + 32)
                    mm(psum[:, (4 + h) * BANK:(4 + h) * BANK + S], C_kt[rows, 4 * (c // 4) + h, :],
                       C_v[rows, c // 4, h * S:(h + 1) * S], start=True, stop=True,
                       tile_position=(32 * (c % 4), 0)).then_inc(sig("gla_upd"), 1)
            wait_evac(pe, TILE["gla_att"] + 1)
            pe.wait_ge(sig("gla_state"), 28)
            for h in range(4):
                for e in range(2):
                    n = TILE["gla_o"] + 2 * h + e
                    b = open_tile(n)
                    for t in range(2):
                        mm(b[:, t * P:(t + 1) * P], C_v[:, t, h * S + e * P:h * S + (e + 1) * P],
                           C_at[:, 4 * t + h, :], start=(t == 0), stop=False, skip_group_check=True)
                    for c in range(1, 8):
                        st = C_st[:, h, (c - 1) * S + e * P:(c - 1) * S + (e + 1) * P]
                        last = mm(b[:, 32 * c:32 * c + 32], st, C_q[:, h, 32 * c:32 * c + 32],
                                  start=False, stop=(c == 7), skip_group_check=True)
                    last.then_inc(filled, 1)
            for h in range(4):
                b = open_tile(TILE["gla_n"] + h)
                pe.wait_ge(sig("gla_sq"), 2 * h + 2)
                for e in range(2):
                    last = mm(b[:, 0:S], C("ones"), C_st[:, h, e * S:(e + 1) * S], start=(e == 0), stop=(e == 1))
                last.then_inc(filled, 1)
            merge("C", C_og, lambda: pe.wait_ge(sig("gla_y"), KT))
            fence(pe, "pe", ("act", "dve", "pool"), 2)

            def scores(u):
                kind, g, t = UNITS[u]
                if u > 0:
                    pe.wait_ge(sig("att_exp"), u)
                if kind == "nsa":
                    nk = P * (t + 1)

                    def compressed(a):
                        half = slice(64 * a, 64 * a + 64)
                        for j in range(2):
                            at = 4 * BANK + (2 * a + j) * CMP_N
                            last = mm(psum[:, at:at + CMP_N], B_q[half, 2 * g + j, t * P:(t + 1) * P],
                                      B_kcT[half, g * CMP_N:(g + 1) * CMP_N], start=True, stop=True)
                        return last

                    compressed(0).then_inc(sig("cmp_even"), 1)
                    for r in range(4):
                        half = slice(64 * (r % 2), 64 * (r % 2) + 64)
                        for seg in range(2):
                            kk = (B_kk if g % 2 == r % 2 else B_ks)[half, 2 * seg + g // 2, 0:nk]
                            at = place(seg, r) * S
                            mm(psum[:, at:at + nk], B_q[half, 2 * g + r // 2, t * P:(t + 1) * P], kk,
                               start=True, stop=True)
                    pe.wait_ge(sig("cmp_even"), u + 1)
                    last = compressed(1)
                else:
                    ev = kind == "ev"
                    k0 = S if t >= 2 else 0
                    for r in range(4):
                        h = 4 * g + r
                        half = slice(64 * (r % 2), 64 * (r % 2) + 64)
                        if ev:
                            q = E_qk[half, h // 2, t * P:(t + 1) * P]
                            kk = (E_qk[half, 4, k0:TOK] if g == r % 2 else E_ks[half, k0:TOK])
                        else:
                            q = O_q[half, h // 2, t * P:(t + 1) * P]
                            kk = O_k[half, h // 2, 0:TOK]
                        last = mm(psum[:, r * BANK + k0:(r + 1) * BANK], q, kk, start=True, stop=True)
                last.then_inc(sig("att_score"), 1)

            def att_out(u, Pb, PT):
                kind, g, t = UNITS[u]
                bs = batches(u)
                gb0 = batches_before(u)

                def keys(i):
                    return CMP_N if bs[i][0] == 2 else P

                def turn(i):
                    seg, blk = bs[i]
                    gb = gb0 + i
                    if gb >= 2:
                        pe.wait_ge(sig("att_copied"), gb - 1)
                    pt = psum[:, (5 + gb % 2) * BANK:(6 + gb % 2) * BANK]
                    for r in range(4):
                        if kind == "nsa":
                            at = 2048 + (2 * (r % 2) + r // 2) * CMP_N if seg == 2 else place(seg, r) * S + blk * P
                        else:
                            at = r * BANK + blk * P
                        last = nc.tensor.transpose(pt[0:keys(i), r * P:(r + 1) * P], Pb[:, at:at + keys(i)],
                                                   C("ident"))
                    last.then_inc(sig("att_turned"), 1)

                def multiply(i):
                    seg, blk = bs[i]
                    gb = gb0 + i
                    pe.wait_ge(sig("att_copied"), gb + 1)
                    if i == 0 and u > 0:
                        pe.wait_ge(sig("att_out"), u)
                    pt = PT[0:keys(i), gb % 3, :].rearrange("p (j a t) -> p a j t", j=2, a=2)
                    for a in range(2):
                        o = psum[64 * a:64 * a + 64, 7 * BANK:7 * BANK + 2 * P]
                        if kind == "od":
                            for j in range(2):
                                h = 4 * g + 2 * j + a
                                last = mm(o[:, j * P:(j + 1) * P], O_v[:, blk, h * HD:(h + 1) * HD], pt[:, a, j, :],
                                          start=(i == 0 and j == 0), stop=(i == len(bs) - 1 and j == 1),
                                          skip_group_check=True)
                        else:
                            if kind == "ev":
                                v = E_v[:, blk, g * HD:(g + 1) * HD]
                            elif seg == 2:
                                v = B_vc[0:CMP_N, g, :]
                            else:
                                v = B_v[:, blk, seg * S + g * HD:seg * S + (g + 1) * HD]
                            last = mm(o.rearrange("p (j t) -> p j t", j=2), v, pt[:, a, :, :],
                                      start=(i == 0), stop=(i == len(bs) - 1), skip_group_check=True)
                    last.then_inc(sig("att_mult"), 1)

                pe.wait_ge(sig("att_p"), u + 1)
                for i in range(len(bs)):
                    turn(i)
                    if i >= 1:
                        multiply(i - 1)
                multiply(len(bs) - 1)

            def attention(u0, u1, Pb, PT, ready):
                ready()
                scores(u0)
                for u in range(u0, u1):
                    if u + 1 < u1:
                        scores(u + 1)
                    att_out(u, Pb, PT)

            pe.wait_ge(sig("stage_in"), 16)
            for i in range(8):
                b = open_tile(TILE["flip"] + i)
                mm(b[:, :], C("flip"), area(4096 + i * BANK, BANK), start=True, stop=True).then_inc(filled, 1)
            for c in range(2):
                feature_tiles(f"nsa_q{c}", w3(f"nsa_q{c}"), range(0, 512, P), hrhs, S)
            feature_tiles("nsa_kvc", w3("nsa_kvc"), range(0, 512, P), hrhs, S)
            feature_tiles("nsa_ksw", w3("nsa_ksw"), range(0, 512, P), hrhs, S)
            token_tiles("nsa_vsw", w3("nsa_vsw"), lambda k, j: zT[:, k, j * P:(j + 1) * P], 2, 0, 512)
            token_tiles("nsa_gate", wsm, lambda k, j: zT[:, k, j * P:(j + 1) * P], 2, 0, 48)
            for i in range(2):
                w = w3(f"cmp_hid{i}", 16)
                pe.wait_ge(sig("cmp_blocks"), 4 * i + 4)
                for hh in range(2):
                    n = TILE[f"cmp_hid{i}"] + hh
                    b = open_tile(n)
                    for m in range(16):
                        last = mm(b[:, 0:60], w[:, m, hh * P:(hh + 1) * P], B_bl[:, i, m, :],
                                  start=(m == 0), stop=(m == 15))
                    last.then_inc(filled, 1)
            wait_evac(pe, TILE["cmp_hid1"] + 1)
            b = open_tile(TILE["cmp_kv"])
            w2k = V("w2k").rearrange("p (k n) -> p k n", k=2)
            w2v = V("w2v").rearrange("p (k n) -> p k n", k=2)
            for k in range(2):
                last = mm(b[:, 0:60], w2k[:, k, :], B_hid[:, 0, k, :], start=(k == 0), stop=(k == 1))
            last.then_inc(filled, 1)
            b = open_tile(TILE["cmp_kv"] + 1)
            for g in range(4):
                for k in range(2):
                    last = mm(b[0:CMP_N, g * HD:(g + 1) * HD], B_hid[:, 1, k, g * CMP_N:(g + 1) * CMP_N],
                              w2v[:, k, :], start=(k == 0), stop=(k == 1))
            last.then_inc(filled, 1)
            ada(0, 12, 18)

            def nsa_ready():
                wait_evac(pe, TILE["ada0_17"])
                wait_evac(pe, TILE["nsa_gate"] + 1)
                pe.wait_ge(sig("kswap_in"), 32)

            fence(pe, "pe", ("act", "dve", "pool"), 3)
            attention(*NSA_U, B_P, B_PT, nsa_ready)
            merge("B", B_y, lambda: pe.wait_ge(sig("att_out"), NSA_U[1]))
            wait_evac(pe, TILE["mergeB3"] + 3)
            for c in range(2):
                feature_tiles(f"w_out{c}", w3(f"w_out{c}"), range(0, 512, P), lambda k: zT[:, k, S:TOK], S)
            norm(1, S)
            norm(2, S)
            fence(pe, "pe", ("act", "dve", "pool"), 4)
            ffn(0, S, 2)
            norm(3, S)

            norm(4, TOK)
            ffn(1, TOK, 4)
            norm(5, TOK)
            fence(pe, "pe", ("act", "dve", "pool"), 5)
            feature_tiles("ev_q", w3("ev_q"), range(0, 512, P), lambda k: zT[:, k, :], TOK, first=normed(5))
            wkv = w3("ev_k")
            feature_tiles("ev_k", wkv, (0,), lambda k: zT[:, k, :], TOK)
            tok = lambda k, j: zT[:, k, j * P:(j + 1) * P]
            token_tiles("ev_v", wkv, tok, 4, P, P)
            token_tiles("ev_bv", w3("ev_bv"), tok, 4, 0, 512)
            feature_tiles("ev_bu", w3("ev_bu"), range(0, 512, P), lambda k: zT[:, k, :], TOK)
            for j in range(5):
                b = open_tile(TILE["ev_qn"] + j)
                pe.wait_ge(sig("head_sq"), j + 1)
                mm(b[:, :], C("blk64"), E_rt[:, j, :], start=True, stop=True).then_inc(filled, 1)
            for j in range(5):
                b = open_tile(TILE["ev_rope"] + j)
                pe.wait_ge(sig("head_n"), j + 1)
                mm(b[:, 0:S], C("rope_r"), E_qk[:, j, 0:S], start=True, stop=True).then_inc(filled, 1)
            pe.wait_ge(sig("ev_small_in"), 16)
            pe.wait_ge(sig("ev_vv"), 4)
            wsT = E_w[:, 1024:2048].rearrange("p (g i) -> p g i", g=8)
            for jp in range(4):
                b = open_tile(TILE["ev_mix"] + jp)
                for a in range(2):
                    g = 2 * jp + a
                    for t in range(4):
                        last = mm(b[64 * a:64 * a + 64, t * P:(t + 1) * P], E_bv[:, t, g * HD:(g + 1) * HD],
                                  wsT[:, g, :], start=True, stop=True)
                last.then_inc(filled, 1)

            def ev_ready():
                pe.wait_ge(sig("ekswap_in"), 32)
                wait_evac(pe, TILE["ev_rope"] + 4)
                wait_evac(pe, TILE["ev_mix"] + 3)
                wait_evac(pe, TILE["ev_v"] + 3)

            attention(*EV_U, E_P, E_PT, ev_ready)
            pe.wait_ge(sig("att_out"), EV_U[1])
            pe.wait_ge(sig("mix_y"), 4)
            for c in range(2):
                feature_tiles(f"ev_out{c}", w3(f"ev_out{c}"), range(0, 512, P), lambda k: E_y[:, k, :], TOK)
            fence(pe, "pe", ("act", "dve", "pool"), 6)
            norm(6, TOK)
            ffn(2, TOK, 6)
            ada(1, 0, 18)

            norm(7, TOK)
            ffn(3, TOK, 7)
            norm(8, TOK)
            fence(pe, "pe", ("act", "dve", "pool"), 7)
            feature_tiles("od_q", w3("od_q"), range(0, 512, P), hrhs, S, first=normed(8))
            feature_tiles("od_k", w3("od_k"), range(0, 512, P), lambda k: zT[:, k, :], TOK)
            token_tiles("od_v", w3("od_v"), tok, 4, 0, 512)
            feature_tiles("od_xp", w3("od_xp"), range(0, 512, P), hrhs, S)
            for j in range(8):
                b = open_tile(TILE["od_qn"] + j)
                nt = S if j < 4 else TOK
                pe.wait_ge(sig("head_sq"), 5 + j + 1)
                mm(b[:, 0:nt], C("blk64"), O_tmp[:, j % 2, 0:nt], start=True, stop=True).then_inc(filled, 1)
            pe.wait_ge(sig("rpb_stage"), 16 * 16)
            for i in range(8):
                b = open_tile(TILE["od_flip"] + i)
                mm(b[:, :], C("flip"), area(8384 + i * BANK, BANK), start=True, stop=True).then_inc(filled, 1)
            pe.wait_ge(sig("pool_w_in"), 16)
            for g in range(4):
                b = open_tile(TILE["od_pool"] + g)
                pe.wait_ge(sig("pooled"), g + 1)
                mm(b[:, 0:S], O_wp[:, g * P:(g + 1) * P], O_s1[:, g, 0:S], start=True, stop=True)\
                    .then_inc(filled, 1)

            def od_ready():
                pe.wait_ge(sig("head_n"), 13)
                wait_evac(pe, TILE["od_pool"] + 3)
                wait_evac(pe, TILE["od_v"] + 3)

            fence(pe, "pe", ("act", "dve", "pool"), 8)
            attention(*OD_U, O_P, O_PT, od_ready)
            pe.wait_ge(sig("att_out"), OD_U[1])
            for c in range(2):
                feature_tiles(f"od_out{c}", w3(f"od_out{c}"), range(0, 512, P), lambda k: O_y[:, k, :], S)
            norm(9, S)
            fence(pe, "pe", ("act", "dve"), 9)
            ffn(4, S, 9)

        @block.scalar
        def _(act):
            A = nc.scalar.activation
            steps = [0]

            def link(ins):
                steps[0] += 1
                ins.then_inc(sig("act_step"), 1)
                act.wait_ge(sig("act_step"), steps[0])

            def empty(n):
                act.wait_ge(filled, n + 1)
                return bank(n)

            def copy_tiles(stage, n, dst, nt=S, func=ACT.Identity, rows=P, scale=1.0, pre=None):
                for j in range(n):
                    b = empty(TILE[stage] + j)
                    if pre is not None:
                        pre(j)
                    A(dst(j), b[0:rows, 0:nt], func, scale=scale).then_inc(evac["A"], 1)

            def norm(q, nt, src, ready, final=None):
                ready()
                for k in range(KT):
                    A(zT[:, k, 0:nt], src[:, k, 0:nt], ACT.Square).then_inc(sig("norm_sq"), 1)
                b = empty(TILE[f"norm{q}"])
                if q > 0:
                    act.wait_ge(sig("norm_recip"), q)
                A(rt[:, 0:nt], b[:, 0:nt], ACT.Sqrt, scale=1.0 / D, bias=C("eps")).then_inc(evac["A"], 1)
                if q in MODN:
                    j = MODN[q][0]
                    for k in range(KT):
                        act.wait_ge(sig("norm_xr"), norm_xr_before(q) + k + 1)
                        A(zT[:, k, 0:S], zT[:, k, 0:S], ACT.Identity,
                          scale=modA[:, 2 * (8 * j + k):2 * (8 * j + k) + 1],
                          bias=mod[:, 2 * (24 * j + k):2 * (24 * j + k) + 1]).then_inc(sig("norm_zm"), 1)

            def ffn(f, nt):
                for c in range(FFC):
                    for j in range(2):
                        n = TILE[f"ffn{f}_in{c}"] + 2 * j
                        b = empty(n)
                        A(F_a[:, 2 * c + j, 0:nt], b[:, 0:nt], ACT.Silu).then_inc(evac["A"], 1)

            def merge(br, tmp):
                for c in range(4):
                    for j in range(2):
                        n = TILE[f"merge{br}{c}"] + 2 * j
                        b = empty(n)
                        i = 2 * c + j
                        if i >= 2:
                            m = TILE[f"merge{br}{(i - 2) // 2}"] + 2 * (i % 2) + 1
                            wait_evac(act, m)
                        A(tmp[:, i % 2, :], b[:, 0:S], ACT.Sigmoid).then_inc(evac["A"], 1)

            act.wait_ge(sig("vec_in"), 16)
            act.wait_ge(sig("cst_in"), 16)
            A(cs[:, :], V("c"), ACT.Silu).then_inc(sig("cs_ready"), 1)
            norm(0, S, xT, lambda: act.wait_ge(sig("x_in"), 16))
            for c in range(2):
                copy_tiles(f"lru_x{c}", 4, lambda j: A_xp[:, 4 * c + j, 3:S + 3])
            for c in range(2):
                copy_tiles(f"lru_g{c}", 4, lambda j: A_g[:, 4 * c + j, :], func=ACT.Gelu_apprx_tanh)
            wait_evac(act, TILE["lru_x1"] + 3)
            for k in range(KT):
                A(A_xc[:, k, :], A_xp[:, k, 3:S + 3], ACT.Identity, scale=V("conv_w", 24 + k, 1),
                  bias=V("conv_b", k, 1)).then_inc(sig("lru_tap"), 1)
            for k in range(KT):
                for g, dst in enumerate((A_r, A_i)):
                    n = TILE["lru_gates"] + 2 * k + g
                    b = empty(n)
                    A(dst[:, k, :], b[:, 0:S], ACT.Sigmoid, bias=V("b_gates", 8 * g + k, 1)).then_inc(evac["A"], 1)
            link(A(small[:, 0:8], V("lam"), ACT.Abs))
            link(A(small[:, 8:16], small[:, 0:8], ACT.Exp, scale=-1.0))
            A(small[:, 16:24], small[:, 8:16], ACT.Ln, bias=C("one")).then_inc(sig("lru_ln"), 1)
            act.wait_ge(sig("lru_coef"), 1)
            wait_evac(act, TILE["lru_gates"] + 15)
            for k in range(KT):
                A(A_a[:, k, :], A_r[:, k, :], ACT.Exp, scale=small[:, 32 + k:33 + k]).then_inc(sig("lru_a"), 1)
            for k in range(KT):
                A(A_t[:, k, :], A_r[:, k, :], ACT.Tanh, scale=small[:, 40 + k:41 + k]).then_inc(sig("lru_tanh"), 1)
            act.wait_ge(sig("lru_v"), 1)
            A(A_t, A_t, ACT.Sqrt, scale=2.0).then_inc(sig("lru_root"), 1)
            merge("A", mg_t)
            fence(act, "act", ("pe", "dve", "pool"), 1)

            copy_tiles("gla_q", 4, lambda j: C_q[:, j, :], scale=float(P) ** -0.5)
            copy_tiles("gla_k", 4, lambda j: C_k[:, j, :])
            copy_tiles("gla_lr", 1, lambda j: C_lr[0:16, :], rows=16)
            for h in range(4):
                b = empty(TILE["gla_al"] + h)
                A(C_Y[:, h, :], b[:, 0:S], ACT.Identity, bias=V("gla_ba", h, 1)).then_inc(evac["A"], 1)
            wait_evac(act, TILE["gla_al"] + 3)
            link(A(C_e, C_Y, ACT.Abs))
            link(A(C_e, C_e, ACT.Exp, scale=-1.0))
            A(C_e, C_e, ACT.Ln, bias=C("one")).then_inc(sig("gla_ln"), 1)
            act.wait_ge(sig("gla_b"), 1)
            A(C_Y, C_b, ACT.Exp, scale=1.0 / 16).then_inc(sig("gla_eb"), 1)
            A(C_e, C_b, ACT.Exp, scale=-1.0 / 16).then_inc(sig("gla_eb"), 1)
            act.wait_ge(sig("gla_bd"), 1)
            A(C_b, C_b, ACT.Exp, scale=1.0 / 16).then_inc(sig("gla_eb"), 1)
            for c in range(2):
                copy_tiles(f"gla_og{c}", 4, lambda j: C_og[:, 4 * c + j, :], func=ACT.Silu)
            for t in range(2):
                b = empty(TILE["gla_t"] + t)
                A(C_kt[:, 4 * t:4 * t + 4, :], b[:, :].rearrange("p (h d) -> p h d", h=4), ACT.Identity)\
                    .then_inc(evac["A"], 1)
            for j in range(8):
                b = empty(TILE["gla_o"] + j)
                if j == 0:
                    act.wait_ge(sig("gla_state"), 28)
                A(C_o[:, j, :], b[:, 0:S], ACT.Identity).then_inc(evac["A"], 1)
            wait_evac(act, TILE["gla_o"] + 7)
            for j in range(8):
                A(C_st[:, j // 2, (j % 2) * S:(j % 2 + 1) * S], C_o[:, j, :], ACT.Square).then_inc(sig("gla_sq"), 1)
            for h in range(4):
                b = empty(TILE["gla_n"] + h)
                A(C_st[:, h, 2 * S:3 * S], b[:, 0:S], ACT.Sqrt, scale=1.0 / 256, bias=C("eps"))\
                    .then_inc(evac["A"], 1)
            merge("C", mgC_t)
            fence(act, "act", ("pe", "dve", "pool"), 2)

            def att_exp(u, Pb, gate=None):
                kind, g, t = UNITS[u]
                act.wait_ge(sig("att_max"), u + 1)
                act.wait_ge(sig("att_turned"), batches_before(u)) if batches_before(u) else None
                nm, sm = small[:, 0:12], small[:, 16:28]
                if kind == "nsa":
                    nk = P * (t + 1)
                    for i in range(8):
                        A(Pb[:, i * S:i * S + nk], psum[:, i * S:i * S + nk], ACT.Exp,
                          bias=nm[:, i:i + 1], accum_out=sm[:, i:i + 1])
                    for r in range(4):
                        at = r * CMP_N
                        last = A(Pb[:, 2048 + at:2048 + at + CMP_N], psum[:, 4 * BANK + at:4 * BANK + at + CMP_N],
                                 ACT.Exp, bias=nm[:, 8 + r:9 + r], accum_out=sm[:, 8 + r:9 + r])
                else:
                    k0 = S if t >= 2 else 0
                    if kind == "ev":
                        A(small[:, 32:36], small[:, 28:32], ACT.Exp)
                    for r in range(4):
                        last = A(Pb[:, r * BANK + k0:(r + 1) * BANK], psum[:, r * BANK + k0:(r + 1) * BANK],
                                 ACT.Exp, bias=nm[:, r:r + 1], accum_out=sm[:, r:r + 1])
                last.then_inc(sig("att_exp"), 1)

            def att_copies(u, PT):
                bs, gb0 = batches(u), batches_before(u)
                for i, (seg, _) in enumerate(bs):
                    gb = gb0 + i
                    act.wait_ge(sig("att_turned"), gb + 1)
                    if gb >= 3:
                        act.wait_ge(sig("att_mult"), gb - 2)
                    n = CMP_N if seg == 2 else P
                    A(PT[0:n, gb % 3, :], psum[0:n, (5 + gb % 2) * BANK:(6 + gb % 2) * BANK], ACT.Identity)\
                        .then_inc(sig("att_copied"), 1)

            def attention(u0, u1, Pb, PT):
                att_exp(u0, Pb)
                for u in range(u0, u1):
                    att_copies(u, PT)
                    if u + 1 < u1:
                        att_exp(u + 1, Pb)

            for c in range(2):
                copy_tiles(f"nsa_q{c}", 4, lambda j: B_q[:, 4 * c + j, :], scale=HD ** -0.5)
            wait_evac(act, TILE["flip"] + 7)
            copy_tiles("nsa_kvc", 4, lambda j: B_kc[:, j, :])
            copy_tiles("nsa_ksw", 4, lambda j: B_kk[:, j, :])
            copy_tiles("nsa_gate", 2, lambda j: B_gate[:, j, :], nt=48, func=ACT.Sigmoid)
            for i in range(2):
                copy_tiles(f"cmp_hid{i}", 2, lambda j: B_hid[:, i, j, :], nt=60, func=ACT.Gelu_apprx_tanh)
            fence(act, "act", ("pe", "dve", "pool"), 3)
            attention(*NSA_U, B_P, B_PT)
            merge("B", mgB_t)
            for c in range(2):
                copy_tiles(f"w_out{c}", 4, lambda j: Y_y[:, 4 * c + j, :])
            norm(1, S, Y_y, lambda: wait_evac(act, TILE["w_out1"] + 3))
            norm(2, S, xT, lambda: act.wait_ge(sig("norm_x"), KT))
            fence(act, "act", ("pe", "dve", "pool"), 4)
            ffn(0, S)
            for c in range(4):
                copy_tiles(f"ffn0_out{c}", 2, lambda j: Y_y[:, 2 * c + j, :])
            norm(3, S, Y_y, lambda: wait_evac(act, TILE["ffn0_out3"] + 1))

            def ready4():
                act.wait_ge(sig("norm_x"), 2 * KT)
                act.wait_ge(sig("ctx_in"), 16)
                act.wait_ge(sig("mod_ready"), 1)

            norm(4, TOK, xT, ready4)
            ffn(1, TOK)
            norm(5, TOK, xT, lambda: wait_evac(act, TILE["ffn1_out3"] + 1))
            fence(act, "act", ("pe", "dve", "pool"), 5)
            copy_tiles("ev_q", 4, lambda j: E_qk[:, j, :], nt=TOK)
            copy_tiles("ev_k", 1, lambda j: E_qk[:, 4, :], nt=TOK)
            copy_tiles("ev_bv", 4, lambda j: E_bv[:, j, :], nt=TOK, func=ACT.Gelu_apprx_tanh)
            copy_tiles("ev_bu", 4, lambda j: E_u[:, j, :], nt=TOK, func=ACT.Gelu_apprx_tanh)
            wait_evac(act, TILE["ev_bu"] + 3)
            for j in range(5):
                A(E_rt[:, j, :], E_qk[:, j, :], ACT.Square).then_inc(sig("head_sq"), 1)
            for j in range(5):
                b = empty(TILE["ev_qn"] + j)
                A(E_rt[:, j, :], b[:, :], ACT.Sqrt, scale=1.0 / HD, bias=C("eps")).then_inc(evac["A"], 1)
            act.wait_ge(sig("ev_vsum"), 1)
            A(small[:, 96:128], small[:, 64:96], ACT.Sqrt, scale=1.0 / HD, bias=C("eps")).then_inc(sig("ev_vrt"), 1)
            attention(*EV_U, E_P, E_PT)
            fence(act, "act", ("pe", "dve", "pool"), 6)
            norm(6, TOK, xT, lambda: wait_evac(act, TILE["ev_out1"] + 3))
            ffn(2, TOK)

            def ready7():
                wait_evac(act, TILE["ffn2_out3"] + 1)
                act.wait_ge(sig("mod_ready"), 2)

            norm(7, TOK, xT, ready7)
            ffn(3, TOK)
            norm(8, TOK, xT, lambda: wait_evac(act, TILE["ffn3_out3"] + 1))
            fence(act, "act", ("pe", "dve", "pool"), 7)
            copy_tiles("od_q", 4, lambda j: O_q[:, j, :])
            copy_tiles("od_k", 4, lambda j: O_k[:, j, :], nt=TOK)
            copy_tiles("od_xp", 4, lambda j: O_xp[:, j, 8:S + 8])
            wait_evac(act, TILE["od_xp"] + 3)
            for j in range(8):
                nt = S if j < 4 else TOK
                src = O_q[:, j, :] if j < 4 else O_k[:, j - 4, :]
                if j >= 2:
                    act.wait_ge(sig("head_n"), 5 + j - 1)
                A(O_tmp[:, j % 2, 0:nt], src, ACT.Square).then_inc(sig("head_sq"), 1)
                b = empty(TILE["od_qn"] + j)
                A(O_tmp[:, j % 2, 0:nt], b[:, 0:nt], ACT.Sqrt, scale=1.0 / HD, bias=C("eps")).then_inc(evac["A"], 1)
            wait_evac(act, TILE["od_flip"] + 7)
            for g in range(4):
                b = empty(TILE["od_pool"] + g)
                A(O_y[:, g, :], b[:, 0:S], ACT.Copy, scale=V("c_scale", g, 1)).then_inc(evac["A"], 1)
            fence(act, "act", ("pe", "dve", "pool"), 8)
            attention(*OD_U, O_P, O_PT)
            norm(9, S, xT, lambda: wait_evac(act, TILE["od_out1"] + 3))
            fence(act, "act", ("pe", "dve"), 9)
            ffn(4, S)

        @block.vector
        def _(dve):
            v = nc.vector
            steps = [0]

            def link(ins):
                steps[0] += 1
                ins.then_inc(sig("dve_step"), 1)
                dve.wait_ge(sig("dve_step"), steps[0])

            def empty(n):
                dve.wait_ge(filled, n + 1)
                return bank(n)

            def norm(q, nt, src, gain=None):
                wait_evac(dve, TILE[f"norm{q}"])
                v.reciprocal(rr[:, 0:nt], rt[:, 0:nt]).then_inc(sig("norm_recip"), 1)
                dve.wait_ge(sig("norm_recip"), q + 1)
                for k in range(KT):
                    if q in MODN:
                        v.tensor_tensor(out=zT[:, k, 0:nt], in0=src[:, k, 0:nt], in1=rr[:, 0:nt], op=ALU.mult)\
                            .then_inc(sig("norm_xr"), 1)
                    elif q in (0, 2):
                        v.scalar_tensor_tensor(out=zT[:, k, 0:nt], in0=src[:, k, 0:nt], scalar=gain(k),
                                               in1=rr[:, 0:nt], op0=ALU.mult, op1=ALU.mult)\
                            .then_inc(sig("norm_z"), 1)
                    else:
                        link(v.scalar_tensor_tensor(out=src[:, k, 0:nt], in0=src[:, k, 0:nt], scalar=gain(k),
                                                    in1=rr[:, 0:nt], op0=ALU.mult, op1=ALU.mult))
                        v.tensor_tensor(out=xT[:, k, 0:nt], in0=src[:, k, 0:nt], in1=xT[:, k, 0:nt], op=ALU.add)\
                            .then_inc(sig("norm_x"), 1)

            def ada(li, a, b_):
                for c in range(a, b_):
                    n = TILE[f"ada{li}_{c}"]
                    b = empty(n)
                    v.tensor_tensor(out=mod[:, 8 * c:8 * c + 8].rearrange("p (j s) -> p j s", s=2),
                                    in0=b[:, 0:8].rearrange("p (j s) -> p j s", s=2),
                                    in1=rep(V("ada_b", 72 * li + 4 * c, 4), 2), op=ALU.add).then_inc(evac["V"], 1)

            def mods(li):
                wait_evac(dve, TILE[f"ada{li}_17"])
                for j in range(3):
                    g = rep(V("norm_g2", 24 * li + 8 * j, 8), 2)
                    last = v.scalar_tensor_tensor(
                        out=modA[:, 16 * j:16 * j + 16].rearrange("p (k s) -> p k s", s=2),
                        in0=mod[:, 16 * (3 * j + 1):16 * (3 * j + 2)].rearrange("p (k s) -> p k s", s=2),
                        scalar=1.0, in1=g, op0=ALU.add, op1=ALU.mult)
                for j in range(2):
                    last = v.tensor_scalar(out=gates_h[:, 16 * j:16 * j + 16],
                                           in0=mod[:, 16 * (6 * j + 2):16 * (6 * j + 3)],
                                           scalar1=0.5, scalar2=None, op0=ALU.mult)
                last.then_inc(sig("mod_ready"), 1)
                dve.wait_ge(sig("mod_ready"), li + 1)

            def residual(stage, n, base, nt, gate):
                for j in range(n):
                    k = base + j
                    b = empty(TILE[stage] + j)
                    for s in range(nt // S):
                        last = v.scalar_tensor_tensor(out=xT[:, k, s * S:(s + 1) * S], in0=b[:, s * S:(s + 1) * S],
                                                      scalar=gate(k, s), in1=xT[:, k, s * S:(s + 1) * S],
                                                      op0=ALU.mult, op1=ALU.add)
                    last.then_inc(evac["V"], 1)

            def ffn(f, nt, which=None):
                for c in range(FFC):
                    for j in range(2):
                        n = TILE[f"ffn{f}_in{c}"] + 2 * j + 1
                        b = empty(n)
                        wait_evac(dve, n - 1)
                        v.tensor_tensor(out=F_a[:, 2 * c + j, 0:nt], in0=b[:, 0:nt], in1=F_a[:, 2 * c + j, 0:nt],
                                        op=ALU.mult).then_inc(evac["V"], 1)
                if which is not None:
                    for c in range(4):
                        residual(f"ffn{f}_out{c}", 2, 2 * c, nt,
                                 lambda k, s: gates_h[:, 16 * which + 2 * k + s:16 * which + 2 * k + s + 1])

            def merge(br, tmp):
                for c in range(4):
                    for j in range(2):
                        i = 2 * c + j
                        n = TILE[f"merge{br}{c}"] + 2 * j + 1
                        b = empty(n)
                        wait_evac(dve, n - 1)
                        m = zT[:, i, S:TOK]
                        if br == "A":
                            v.tensor_tensor(out=m, in0=b[:, 0:S], in1=tmp[:, i % 2, :], op=ALU.mult)\
                                .then_inc(evac["V"], 1)
                        else:
                            link(v.tensor_tensor(out=tmp[:, i % 2, :], in0=b[:, 0:S], in1=tmp[:, i % 2, :],
                                                 op=ALU.mult))
                            v.tensor_tensor(out=m, in0=m, in1=tmp[:, i % 2, :], op=ALU.add).then_inc(evac["V"], 1)

            dve.wait_ge(sig("vec_in"), 16)
            dve.wait_ge(sig("cst_in"), 16)
            link(v.memset(A_xp[:, :, 0:3], 0.0))
            dve.wait_ge(sig("x_in"), 16)
            norm(0, S, xT, lambda k: V("norm_g", k, 1))
            b = empty(TILE["strip"])
            v.tensor_copy(K_strip[0:16, :], b[0:16, 0:384]).then_inc(evac["V"], 1)
            b = empty(TILE["cbias"])
            v.tensor_copy(K_C.rearrange("p (t h c) -> p t c h", t=2, h=16),
                          b[:, 0:480].rearrange("p (t c h) -> p t c h", t=2, c=CMP_N)).then_inc(evac["V"], 1)
            for k in range(KT):
                dve.wait_ge(sig("lru_tap"), k + 1)
                for i in range(3):
                    ins = v.scalar_tensor_tensor(out=A_xc[:, k, :], in0=A_xp[:, k, i:i + S],
                                                 scalar=V("conv_w", 8 * i + k, 1), in1=A_xc[:, k, :],
                                                 op0=ALU.mult, op1=ALU.add)
                    if i < 2:
                        link(ins)
                    else:
                        ins.then_inc(sig("lru_xc"), 1)
            link(v.tensor_scalar(out=small[:, 48:56], in0=V("lam"), scalar1=-1.0, scalar2=0.0,
                                 op0=ALU.mult, op1=ALU.max))
            dve.wait_ge(sig("lru_ln"), 1)
            link(v.tensor_tensor(out=small[:, 48:56], in0=small[:, 48:56], in1=small[:, 16:24], op=ALU.add))
            v.tensor_scalar(out=small[:, 32:40], in0=small[:, 48:56], scalar1=-8.0, scalar2=None, op0=ALU.mult)
            v.tensor_scalar(out=small[:, 40:48], in0=small[:, 48:56], scalar1=8.0, scalar2=None, op0=ALU.mult)\
                .then_inc(sig("lru_coef"), 1)
            wait_evac(dve, TILE["lru_gates"] + 15)
            dve.wait_ge(sig("lru_xc"), KT)
            link(v.tensor_tensor(out=A_i, in0=A_i, in1=A_xc, op=ALU.mult))
            dve.wait_ge(sig("lru_tanh"), KT)
            link(v.tensor_scalar(out=A_r, in0=A_t, scalar1=1.0, scalar2=None, op0=ALU.add))
            link(v.reciprocal(A_r, A_r))
            v.tensor_tensor(out=A_t, in0=A_t, in1=A_r, op=ALU.mult).then_inc(sig("lru_v"), 1)
            dve.wait_ge(sig("lru_root"), 1)
            dve.wait_ge(sig("lru_a"), KT)
            link(v.tensor_tensor(out=A_i, in0=A_i, in1=A_t, op=ALU.mult))
            for k in range(KT):
                last = v.tensor_tensor_scan(out=A_r[:, k, :], data0=A_a[:, k, :], data1=A_i[:, k, :], initial=0.0,
                                            op0=ALU.mult, op1=ALU.add)
            link(last)
            for k in range(KT):
                v.tensor_tensor(out=A_y[:, k, :], in0=A_r[:, k, :], in1=A_g[:, k, :], op=ALU.mult)\
                    .then_inc(sig("lru_y"), 1)
            ada(0, 0, 6)
            merge("A", mg_t)
            fence(dve, "dve", ("pe", "act", "pool"), 1)

            dve.wait_ge(sig("gla_ln"), 1)
            link(v.tensor_scalar(out=C_Y, in0=C_Y, scalar1=0.0, scalar2=None, op0=ALU.min))
            link(v.tensor_tensor(out=C_Y, in0=C_Y, in1=C_e, op=ALU.subtract))
            for h in range(4):
                last = v.tensor_tensor_scan(out=C_b[:, h, :], data0=C("scan_mask"), data1=C_Y[:, h, :], initial=0.0,
                                            op0=ALU.mult, op1=ALU.add)
            last.then_inc(sig("gla_b"), 1)
            dve.wait_ge(sig("gla_b"), 1)
            dve.wait_ge(sig("gla_eb"), 2)
            blast = small[:, 128:160]
            link(v.tensor_copy(blast, arena[:, 4096 + 31:4096 + 1024:32]))
            v.tensor_tensor(out=arena[:, 4096:5120].rearrange("p (c i) -> p c i", i=32), in0=rep(blast, 32),
                            in1=arena[:, 4096:5120].rearrange("p (c i) -> p c i", i=32), op=ALU.subtract)\
                .then_inc(sig("gla_bd"), 1)
            v.tensor_copy(small[:, 0:32], arena[:, 2048 + 31:2048 + 1024:32])
            wait_evac(dve, TILE["gla_k"] + 3)
            v.tensor_tensor(out=C_q, in0=C_q, in1=C_Y, op=ALU.mult)
            dve.wait_ge(sig("gla_eb"), 3)
            link(v.tensor_tensor(out=C_b, in0=C_b, in1=C_k, op=ALU.mult))
            link(v.tensor_tensor(out=C_k, in0=C_k, in1=C_e, op=ALU.mult))
            v.tensor_copy(C_e, C_b).then_inc(sig("gla_kend"), 1)
            for c in range(2):
                for t in range(2):
                    b = empty(TILE[f"gla_v{c}"] + t)
                    v.tensor_copy(C_v[:, t, c * 512:(c + 1) * 512], b[:, :]).then_inc(evac["V"], 1)
            ada(0, 6, 12)
            link(v.memset(C_at, 0.0))
            mask = C("gla_mask").bitcast(mybir.dt.uint32)
            for t in range(2):
                b = empty(TILE["gla_att"] + t)
                for h in range(4):
                    last = v.copy_predicated(C_at[:, 4 * t + h, :], mask, b[:, h * P:(h + 1) * P])
                last.then_inc(evac["V"], 1)
            for c in range(7):
                for h in range(4):
                    dve.wait_ge(sig("gla_upd"), 4 * c + h + 1)
                    upd = psum[:, (4 + h) * BANK:(4 + h) * BANK + S]
                    dst = C_st[:, h, c * S:(c + 1) * S]
                    if c == 0:
                        v.tensor_copy(dst, upd).then_inc(sig("gla_state"), 1)
                    else:
                        dve.wait_ge(sig("gla_state"), 4 * (c - 1) + h + 1)
                        v.scalar_tensor_tensor(out=dst, in0=C_st[:, h, (c - 1) * S:c * S],
                                               scalar=small[:, 8 * h + c:8 * h + c + 1], in1=upd,
                                               op0=ALU.mult, op1=ALU.add).then_inc(sig("gla_state"), 1)
            for h in range(4):
                wait_evac(dve, TILE["gla_n"] + h)
                r = C_st[:, h, 2 * S:3 * S]
                link(v.reciprocal(r, r))
                for e in range(2):
                    o = C_o[:, 2 * h + e, :]
                    link(v.scalar_tensor_tensor(out=o, in0=o, scalar=V("gla_norm", e, 1), in1=r,
                                                op0=ALU.mult, op1=ALU.mult))
                    v.tensor_tensor(out=C_og[:, 2 * h + e, :], in0=C_og[:, 2 * h + e, :], in1=o, op=ALU.mult)\
                        .then_inc(sig("gla_y"), 1)
            merge("C", mgC_t)
            fence(dve, "dve", ("pe", "act", "pool"), 2)

            def att_max(u):
                kind, g, t = UNITS[u]
                nm = small[:, 0:12]
                dve.wait_ge(sig("att_score"), u + 1)
                if kind == "nsa":
                    nk = P * (t + 1)
                    j0 = P if t == 0 else 0
                    for a in range(2):
                        s_ = psum[:, 4 * a * S:4 * (a + 1) * S].rearrange("p (s j k) -> p s j k", s=2, j=2)
                        s_ = s_[:, :, :, 0:nk]
                        bias = B_T[:, 4 * g + 2 * a:4 * g + 2 * a + 2, j0:j0 + nk].unsqueeze(1)\
                            .to_broadcast([P, 2, 2, nk])
                        v.tensor_tensor(out=s_, in0=s_, in1=bias, op=ALU.add)
                    sc = psum[:, 4 * BANK:4 * BANK + 4 * CMP_N].rearrange("p (r c) -> p r c", r=4)
                    link(v.tensor_tensor(out=sc, in0=sc, in1=B_C[:, t, 4 * g:4 * g + 4, :], op=ALU.add))
                    v.reduce_max(nm[:, 0:8], psum[:, 0:8 * S].rearrange("p (r k) -> p r k", r=8)[:, :, 0:nk],
                                 AX, negate=True)
                    v.reduce_max(nm[:, 8:12], sc, AX, negate=True).then_inc(sig("att_max"), 1)
                    return
                k0 = S if t >= 2 else 0
                s_ = psum[:, 0:4 * BANK].rearrange("p (r k) -> p r k", r=4)
                if k0 == 0:
                    if kind == "ev":
                        wm = C("win_mask").rearrange("p (t k) -> p t k", t=2)[:, t, :]
                        m = b3(wm, 4, S)
                    else:
                        m = O_nb[:, 8 * t + 4 * g:8 * t + 4 * g + 4, :]
                    link(v.tensor_tensor(out=s_[:, :, 0:S], in0=s_[:, :, 0:S], in1=m, op=ALU.add))
                ins = v.reduce_max(nm[:, 0:4], s_[:, :, k0:BANK], AX, negate=True)
                if kind == "ev":
                    link(ins)
                    sink = V("sink", 4 * g, 4)
                    link(v.scalar_tensor_tensor(out=nm[:, 0:4], in0=sink, scalar=-1.0, in1=nm[:, 0:4],
                                                op0=ALU.mult, op1=ALU.min))
                    ins = v.tensor_tensor(out=small[:, 28:32], in0=sink, in1=nm[:, 0:4], op=ALU.add)
                ins.then_inc(sig("att_max"), 1)

            def att_norm(u, Pb):
                kind, g, t = UNITS[u]
                sm = small[:, 16:28]
                dve.wait_ge(sig("att_exp"), u + 1)
                if kind == "nsa":
                    nk = P * (t + 1)
                    link(v.reciprocal(sm, sm))
                    for seg, br in enumerate((1, 2, 0)):
                        gate = B_gate[:, t, 16 * br + 4 * g:16 * br + 4 * g + 4]
                        if seg == 2:
                            ins = v.tensor_tensor(out=small[:, 44:48], in0=sm[:, 8:12], in1=gate, op=ALU.mult)
                        else:
                            out = small[:, 36:44].rearrange("p (a s j) -> p a s j", a=2, s=2)[:, :, seg, :]
                            si = sm[:, 0:8].rearrange("p (a s j) -> p a s j", a=2, s=2)[:, :, seg, :]
                            v.tensor_tensor(out=out, in0=si, in1=gate.rearrange("p (a j) -> p a j", a=2), op=ALU.mult)
                    link(ins)
                    p_ = Pb[:, 0:2048].rearrange("p (r k) -> p r k", r=8)[:, :, 0:nk]
                    v.tensor_tensor(out=p_, in0=p_, in1=rep(small[:, 36:44], nk), op=ALU.mult)
                    pc = Pb[:, 2048:2108].rearrange("p (r c) -> p r c", r=4)
                    link(v.tensor_tensor(out=pc, in0=pc, in1=rep(small[:, 44:48], CMP_N), op=ALU.mult))
                    va = C("valid_c").rearrange("p (t c) -> p t c", t=2)[:, t, :]
                    v.tensor_tensor(out=pc, in0=pc, in1=b3(va, 4, CMP_N), op=ALU.mult).then_inc(sig("att_p"), 1)
                    return
                k0 = S if t >= 2 else 0
                if kind == "ev":
                    link(v.tensor_tensor(out=sm[:, 0:4], in0=sm[:, 0:4], in1=small[:, 32:36], op=ALU.add))
                link(v.reciprocal(small[:, 36:40], sm[:, 0:4]))
                p_ = Pb[:, 0:2048].rearrange("p (r k) -> p r k", r=4)[:, :, k0:BANK]
                v.tensor_tensor(out=p_, in0=p_, in1=rep(small[:, 36:40], BANK - k0), op=ALU.mult)\
                    .then_inc(sig("att_p"), 1)

            def att_done(u, y):
                kind, g, t = UNITS[u]
                dve.wait_ge(sig("att_mult"), batches_before(u + 1))
                if kind == "od":
                    k = 4 + 2 * g
                else:
                    k = 2 * g
                v.tensor_copy(y[:, k:k + 2, t * P:(t + 1) * P],
                              psum[:, 7 * BANK:7 * BANK + 2 * P].rearrange("p (j t) -> p j t", j=2))\
                    .then_inc(sig("att_out"), 1)

            def attention(u0, u1, Pb, y):
                att_max(u0)
                for u in range(u0, u1):
                    att_norm(u, Pb)
                    if u + 1 < u1:
                        att_max(u + 1)
                    att_done(u, y)

            for i in range(8):
                b = empty(TILE["flip"] + i)
                v.tensor_copy(area(9328 + i * BANK, BANK), b[:, :]).then_inc(evac["V"], 1)
            v.tensor_copy(B_C, K_C.rearrange("p (t h c) -> p t h c", t=2, h=16)).then_inc(sig("cbias_moved"), 1)
            for t in range(2):
                b = empty(TILE["nsa_vsw"] + t)
                v.tensor_copy(B_v[:, t, :], b[:, :]).then_inc(evac["V"], 1)
            for i in range(2):
                pos = V("pos_k" if i == 0 else "pos_v")
                dve.wait_ge(sig("stack_in"), 16 * 16)
                for g in range(4):
                    st = 5120 + (4 * i + g) * S
                    for half in range(1):
                        src = arena[:, st:st + 240].rearrange("p (c m two) -> p m c two", m=8, two=2)[:, :, :, 0]
                        v.tensor_tensor(out=B_bl[:, i, 0:8, g * CMP_N:(g + 1) * CMP_N], in0=src,
                                        in1=rep(pos[:, 0:8], CMP_N), op=ALU.add)
                        src = arena[:, st + 16:st + 256].rearrange("p (c m two) -> p m c two", m=8, two=2)[:, :, :, 0]
                        v.tensor_tensor(out=B_bl[:, i, 8:16, g * CMP_N:(g + 1) * CMP_N], in0=src,
                                        in1=rep(pos[:, 8:16], CMP_N), op=ALU.add).then_inc(sig("cmp_blocks"), 1)
            b = empty(TILE["cmp_kv"])
            v.tensor_copy(B_kcT, b[:, 0:60]).then_inc(evac["V"], 1)
            b = empty(TILE["cmp_kv"] + 1)
            v.tensor_copy(B_vc[0:CMP_N, :, :], b[0:CMP_N, 0:256].rearrange("p (g d) -> p g d", g=4))\
                .then_inc(evac["V"], 1)
            ada(0, 12, 18)
            mods(0)
            fence(dve, "dve", ("pe", "act", "pool"), 3)
            attention(*NSA_U, B_P, B_y)
            merge("B", mgB_t)
            norm(1, S, Y_y, lambda k: V("norm_g", 8 + k, 1))
            norm(2, S, xT, lambda k: V("norm_g", 16 + k, 1))
            fence(dve, "dve", ("pe", "act", "pool"), 4)
            ffn(0, S)
            norm(3, S, Y_y, lambda k: V("norm_g", 24 + k, 1))

            dve.wait_ge(sig("norm_x"), 2 * KT)
            norm(4, TOK, xT)
            ffn(1, TOK, 0)
            norm(5, TOK, xT)
            fence(dve, "dve", ("pe", "act", "pool"), 5)
            for t in range(4):
                b = empty(TILE["ev_v"] + t)
                v.tensor_copy(E_v[:, t, :], b[:, 0:P]).then_inc(evac["V"], 1)
            wait_evac(dve, TILE["ev_bv"] + 3)
            link(v.tensor_tensor(out=E_sq, in0=E_bv, in1=E_bv, op=ALU.mult))
            v.tensor_reduce(out=small[:, 64:96], in_=E_sq.rearrange("p t (g d) -> p (t g) d", d=HD), axis=AX,
                            op=ALU.add).then_inc(sig("ev_vsum"), 1)

            def head_norm(stage, j, x, rtile, gain, scale, last_sig=True):
                wait_evac(dve, TILE[stage] + j)
                link(v.reciprocal(rtile, rtile))
                if scale != 1.0:
                    link(v.tensor_scalar(out=x, in0=x, scalar1=scale, scalar2=None, op0=ALU.mult))
                v.scalar_tensor_tensor(out=x, in0=x, scalar=gain, in1=rtile, op0=ALU.mult, op1=ALU.mult)\
                    .then_inc(sig("head_n"), 1)

            for j in range(5):
                head_norm("ev_qn", j, E_qk[:, j, :], E_rt[:, j, :], V("qg_ev") if j < 4 else V("kg_ev"),
                          HD ** -0.5 if j < 4 else 1.0)
            for j in range(5):
                b = empty(TILE["ev_rope"] + j)
                link(v.tensor_tensor(out=E_rt[:, j, 0:S], in0=b[:, 0:S], in1=C("rope_s"), op=ALU.mult))
                link(v.tensor_tensor(out=E_qk[:, j, 0:S], in0=E_qk[:, j, 0:S], in1=C("rope_c"), op=ALU.mult))
                v.tensor_tensor(out=E_qk[:, j, 0:S], in0=E_qk[:, j, 0:S], in1=E_rt[:, j, 0:S], op=ALU.add)\
                    .then_inc(evac["V"], 1)
            dve.wait_ge(sig("ev_vrt"), 1)
            link(v.reciprocal(small[:, 96:128], small[:, 96:128]))
            bv = E_bv.rearrange("p t (g d) -> p (t g) d", d=HD)
            link(v.tensor_tensor(out=bv, in0=bv, in1=rep(small[:, 96:128], HD), op=ALU.mult))
            dve.wait_ge(sig("ev_small_in"), 16)
            for t in range(4):
                v.tensor_tensor(out=E_bv[:, t, :], in0=E_bv[:, t, :], in1=E_w[:, 0:512], op=ALU.mult)\
                    .then_inc(sig("ev_vv"), 1)
            for jp in range(4):
                b = empty(TILE["ev_mix"] + jp)
                mixed = E_y[:, 4 + jp, :]
                wait_evac(dve, TILE["ev_bu"] + 3)
                v.tensor_tensor(out=mixed.rearrange("p (t i) -> p t i", t=4),
                                in0=b[:, :].rearrange("p (t i) -> p t i", t=4),
                                in1=b3(E_w[:, 512 + jp * P:512 + (jp + 1) * P], 4, P), op=ALU.add)\
                    .then_inc(evac["V"], 1)
                wait_evac(dve, TILE["ev_mix"] + jp)
                v.tensor_tensor(out=mixed, in0=mixed, in1=E_u[:, jp, :], op=ALU.mult).then_inc(sig("mix_y"), 1)
            attention(*EV_U, E_P, E_y)
            for c in range(2):
                residual(f"ev_out{c}", 4, 4 * c, TOK, lambda k, s: mod[:, 80 + 2 * k + s:80 + 2 * k + s + 1])
            fence(dve, "dve", ("pe", "act", "pool"), 6)
            norm(6, TOK, xT)
            ffn(2, TOK, 1)
            ada(1, 0, 18)
            mods(1)

            norm(7, TOK, xT)
            ffn(3, TOK, 0)
            norm(8, TOK, xT)
            fence(dve, "dve", ("pe", "act", "pool"), 7)
            v.memset(O_xp[:, :, 0:8], 0.0)
            link(v.memset(O_xp[:, :, S + 8:S + 16], 0.0))
            for t in range(4):
                b = empty(TILE["od_v"] + t)
                v.tensor_copy(O_v[:, t, :], b[:, :]).then_inc(evac["V"], 1)
            for j in range(8):
                x = O_q[:, j, :] if j < 4 else O_k[:, j - 4, :]
                head_norm("od_qn", j, x, O_tmp[:, j % 2, 0:S if j < 4 else TOK],
                          V("qg_od") if j < 4 else V("kg_od"), HD ** -0.5 if j < 4 else 1.0)
            for i in range(8):
                b = empty(TILE["od_flip"] + i)
                t = i // 4
                na = C("na_mask").rearrange("p (t k) -> p t k", t=2)[:, t, :]
                v.tensor_tensor(out=O_nb[:, 2 * i:2 * i + 2, :], in0=b[:, :].rearrange("p (h k) -> p h k", h=2),
                                in1=b3(na, 2, S), op=ALU.add).then_inc(evac["V"], 1)
            ic = C("inv_count").rearrange("p (g t) -> p g t", g=4)
            for g, w in enumerate((2, 4, 8, 16)):
                wait_evac(dve, TILE["od_xp"] + g)
                src, dst, n, step = O_xp[:, g, :], O_s1[:, g, :], S + 16, 1
                other = O_s2[:, g, :]
                while step < w:
                    n -= step
                    link(v.tensor_tensor(out=dst[:, 0:n], in0=src[:, 0:n], in1=src[:, step:step + n], op=ALU.add))
                    src, dst, other = dst, other, dst
                    step *= 2
                at = 8 - w // 2
                link(v.tensor_tensor(out=dst[:, 0:S], in0=src[:, at:at + S], in1=ic[:, g, :], op=ALU.mult))
                link(v.tensor_tensor(out=src[:, 0:S], in0=dst[:, 0:S], in1=O_xp[:, g, 8:S + 8], op=ALU.subtract))
                v.tensor_copy(O_s1[:, g, 0:S], src[:, 0:S]).then_inc(sig("pooled"), 1)
            fence(dve, "dve", ("pe", "act", "pool"), 8)
            attention(*OD_U, O_P, O_y)
            for c in range(2):
                residual(f"od_out{c}", 4, 4 * c, S, lambda k, s: mod[:, 80 + 2 * k + s:80 + 2 * k + s + 1])
            norm(9, S, xT)
            fence(dve, "dve", ("pe", "act"), 9)
            ffn(4, S, 1)


def col(a):
    return np.ascontiguousarray(a.reshape(-1, P).T)


def pack(w):
    k, n = w.shape
    return w.reshape(k // P, P, n).transpose(1, 0, 2).reshape(P, -1)


def kernel(**inputs):
    import concourse.bacc as _bacc
    from concourse.bass_utils import run_bass_kernel_spmd as _run

    x = {k: np.asarray(v) for k, v in inputs.items()}
    w_in = x["w_in"][0]
    cat = np.concatenate

    def cols(a, b):
        return w_in[:, a:b]

    o_q, o_kv, o_gate, o_gq = 2048, 3072, 4608, 4656
    o_gv, o_og, o_lr, o_merge = 5680, 6704, 7728, 7744
    kv = [cols(o_kv + 256 * i, o_kv + 256 * (i + 1)) for i in range(6)]
    ch = [cols(0, 512), cols(512, 1024), cols(1024, 1536), cols(1536, 2048)]

    def merges(i):
        return [cat([cols(o_merge + D * i + 256 * c, o_merge + D * i + 256 * (c + 1)),
                     x["w_branch"][0, i][:, 256 * c:256 * (c + 1)]], axis=1) for c in range(4)]

    ch += merges(0)
    ch += [cols(o_gq, o_gq + 512), cols(o_gq + 512, o_gq + 1024), cols(o_gv, o_gv + 512),
           cols(o_gv + 512, o_gv + 1024), cols(o_og, o_og + 512), cols(o_og + 512, o_og + 1024)]
    ch += merges(2)
    ch += [cols(o_q, o_q + 512), cols(o_q + 512, o_q + 1024), cat([kv[0], kv[1]], 1), cat([kv[2], kv[4]], 1),
           cat([kv[3], kv[5]], 1)]
    chunks = [pack(w) for w in ch]
    chunks += [pack(x["cmp_w1"][0, i]) for i in range(2)]
    chunks += [pack(w) for w in merges(1)]
    chunks += [pack(x["w_out"][0][:, 512 * c:512 * (c + 1)]) for c in range(2)]
    ffs = [(x["w_ffn_in"][0], x["w_ffn_out"][0])] + [(x["ffn_w_gu_2"][l, i], x["ffn_w_down_2"][l, i])
                                                     for l in range(2) for i in range(2)]
    for gu, _ in ffs:
        for c in range(FFC):
            chunks.append(pack(cat([gu[:, 256 * c:256 * (c + 1)], gu[:, FF + 256 * c:FF + 256 * (c + 1)]], 1)))
    for l in range(2):
        chunks += [pack(x["ada_w_2"][l][:, 512 * c:512 * (c + 1)]) for c in range(18)]
    ev = x["ev_w_in_2"][0]
    chunks += [pack(ev[:, 0:512]), pack(ev[:, 1280:1792]), pack(ev[:, 768:1280])]
    chunks += [pack(x["ev_w_out_2"][0][:, 512 * c:512 * (c + 1)]) for c in range(2)]
    od = x["od_w_in_2"][0]
    chunks += [pack(od[:, 512 * c:512 * (c + 1)]) for c in (1, 2, 3, 0)]
    chunks += [pack(x["od_w_out_2"][0][:, 512 * c:512 * (c + 1)]) for c in range(2)]
    assert len(chunks) == W8_N, (len(chunks), W8_N)
    d = {"w8": np.stack(chunks)}
    d["w22"] = np.stack([pack(dn[:, 256 * c:256 * (c + 1)]) for _, dn in ffs for c in range(4)])
    d["w4"] = np.stack([x["lru_w_gates"][0].transpose(2, 0, 1, 3).reshape(P, 2048), pack(ev[:, 512:768])])
    vec = np.zeros((P, VN), np.float32)

    def put(name, a):
        at, n = VOFF[name]
        a = np.asarray(a)
        vec[:a.shape[0], at:at + n] = a.reshape(a.shape[0], n)

    put("norm_g", col(x["norm_g"][0]))
    put("conv_w", col(x["conv_w"][0]))
    put("conv_b", col(x["conv_b"][0]))
    put("b_gates", col(x["lru_b_gates"][0]))
    put("lam", col(x["lru_lambda"][0]))
    put("gla_ba", col(x["gla_ba"][0]))
    put("gla_norm", col(x["gla_norm"][0]))
    put("c", np.stack([col(x["c_2"][0]), col(x["c_ctx_2"])], axis=2))
    put("ada_b", col(x["ada_b_2"]))
    put("norm_g2", col(x["norm_g_2"]))
    for name, src in (("qg_ev", "a_q_gain_2"), ("kg_ev", "a_k_gain_2"), ("qg_od", "d_q_gain_2"),
                      ("kg_od", "d_k_gain_2")):
        put(name, np.tile(x[src][0], 2)[:, None])
    put("c_scale", col(x["c_scale_2"][0]))
    put("sink", np.broadcast_to(x["a_sink_2"][0][None, :], (P, 8)))
    put("pos_k", col(x["cmp_pos"][0, 0]))
    put("pos_v", col(x["cmp_pos"][0, 1]))
    put("w2k", pack(np.tile(x["cmp_w2"][0, 0], (1, 2))))
    put("w2v", pack(x["cmp_w2"][0, 1]))
    order = np.arange(16).reshape(4, 2, 2).transpose(0, 2, 1).ravel()
    gate = cols(o_gate, o_gate + 48).reshape(D, 3, 16)[:, :, order].reshape(D, 48)
    put("w_small", pack(cat([gate, cols(o_lr, o_lr + 16)], 1)))
    put("wa2", x["gla_wa2"][0])
    d["vec"] = vec
    d["cst"] = constants()
    d["tbl"] = x["rel_table"][:, order]
    d["rpb"] = x["d_rpb_2"][0].reshape(120, 31)
    d["ev_small"] = cat([np.broadcast_to(x["b_v_gain_2"], (P, 512)),
                         np.repeat(x["b_bias_2"][0].reshape(4, 2, 128), 64, axis=1).transpose(1, 0, 2).reshape(P, 512),
                         x["b_ws_2"][0].transpose(2, 0, 1).reshape(P, 1024)], axis=1)
    d["pool_w"] = x["c_w_pool_2"][0].transpose(1, 0, 2).reshape(P, 512)
    d["x"] = x["x"][0].T.reshape(KT, P, S)
    d["ctx"] = x["ctx_2"][0].T.reshape(KT, P, CL)
    d = {k: np.ascontiguousarray(v) for k, v in d.items()}

    nc = _bacc.Bacc("TRN2", target_bir_lowering=False, num_devices=1)
    f32 = mybir.dt.float32
    aps = {k: nc.dram_tensor(f"in_{k}", v.shape, f32, kind="ExternalInput").ap() for k, v in d.items()}
    out = nc.dram_tensor("out_x", (KT, P, S), f32, kind="ExternalOutput").ap()
    build(nc, aps, out)
    r = _run(nc, [{f"in_{k}": v for k, v in d.items()}], core_ids=[0])
    y = np.asarray(r.results[0]["out_x"])
    return np.ascontiguousarray(y.reshape(D, S).T)[None]
```

```python
import math
from contextlib import ExitStack

import numpy as np
import concourse.bass as bass
from concourse import mybir

P = 128
D = 1024
KT = D // P
S = 256
CL = 256
TOK = S + CL
FF = 2816
FT = FF // P
GROUPS = ((0, 8), (8, 8), (16, 6))
FFN_CHUNKS = 17
FFN_HALVES = 2 * FFN_CHUNKS
LRU, NSAW, GKW, GVW = 1024, 1024, 512, 1024
HD = 64
CMP_N = S // 16 - 1
NEG = -1e30
EPS = 1e-6
NSLOT = 3
W8 = KT * 512
SLOT = W8
HALF = W8 // 2
NSPLIT = 3
BANK = 512
NG = 4

VEC = [("norm_g", 32), ("conv_w", 32), ("conv_b", 8), ("b_gates", 16), ("lam", 8), ("gla_ba", 4),
       ("gla_norm", 2), ("c", 16), ("ada_b", 144), ("norm_g2", 48), ("qg_ev", 1), ("kg_ev", 1),
       ("qg_od", 1), ("kg_od", 1), ("c_scale", 4), ("sink", 8), ("pos_k", 16), ("pos_v", 16),
       ("w2k", 256), ("w2v", 128), ("w_small", 512), ("wa2", 512), ("tbl", 16)]
CST = [("ident", 128), ("ones", 128), ("blk64", 128), ("flip", 128), ("rope_r", 128),
       ("oh_fwd", 512), ("oh_rev", 384), ("valid_c", 2 * CMP_N), ("gla_mask", 128), ("scan_mask", S),
       ("win_mask", 2 * S), ("rope_c", S), ("rope_s", S), ("eps", 1), ("one", 1), ("ada_sel", 2)]
CST_OD = [("na_mask", 2 * S), ("inv_count", 4 * S)]


def offsets(table):
    at, out = 0, {}
    for name, n in table:
        out[name] = (at, n)
        at += n
    return out, at


VOFF, VN = offsets(VEC)
COFF, CN = offsets(CST)


def constants():
    c = np.zeros((P, CN), np.float32)

    def put(name, a):
        at, n = COFF[name]
        a = np.asarray(a, np.float32)
        c[:a.shape[0], at:at + n] = a.reshape(a.shape[0], n)

    put("ident", np.eye(P))
    put("ones", np.ones((P, P)))
    put("blk64", np.kron(np.eye(2), np.ones((64, 64))))
    put("flip", np.eye(P)[::-1])
    r = np.zeros((P, P))
    for i in range(P):
        if i % 32 < 16:
            r[i + 16, i] = -1.0
        else:
            r[i - 16, i] = 1.0
    put("rope_r", r)
    n = np.arange(0, 512)
    nf = np.maximum(n, 16).astype(np.float32)
    large = 16 + (np.log(nf / np.float32(16)) / np.float32(math.log(128 / 16)) * np.float32(16)).astype(np.int32)
    bucket = np.where(n < 16, n, np.minimum(large, 31))

    def onehot(dist):
        out = np.zeros((33, len(dist)), np.float32)
        for i, d in enumerate(dist):
            out[bucket[d] if d >= 0 else 32, i] = 1.0
        return out

    put("oh_fwd", onehot(np.arange(512) - 271))
    put("oh_rev", onehot(255 - np.arange(384)))
    t = np.arange(S)
    valid = (16 * np.arange(CMP_N) + 31)[None, :] <= t[:, None]
    put("valid_c", valid.reshape(2, P, CMP_N).transpose(1, 0, 2))
    s_, c_ = np.arange(P)[:, None], np.arange(P)[None, :]
    put("gla_mask", (s_ // 32 == c_ // 32) & (s_ <= c_))
    put("scan_mask", np.broadcast_to((t % 32 != 0), (P, S)))
    win = np.where(np.abs(t[:, None] - t[None, :]) <= 128, 0.0, NEG)
    put("win_mask", win.reshape(2, P, S).transpose(1, 0, 2))
    qc, kc = t[:, None] % 64, t[None, :] % 64
    start = np.clip(qc - 8, 0, 48)
    na = np.where((kc >= start) & (kc < start + 16), 0.0, NEG)
    inv = (1.0 / (np.float32(10000.0) ** (np.arange(16, dtype=np.float32) / np.float32(16)))).astype(np.float32)
    row, col = (t // 64).astype(np.float32), (t % 64).astype(np.float32)
    f = np.arange(P)
    ang = np.where((f % 64 < 32)[:, None], row[None, :], col[None, :]) * inv[f % 16][:, None]
    put("rope_c", np.cos(ang.astype(np.float32)))
    put("rope_s", np.sin(ang.astype(np.float32)))
    cnt = np.stack([np.clip(t + w - w // 2, 0, S) - np.clip(t - w // 2, 0, S) for w in (2, 4, 8, 16)])
    od = np.concatenate([na.reshape(2, P, S).transpose(1, 0, 2).reshape(P, 2 * S),
                         np.broadcast_to((1.0 / cnt).reshape(1, -1), (P, 4 * S))], axis=1).astype(np.float32)
    sel = np.zeros((P, 2))
    for g in range(4):
        sel[32 * g, 0] = sel[32 * g + 1, 1] = 1.0
    put("ada_sel", sel)
    put("eps", np.full((P, 1), EPS))
    put("one", np.ones((P, 1)))
    return c, od


def w8(i):
    return ("w8", i, W8)


W8_LRU_X, W8_LRU_G, W8_MERGE_A, W8_GQK, W8_GV, W8_OG, W8_MERGE_C = 0, 2, 4, 8, 10, 12, 14
W8_NQ, W8_KVC, W8_KSW, W8_VSW, W8_CW1, W8_MERGE_B, W8_OUT = 18, 20, 21, 22, 23, 25, 29
W8_ADA = 31
W8_EQ = W8_ADA + 36
W8_EO = W8_EQ + 3
W8_OD = W8_EO + 2
W8_OO = W8_OD + 4
W8_N = W8_OO + 2


def make_plan():
    plan = []

    def add(stage, chunk, who, free="tiles"):
        plan.append((stage, chunk, who, free))

    def ada(a, b):
        for c in range(a, b):
            add(f"ada{c}", w8(W8_ADA + c), "", "ada")

    def ffn(f):
        c = 0
        for g, (_, nf) in enumerate(GROUPS):
            for i in range(nf // 2):
                add(f"ffn{f}_in{g}_{2 * i}", ("wf", FFN_CHUNKS * f + c, W8), "AV", "split")
                add(f"ffn{f}_in{g}_{2 * i + 1}", None, "AV")
                c += 1
            for i in range(2):
                add(f"ffn{f}_out{g}_{2 * i}", ("wf", FFN_CHUNKS * f + c, nf * 512), "VV", "split")
                add(f"ffn{f}_out{g}_{2 * i + 1}", None, "VV")
                c += 1

    ada(0, 2)
    add("norm0", None, "A")
    for c in range(2):
        add(f"lru_x{c}", w8(W8_LRU_X + c), "AAAA")
    for c in range(2):
        add(f"lru_g{c}", w8(W8_LRU_G + c), "AAAA")
    add("strip", None, "V")
    add("cbias", None, "V")
    add("lru_gates", ("w4", 0, 2048), "A" * 16)
    add("gla_q", w8(W8_GQK), "AAAA")
    add("gla_k", w8(W8_GQK + 1), "AAAA")
    add("gla_lr", None, "A")
    add("gla_al", None, "AAAA")
    for c in range(2):
        add(f"gla_v{c}", w8(W8_GV + c), "VV")
    for c in range(2):
        add(f"gla_og{c}", w8(W8_OG + c), "AAAA")
    for c in range(4):
        add(f"mergeA{c}", w8(W8_MERGE_A + c), "AVAV")
    ada(2, 6)
    add("gla_t", None, "AA")
    add("gla_att", None, "VV")
    for c in range(2):
        add(f"nsa_q{c}", w8(W8_NQ + c), "AAAA")
    add("nsa_kvc", w8(W8_KVC), "AAAA")
    add("nsa_ksw", w8(W8_KSW), "AAAA")
    add("nsa_vsw", w8(W8_VSW), "VV")
    add("nsa_gate", None, "AA")
    add("gla_o", None, "A" * 8)
    add("gla_n", None, "AAAA")
    ada(6, 10)
    for c in range(4):
        add(f"mergeC{c}", w8(W8_MERGE_C + c), "AVAV")
    add("flip", None, "V" * 8)
    for i in range(2):
        add(f"cmp_hid{i}", w8(W8_CW1 + i), "AA")
    add("cmp_kv", None, "VV")
    ada(10, 14)
    for c in range(4):
        add(f"mergeB{c}", w8(W8_MERGE_B + c), "AVAV")
    ada(14, 18)
    for c in range(2):
        add(f"w_out{c}", w8(W8_OUT + c), "AAAA")
    add("norm1", None, "A")
    add("norm2", None, "A")
    ffn(0)
    add("norm3", None, "A")
    add("norm4", None, "A")
    ffn(1)
    add("norm5", None, "A")
    add("ev_q", w8(W8_EQ), "AAAA")
    add("ev_k", ("w4", 1, 2048), "A")
    add("ev_v", None, "VVVV")
    add("ev_bv", w8(W8_EQ + 1), "AAAA")
    add("ev_bu", w8(W8_EQ + 2), "AAAA")
    ada(18, 22)
    add("ev_qn", None, "A" * 5)
    add("ev_rope", None, "V" * 5)
    add("ev_mix", None, "V" * 4)
    ada(22, 36)
    for c in range(2):
        add(f"ev_out{c}", w8(W8_EO + c), "VVVV")
    add("norm6", None, "A")
    ffn(2)
    add("norm7", None, "A")
    ffn(3)
    add("norm8", None, "A")
    add("od_q", w8(W8_OD), "AAAA")
    add("od_k", w8(W8_OD + 1), "AAAA")
    add("od_v", w8(W8_OD + 2), "VVVV")
    add("od_xp", w8(W8_OD + 3), "AAAA")
    add("od_qn", None, "A" * 8)
    add("od_flip", None, "V" * 8)
    add("od_pool", None, "A" * 4)
    for c in range(2):
        add(f"od_out{c}", w8(W8_OO + c), "VVVV")
    add("norm9", None, "A")
    ffn(4)
    return plan


PLAN = make_plan()
TILE, WHO, CHUNKS, CHUNK_OF = {}, "", [], {}
_adas = _halves = 0
for _stage, _chunk, _who, _free in PLAN:
    TILE[_stage] = len(WHO)
    WHO += _who
    if _chunk is not None:
        CHUNK_OF[_stage] = len(CHUNKS)
        if _free == "ada":
            _adas += 1
            CHUNKS.append((_chunk, "ada_rows", _adas))
        elif _free == "split":
            _halves += 2
            CHUNKS.append((_chunk, "w_lo", _halves))
        else:
            CHUNKS.append((_chunk, "tiles_filled", len(WHO) + (4 if _stage == "ev_k" else 0)))
NTILES = len(WHO)


def emptied(n):
    return WHO[:n + 1].count(WHO[n])


UNITS = ([("nsa", g, t) for g in range(4) for t in range(2)]
         + [("ev", g, t) for g in range(2) for t in range(4)]
         + [("od", g, t) for g in range(2) for t in range(2)])
NSA_U, EV_U, OD_U = (0, 8), (8, 16), (16, 20)


def batches(u):
    kind, _, t = UNITS[u]
    if kind == "nsa":
        return [(seg, b) for seg in range(2) for b in range(t + 1)] + [(2, 0)]
    if kind == "ev" and t >= 2:
        return [(0, 2), (0, 3)]
    return [(0, b) for b in range(4)]


ADA_EV = [(22 + 2 * i, 23 + 2 * i) if i < 6 else (28 + i,) for i in range(8)]
ADA_BESIDE = range(22, 36)


def place(seg, r):
    return 4 * (r % 2) + 2 * seg + r // 2


def batches_before(u):
    return sum(len(batches(v)) for v in range(u))


def build(nc, d, out_x):
    f32 = mybir.dt.float32
    ACT = mybir.ActivationFunctionType
    ALU = mybir.AluOpType
    AX = mybir.AxisListType.X
    ctx = ExitStack()
    with ctx:
        def sb(name, width):
            return ctx.enter_context(nc.sbuf_tensor(name, [P, width], f32))

        xT_ = sb("xT", KT * TOK)
        zT_at = nc.sbuf_base
        zT_ = sb("zT", KT * TOK)
        cst = sb("cst", CN)
        vec = sb("vec", VN)
        ring = sb("ring", NSLOT * SLOT)
        rt = sb("rt", TOK)
        rr = sb("rr", TOK)
        mod_ = sb("mod", 2 * 144)
        modA_ = sb("modA", 2 * 48)
        gates_h_ = sb("gates_h", 2 * 32)
        mod, modA, gates_h = ([t[:, i * w:(i + 1) * w] for i in range(2)]
                              for t, w in ((mod_, 144), (modA_, 48), (gates_h_, 32)))
        cs = sb("cs", KT * 32)
        ab = sb("ada_partial", 2 * BANK)
        small = sb("small", 160)
        ARENA = 24976
        arena_at = nc.sbuf_base
        arena = sb("arena", ARENA)
        f32r = mybir.dt.float32r
        arena_r = nc.alloc_sbuf_tensor_at("arena_r", [P, ARENA], f32r, offset=arena_at)
        zT_r_ = nc.alloc_sbuf_tensor_at("zT_r", [P, KT * TOK], f32r, offset=zT_at)
        psum = ctx.enter_context(nc.psum_tensor("psum", [P, 8 * BANK], f32))
        strip_dram = nc.dram_tensor("strip_scratch", (16, 384), f32, kind="Internal").ap()
        rpb_dram = nc.dram_tensor("rpb_scratch", (120, 128), f32, kind="Internal").ap()

        xT = xT_[:, :].rearrange("p (k t) -> p k t", k=KT)
        zT = zT_[:, :].rearrange("p (k t) -> p k t", k=KT)
        z_lo = zT_r_[:, :].rearrange("p (k t) -> p k t", k=KT)

        def V(name, a=0, n=None):
            at, w = VOFF[name]
            return vec[:, at + a:at + (w if n is None else a + n)]

        def C(name):
            at, w = COFF[name]
            return cst[:, at:at + w]

        def area(at, *shape):
            n = int(np.prod(shape))
            assert at + n <= ARENA, (at, shape)
            v = arena[:, at:at + n]
            if len(shape) == 2:
                return v.rearrange("p (a b) -> p a b", a=shape[0])
            if len(shape) == 3:
                return v.rearrange("p (a b c) -> p a b c", a=shape[0], b=shape[1])
            return v

        def bank(n, width=BANK):
            return psum[:, (n % NG) * BANK:(n % NG) * BANK + width]

        def b3(ap, n, width):
            return ap.unsqueeze(1).to_broadcast([ap.shape[0], n, width])

        def rep(ap, n):
            return ap.unsqueeze(2).to_broadcast([ap.shape[0], ap.shape[1], n])

        CMP_AT = 4 * BANK

        def ada_banks(c):
            return (4, 4) if c in ADA_BESIDE else (4 + c % 2, 6 + c % 2)

        sems = {}

        def sig(name):
            if name not in sems:
                sems[name] = ctx.enter_context(nc.semaphore(name))
            return sems[name]

        landed = [sig(f"weights_landed{i}") for i in range(NSLOT)]
        filled = sig("tiles_filled")
        evac = {"A": sig("tiles_emptied_by_act"), "V": sig("tiles_emptied_by_dve")}

        def wait_evac(eng, n):
            eng.wait_ge(evac[WHO[n]], emptied(n))

        def fence(eng, name, others, k):
            eng.drain().then_inc(sig(f"fence_{name}"), 1)
            for o in others:
                eng.wait_ge(sig(f"fence_{o}"), k)

        A_xp = area(0, KT, S + 3)
        A_y = area(0, KT, S)
        A_xc = area(2072, KT, S)
        A_g = area(4120, KT, S)
        A_r = area(6168, KT, S)
        A_i = area(8216, KT, S)
        A_a = area(10264, KT, S)
        A_t = area(12312, KT, S)
        mgA_t = area(23576, 2, S)
        C_q = area(14360, 4, S)
        C_k = area(15384, 4, S)
        C_Y = area(16408, 4, S)
        C_e = area(17432, 4, S)
        C_b = area(18456, 4, S)
        C_lr = area(18456, S)
        C_v = area(19480, 2, GVW)
        C_og = area(21528, KT, S)
        C_st = area(0, 4, 7 * S)
        C_kt = area(7168, 8, P)
        C_at = area(8192, 8, P)
        C_o = area(16408, KT, S)
        mgC_t = area(7168, 2, S)
        B_q = area(9216, KT, S)
        B_kk = area(11264, 4, S)
        B_ks = area(12288, 4, S)
        B_v = area(13312, 2, BANK)
        B_kc = area(18456, 4, S)
        B_gate = area(23576, 2, 48)
        B_st = area(0, 2, 4, S)
        B_bl = area(2048, 2, 16, 60)
        B_hid = area(3968, 2, 2, 60)
        B_stage = area(4224, 16, S)
        B_kcT = area(8320, 60)
        B_vc = area(8384, 4, HD)
        B_P = area(0, 2108)
        B_PT = area(2108, 3, BANK)
        B_T = area(14360, 16, S)
        B_y = area(19480, KT, S)
        mgB_t = area(22000, 2, S)
        K_strip = area(24088, 384)
        K_C = area(24472, 480)
        B_C = area(24472, 2, 16, CMP_N)
        K_tbl = area(24952, 16)
        Y_y = area(14336, KT, S)

        def part(at, *shape):
            v = arena_r[:, at:at + int(np.prod(shape))]
            return v.rearrange("p (a b) -> p a b", a=shape[0]) if len(shape) == 2 else v

        W_hi = [part(i * W8, HALF) for i in range(NSPLIT)]
        W_lo = [part(i * W8 + HALF, HALF) for i in range(NSPLIT)]

        def z_hi(nt):
            return part(12288, KT, nt)

        def a_parts(nt):
            return part(16384, KT, nt), part(20480, KT, nt)

        E_qk = area(0, 5, TOK)
        E_ks = area(2560, TOK)
        E_u = area(3072, 4, TOK)
        E_v = area(5120, 4, P)
        E_bv = area(5632, 4, BANK)
        E_y = area(7680, KT, TOK)
        E_P = area(11776, 4 * BANK)
        E_sq = area(11776, 4, BANK)
        E_PT = area(13824, 3, BANK)
        E_w = area(15360, 2048)
        E_rt = area(17408, 5, TOK)
        O_q = area(0, 4, S)
        O_k = area(1024, 4, TOK)
        O_v = area(3072, 4, BANK)
        O_xp = area(5120, 4, S + 16)
        O_s1 = area(6208, 4, S + 16)
        O_s2 = area(7296, 4, S + 16)
        O_y = area(8384, KT, S)
        O_P = area(10432, 4 * BANK)
        O_stage = area(8384, 2 * 8, S)
        O_PT = area(12480, 3, BANK)
        O_nb = area(14016, 2 * 8, S)
        O_wp = area(18112, 4 * P)
        O_tmp = area(18624, 2, TOK)
        PAD = area(19900, 128)
        O_cst = area(20028, 6 * S)
        O_na = area(20028, 2, S)
        O_ic = area(20540, 4, S)

        MODN = {4: (0, TOK), 5: (1, TOK), 6: (2, TOK), 7: (0, TOK), 8: (1, TOK), 9: (2, S)}

        def norm_xr_before(q):
            return KT * sum(1 for p in MODN if p < q)

        SPLIT = (2, 4, 6, 7, 9)

        def norm_hi_before(q):
            return KT * sum(1 for p in SPLIT if p < q)

        def halves(f):
            out = []
            for g, (_, nf) in enumerate(GROUPS):
                out += [(g, i, False) for i in range(nf)] + [(g, i, True) for i in range(4)]
            return out

        def half_first_tile(h):
            f, (g, i, second) = h // FFN_HALVES, HALVES[h % FFN_HALVES]
            return TILE[f"ffn{f}_{'out' if second else 'in'}{g}_{i}"]

        HALVES = halves(0)

        def half_width(h):
            g, _, second = HALVES[h % FFN_HALVES]
            return GROUPS[g][1] * 256 if second else HALF

        def norm_zc_before(q):
            return KT * sum(1 for p, (_, n) in MODN.items() if p < q and n == TOK)

        block = ctx.enter_context(nc.Block())

        @block.sync
        def _(sp):
            sp.dma_start(xT[:, :, 0:S], d["x"].rearrange("k p t -> p k t")).then_inc(sig("x_in"), 16)
            sp.dma_start(cst[:, :], d["cst"]).then_inc(sig("cst_in"), 16)
            sp.dma_start(vec[:, :], d["vec"]).then_inc(sig("vec_in"), 16)
            for i, ((arr, idx, size), _, _) in enumerate(CHUNKS):
                if i >= NSLOT:
                    _, name, count = CHUNKS[i - NSLOT]
                    sp.wait_ge(sig(name), count)
                slot = i % NSLOT
                sp.dma_start(ring[:, slot * SLOT:slot * SLOT + size], d[arr][idx, :, 0:size])\
                    .then_inc(landed[slot], 16)
            wait_evac(sp, NTILES - 1)
            sp.dma_start(out_x.rearrange("k p t -> p k t"), xT[:, :, 0:S]).then_inc(sig("out_written"), 16)
            sp.wait_ge(sig("out_written"), 16)

        @block.gpsimd
        def _(pool):
            pool.memset(cs[:, :], 0.0).then_inc(sig("cs_zero"), 1)
            pool.wait_ge(sig("cs_zero"), 1)
            pool.memset(K_tbl[32:33, :], NEG).then_inc(sig("tbl_row"), 1)
            pool.dma_start(K_tbl[0:32, :], d["tbl"]).then_inc(sig("tbl_in"), 16)
            pool.wait_ge(sig("x_in"), 16)
            pool.dma_start(xT[:, :, S:TOK], d["ctx"].rearrange("k p t -> p k t")).then_inc(sig("ctx_in"), 16)
            wait_evac(pool, TILE["strip"])
            pool.dma_start(strip_dram, K_strip[0:16, :]).then_inc(sig("strip_out"), 16)
            pool.wait_ge(sig("strip_out"), 16)
            fence(pool, "pool", ("pe", "act", "dve"), 1)
            fence(pool, "pool", ("pe", "act", "dve"), 2)
            src = bass.AP(tensor=strip_dram.tensor, offset=0, ap=[[1, P], [384, 16], [1, S]])
            pool.dma_start(B_stage, src).then_inc(sig("stage_in"), 16)
            for c in range(2):
                n = TILE["nsa_kvc"] + 2 * c + 1
                wait_evac(pool, n)
                for g in range(4):
                    half = slice(64 * (g % 2), 64 * (g % 2) + 64)
                    src = B_kc[half, 2 * c + g // 2, :]
                    pool.dma_start(B_st[0:64, c, g, :], src).then_inc(sig("stack_in"), 16)
                    pool.dma_start(B_st[64:128, c, g, 0:S - 1], src[:, 1:S]).then_inc(sig("stack_in"), 16)
            wait_evac(pool, TILE["nsa_ksw"] + 3)
            pool.dma_start(B_ks[0:64, :, :], B_kk[64:128, :, :]).then_inc(sig("kswap_in"), 16)
            pool.dma_start(B_ks[64:128, :, :], B_kk[0:64, :, :]).then_inc(sig("kswap_in"), 16)
            for k in range(3, 5):
                fence(pool, "pool", ("pe", "act", "dve"), k)

            def norm_ctx(q, li, j):
                for k in range(KT):
                    pool.wait_ge(sig("norm_xr"), norm_xr_before(q) + k + 1)
                    pool.tensor_scalar(out=zT[:, k, S:TOK], in0=zT[:, k, S:TOK],
                                       scalar1=modA[li][:, 2 * (8 * j + k) + 1:2 * (8 * j + k) + 2],
                                       scalar2=mod[li][:, 2 * (24 * j + k) + 1:2 * (24 * j + k) + 2],
                                       op0=ALU.mult, op1=ALU.add).then_inc(sig("norm_zc"), 1)

            def ffn_parts(f, nt):
                hi, lo = a_parts(nt)
                for g, (k0, nf) in enumerate(GROUPS):
                    if g > 0:
                        pool.wait_ge(filled, TILE[f"ffn{f}_out{g - 1}_3"] + 2)
                    for i in range(nf):
                        a = (rt, rr)[i % 2][:, 0:nt]
                        wait_evac(pool, TILE[f"ffn{f}_in{g}_{i}"] + 1)
                        n = FT * f + k0 + i + 1
                        pool.tensor_copy(hi[:, i, :], a).then_inc(sig("a_hi"), 1)
                        pool.wait_ge(sig("a_hi"), n)
                        pool.tensor_tensor(out=lo[:, i, :], in0=a, in1=hi[:, i, :].bitcast(f32), op=ALU.subtract)\
                            .then_inc(sig("a_lo"), 1)

            ffn_parts(0, S)
            norm_ctx(4, 0, 0)
            ffn_parts(1, TOK)
            norm_ctx(5, 0, 1)
            fence(pool, "pool", ("pe", "act", "dve"), 5)
            pool.dma_start(E_w, d["ev_small"]).then_inc(sig("ev_small_in"), 16)
            wait_evac(pool, TILE["ev_rope"] + 4)
            pool.dma_start(E_ks[0:64, :], E_qk[64:128, 4, :]).then_inc(sig("ekswap_in"), 16)
            pool.dma_start(E_ks[64:128, :], E_qk[0:64, 4, :]).then_inc(sig("ekswap_in"), 16)
            fence(pool, "pool", ("pe", "act", "dve"), 6)
            norm_ctx(6, 0, 2)
            ffn_parts(2, TOK)
            norm_ctx(7, 1, 0)
            ffn_parts(3, TOK)
            norm_ctx(8, 1, 1)
            fence(pool, "pool", ("pe", "act", "dve"), 7)
            pool.dma_start(O_cst, d["cst_od"]).then_inc(sig("cst_od_in"), 16)
            pool.memset(PAD[0:120, :], NEG).then_inc(sig("pad_set"), 1)
            pool.wait_ge(sig("pad_set"), 1)
            pool.dma_start(PAD[0:120, 48:79], d["rpb"]).then_inc(sig("rpb_in"), 16)
            pool.wait_ge(sig("rpb_in"), 16)
            pool.dma_start(rpb_dram, PAD[0:120, :]).then_inc(sig("rpb_out"), 16)
            pool.wait_ge(sig("rpb_out"), 16)
            for t in range(2):
                for r in range(2):
                    for kr in range(4):
                        row = kr - (2 * t + 1 - r) + 7
                        src = bass.AP(tensor=rpb_dram.tensor, offset=row * 128,
                                      ap=[[1, 64], [15 * 128, 8], [1, 64]])
                        pool.dma_start(O_stage[64 * r:64 * r + 64, 8 * t:8 * t + 8, 64 * kr:64 * kr + 64], src)\
                            .then_inc(sig("rpb_stage"), 16)
            pool.dma_start(O_wp, d["pool_w"]).then_inc(sig("pool_w_in"), 16)
            fence(pool, "pool", ("pe", "act", "dve"), 8)
            fence(pool, "pool", ("pe", "act", "dve"), 9)
            ffn_parts(4, S)

        @block.tensor
        def _(pe):
            mm = nc.tensor.matmul

            def get(stage):
                i = CHUNK_OF[stage]
                pe.wait_ge(landed[i % NSLOT], 16 * (i // NSLOT + 1))
                size = CHUNKS[i][0][2]
                return ring[:, (i % NSLOT) * SLOT:(i % NSLOT) * SLOT + size]

            def open_tile(n):
                if n >= NG:
                    wait_evac(pe, n - NG)
                return bank(n)

            def feature_tiles(stage, w, cols, rhs, nt, nk=KT, first=None):
                for j, c in enumerate(cols):
                    n = TILE[stage] + j
                    b = open_tile(n)
                    for k in range(nk):
                        if j == 0 and first is not None:
                            first(k)
                        last = mm(b[:, 0:nt], w[:, k, c:c + P], rhs(k), start=(k == 0), stop=(k == nk - 1))
                    last.then_inc(filled, 1)

            def token_tiles(stage, w, lhs, ntt, c0, width, nk=KT):
                for j in range(ntt):
                    n = TILE[stage] + j
                    b = open_tile(n)
                    for k in range(nk):
                        last = mm(b[:, 0:width], lhs(k, j), w[:, k, c0:c0 + width],
                                  start=(k == 0), stop=(k == nk - 1))
                    last.then_inc(filled, 1)

            def w3(stage, nk=KT):
                return get(stage).rearrange("p (k n) -> p k n", k=nk)

            def norm(q, nt):
                b = open_tile(TILE[f"norm{q}"])
                pe.wait_ge(sig("norm_sum"), q + 1)
                mm(b[:, 0:nt], C("ones"), rr[:, 0:nt], start=True, stop=True).then_inc(filled, 1)

            def normed(q):
                def first(k):
                    if q in (0, 2):
                        pe.wait_ge(sig("norm_z"), (KT if q == 2 else 0) + k + 1)
                    else:
                        pe.wait_ge(sig("norm_zm"), norm_xr_before(q) + k + 1)
                        if MODN[q][1] == TOK:
                            pe.wait_ge(sig("norm_zc"), norm_zc_before(q) + k + 1)
                return first

            def ada_rows(c):
                w = w3(f"ada{c}")
                if c in ADA_BESIDE:
                    pe.wait_ge(sig("ada_done"), c)
                elif c >= 2:
                    pe.wait_ge(sig("ada_copied"), c - 1)
                at = ada_banks(c)[0] * BANK
                for k in range(KT):
                    g = k % 4
                    last = mm(psum[32 * g:32 * g + 32, at:at + BANK], cs[:, 32 * k:32 * k + 32], w[:, k, :],
                              start=(k < 4), stop=(k >= 4), skip_group_check=True)
                last.then_inc(sig("ada_rows"), 1)

            def ada_cols(c):
                pe.wait_ge(sig("ada_copied"), c + 1)
                if c >= 2:
                    pe.wait_ge(sig("ada_done"), c - 1)
                to = ada_banks(c)[1] * BANK
                for j in range(4):
                    at = (c % 2) * BANK + j * P
                    last = mm(psum[:, to + 2 * j:to + 2 * j + 2], ab[:, at:at + P], C("ada_sel"),
                              start=True, stop=True)
                last.then_inc(sig("ada_cols"), 1)

            def ada(a, b_):
                for c in range(a, b_):
                    ada_rows(c)
                    if c > a:
                        ada_cols(c - 1)
                ada_cols(b_ - 1)

            def ffn(f, nt, q):
                hi, lo = a_parts(nt)
                zh = z_hi(nt)
                for i, (g, j, second) in enumerate(HALVES):
                    h = FFN_HALVES * f + i
                    nk = GROUPS[g][1] if second else KT
                    wh = W_hi[h % NSPLIT][:, 0:nk * 256].rearrange("p (k n) -> p k n", k=nk)
                    wl = W_lo[h % NSPLIT][:, 0:nk * 256].rearrange("p (k n) -> p k n", k=nk)
                    pe.wait_ge(sig("w_lo"), h + 1)
                    for c in range(2):
                        b = open_tile(half_first_tile(h) + c)
                        for k in range(nk):
                            if i == 0 and c == 0:
                                pe.wait_ge(sig("norm_lo"), norm_hi_before(q) + k + 1)
                            if second and j == 0 and c == 0:
                                pe.wait_ge(sig("a_lo"), FT * f + GROUPS[g][0] + k + 1)
                            xh, xl = (hi, lo) if second else (zh, z_lo)
                            mm(b[:, 0:nt], wh[:, k, c * P:(c + 1) * P], xh[:, k, 0:nt], start=(k == 0), stop=False)
                            mm(b[:, 0:nt], wh[:, k, c * P:(c + 1) * P], xl[:, k, 0:nt], start=False, stop=False)
                            last = mm(b[:, 0:nt], wl[:, k, c * P:(c + 1) * P], xh[:, k, 0:nt],
                                      start=False, stop=(k == nk - 1))
                        last.then_inc(filled, 1)

            def merge(br, y, ready):
                for c in range(4):
                    stage = f"merge{br}{c}"
                    w = w3(stage)
                    for j in range(2):
                        for half in range(2):
                            n = TILE[stage] + 2 * j + half
                            b = open_tile(n)
                            if half and c == 0 and j == 0:
                                ready()
                            for k in range(KT):
                                last = mm(b[:, 0:S], w[:, k, 256 * half + P * j:256 * half + P * j + P],
                                          y[:, k, :] if half else zT[:, k, 0:S], start=(k == 0), stop=(k == KT - 1))
                            last.then_inc(filled, 1)

            hrhs = lambda k: zT[:, k, 0:S]

            pe.wait_ge(sig("cst_in"), 16)
            pe.wait_ge(sig("vec_in"), 16)
            pe.wait_ge(sig("cs_ready"), 1)
            ada(0, 2)
            norm(0, S)
            for c in range(2):
                feature_tiles(f"lru_x{c}", w3(f"lru_x{c}"), range(0, 512, P), hrhs, S,
                              first=normed(0) if c == 0 else None)
            for c in range(2):
                feature_tiles(f"lru_g{c}", w3(f"lru_g{c}"), range(0, 512, P), hrhs, S)
            pe.wait_ge(sig("tbl_in"), 16)
            pe.wait_ge(sig("tbl_row"), 1)
            oh = C("oh_rev")
            b = open_tile(TILE["strip"])
            mm(b[0:16, 0:384], K_tbl[0:33, :], oh[0:33, :], start=True, stop=True).then_inc(filled, 1)
            oh = C("oh_fwd")
            b = open_tile(TILE["cbias"])
            for t in range(2):
                for c in range(CMP_N):
                    at = P * t - 16 * c - 31 + 271
                    col = (t * CMP_N + c) * 16
                    last = mm(b[:, col:col + 16], oh[0:33, at:at + P], K_tbl[0:33, :], start=True, stop=True)
            last.then_inc(filled, 1)
            w = get("lru_gates").rearrange("p (g n e) -> p g n e", g=2, n=8)
            for k in range(KT):
                pe.wait_ge(sig("lru_xc"), k + 1)
                for g in range(2):
                    n = TILE["lru_gates"] + 2 * k + g
                    b = open_tile(n)
                    mm(b[:, 0:S], w[:, g, k, :], A_xc[:, k, :], start=True, stop=True).then_inc(filled, 1)
            feature_tiles("gla_q", w3("gla_q"), range(0, 512, P), hrhs, S)
            feature_tiles("gla_k", w3("gla_k"), range(0, 512, P), hrhs, S)
            wsm = V("w_small").rearrange("p (k n) -> p k n", k=KT)
            b = open_tile(TILE["gla_lr"])
            for k in range(KT):
                last = mm(b[0:16, 0:S], wsm[:, k, 48:64], zT[:, k, 0:S], start=(k == 0), stop=(k == KT - 1))
            last.then_inc(filled, 1)
            wait_evac(pe, TILE["gla_lr"])
            for h in range(4):
                b = open_tile(TILE["gla_al"] + h)
                mm(b[:, 0:S], V("wa2", h * P, P)[0:16, :], C_lr[0:16, :], start=True, stop=True).then_inc(filled, 1)
            for c in range(2):
                token_tiles(f"gla_v{c}", w3(f"gla_v{c}"), lambda k, j: zT[:, k, j * P:(j + 1) * P], 2, 0, 512)
            for c in range(2):
                feature_tiles(f"gla_og{c}", w3(f"gla_og{c}"), range(0, 512, P), hrhs, S)
            merge("A", A_y, lambda: pe.wait_ge(sig("lru_y"), KT))
            ada(2, 6)
            fence(pe, "pe", ("act", "dve", "pool"), 1)

            pe.wait_ge(sig("gla_kend"), 1)
            for t in range(2):
                b = open_tile(TILE["gla_t"] + t)
                for h in range(4):
                    last = nc.tensor.transpose(b[:, h * P:(h + 1) * P], C_e[:, h, t * P:(t + 1) * P], C("ident"))
                last.then_inc(filled, 1)
            for t in range(2):
                b = open_tile(TILE["gla_att"] + t)
                for h in range(4):
                    last = mm(b[:, h * P:(h + 1) * P], C_k[:, h, t * P:(t + 1) * P], C_q[:, h, t * P:(t + 1) * P],
                              start=True, stop=True)
                last.then_inc(filled, 1)
            wait_evac(pe, TILE["gla_t"] + 1)
            between = [lambda: feature_tiles("nsa_q0", w3("nsa_q0"), range(0, 512, P), hrhs, S),
                       lambda: feature_tiles("nsa_q1", w3("nsa_q1"), range(0, 512, P), hrhs, S),
                       lambda: feature_tiles("nsa_kvc", w3("nsa_kvc"), range(0, 512, P), hrhs, S),
                       lambda: feature_tiles("nsa_ksw", w3("nsa_ksw"), range(0, 512, P), hrhs, S),
                       lambda: token_tiles("nsa_vsw", w3("nsa_vsw"), lambda k, j: zT[:, k, j * P:(j + 1) * P],
                                           2, 0, 512),
                       lambda: token_tiles("nsa_gate", wsm, lambda k, j: zT[:, k, j * P:(j + 1) * P], 2, 0, 48)]
            for c in range(7):
                for h in range(4):
                    if c >= 1:
                        pe.wait_ge(sig("gla_state"), 4 * (c - 1) + h + 1)
                    rows = slice(32 * (c % 4), 32 * (c % 4) + 32)
                    mm(psum[:, (4 + h) * BANK:(4 + h) * BANK + S], C_kt[rows, 4 * (c // 4) + h, :],
                       C_v[rows, c // 4, h * S:(h + 1) * S], start=True, stop=True,
                       tile_position=(32 * (c % 4), 0)).then_inc(sig("gla_upd"), 1)
                if c < len(between):
                    between[c]()
            wait_evac(pe, TILE["gla_att"] + 1)
            pe.wait_ge(sig("gla_state"), 28)
            for h in range(4):
                for e in range(2):
                    n = TILE["gla_o"] + 2 * h + e
                    b = open_tile(n)
                    for t in range(2):
                        mm(b[:, t * P:(t + 1) * P], C_v[:, t, h * S + e * P:h * S + (e + 1) * P],
                           C_at[:, 4 * t + h, :], start=(t == 0), stop=False, skip_group_check=True)
                    for c in range(1, 8):
                        st = C_st[:, h, (c - 1) * S + e * P:(c - 1) * S + (e + 1) * P]
                        last = mm(b[:, 32 * c:32 * c + 32], st, C_q[:, h, 32 * c:32 * c + 32],
                                  start=False, stop=(c == 7), skip_group_check=True)
                    last.then_inc(filled, 1)
            for h in range(4):
                b = open_tile(TILE["gla_n"] + h)
                pe.wait_ge(sig("gla_sq"), 2 * h + 2)
                for e in range(2):
                    last = mm(b[:, 0:S], C("ones"), C_st[:, h, e * S:(e + 1) * S], start=(e == 0), stop=(e == 1))
                last.then_inc(filled, 1)
            ada(6, 10)
            merge("C", C_og, lambda: pe.wait_ge(sig("gla_y"), KT))
            fence(pe, "pe", ("act", "dve", "pool"), 2)

            def scores(u):
                kind, g, t = UNITS[u]
                if u > 0:
                    pe.wait_ge(sig("att_exp"), u)
                if kind == "nsa":
                    nk = P * (t + 1)

                    def compressed(a):
                        half = slice(64 * a, 64 * a + 64)
                        for j in range(2):
                            at = CMP_AT + (2 * a + j) * CMP_N
                            last = mm(psum[:, at:at + CMP_N], B_q[half, 2 * g + j, t * P:(t + 1) * P],
                                      B_kcT[half, g * CMP_N:(g + 1) * CMP_N], start=True, stop=True)
                        return last

                    compressed(0).then_inc(sig("cmp_even"), 1)
                    for r in range(4):
                        half = slice(64 * (r % 2), 64 * (r % 2) + 64)
                        for seg in range(2):
                            kk = (B_kk if g % 2 == r % 2 else B_ks)[half, 2 * seg + g // 2, 0:nk]
                            at = place(seg, r) * S
                            mm(psum[:, at:at + nk], B_q[half, 2 * g + r // 2, t * P:(t + 1) * P], kk,
                               start=True, stop=True)
                    pe.wait_ge(sig("cmp_even"), u + 1)
                    last = compressed(1)
                else:
                    ev = kind == "ev"
                    k0 = S if t >= 2 else 0
                    for r in range(4):
                        h = 4 * g + r
                        half = slice(64 * (r % 2), 64 * (r % 2) + 64)
                        if ev:
                            q = E_qk[half, h // 2, t * P:(t + 1) * P]
                            kk = (E_qk[half, 4, k0:TOK] if g == r % 2 else E_ks[half, k0:TOK])
                        else:
                            q = O_q[half, h // 2, t * P:(t + 1) * P]
                            kk = O_k[half, h // 2, 0:TOK]
                        last = mm(psum[:, r * BANK + k0:(r + 1) * BANK], q, kk, start=True, stop=True)
                last.then_inc(sig("att_score"), 1)

            def att_out(u, Pb, PT):
                kind, g, t = UNITS[u]
                bs = batches(u)
                gb0 = batches_before(u)

                def keys(i):
                    return CMP_N if bs[i][0] == 2 else P

                def turn(i):
                    seg, blk = bs[i]
                    gb = gb0 + i
                    if gb >= 2:
                        pe.wait_ge(sig("att_copied"), gb - 1)
                    pt = psum[:, (5 + gb % 2) * BANK:(6 + gb % 2) * BANK]
                    for r in range(4):
                        if kind == "nsa":
                            at = 2048 + (2 * (r % 2) + r // 2) * CMP_N if seg == 2 else place(seg, r) * S + blk * P
                        else:
                            at = r * BANK + blk * P
                        last = nc.tensor.transpose(pt[0:keys(i), r * P:(r + 1) * P], Pb[:, at:at + keys(i)],
                                                   C("ident"))
                    last.then_inc(sig("att_turned"), 1)

                def multiply(i):
                    seg, blk = bs[i]
                    gb = gb0 + i
                    pe.wait_ge(sig("att_copied"), gb + 1)
                    if i == 0 and u > 0:
                        pe.wait_ge(sig("att_out"), u)
                    pt = PT[0:keys(i), gb % 3, :].rearrange("p (j a t) -> p a j t", j=2, a=2)
                    for a in range(2):
                        o = psum[64 * a:64 * a + 64, 7 * BANK:7 * BANK + 2 * P]
                        if kind == "od":
                            for j in range(2):
                                h = 4 * g + 2 * j + a
                                last = mm(o[:, j * P:(j + 1) * P], O_v[:, blk, h * HD:(h + 1) * HD], pt[:, a, j, :],
                                          start=(i == 0 and j == 0), stop=(i == len(bs) - 1 and j == 1),
                                          skip_group_check=True)
                        else:
                            if kind == "ev":
                                v = E_v[:, blk, g * HD:(g + 1) * HD]
                            elif seg == 2:
                                v = B_vc[0:CMP_N, g, :]
                            else:
                                v = B_v[:, blk, seg * S + g * HD:seg * S + (g + 1) * HD]
                            last = mm(o.rearrange("p (j t) -> p j t", j=2), v, pt[:, a, :, :],
                                      start=(i == 0), stop=(i == len(bs) - 1), skip_group_check=True)
                    last.then_inc(sig("att_mult"), 1)

                pe.wait_ge(sig("att_p"), u + 1)
                for i in range(len(bs)):
                    turn(i)
                    if i >= 1:
                        multiply(i - 1)
                multiply(len(bs) - 1)

            def attention(u0, u1, Pb, PT, ready, extra):
                ready()
                scores(u0)
                for u in range(u0, u1):
                    for c in extra(u - u0):
                        ada_rows(c)
                        ada_cols(c)
                    if u + 1 < u1:
                        scores(u + 1)
                    att_out(u, Pb, PT)

            pe.wait_ge(sig("stage_in"), 16)
            for i in range(8):
                b = open_tile(TILE["flip"] + i)
                mm(b[:, :], C("flip"), area(4224 + i * BANK, BANK), start=True, stop=True).then_inc(filled, 1)
            for i in range(2):
                w = w3(f"cmp_hid{i}", 16)
                pe.wait_ge(sig("cmp_blocks"), 4 * i + 4)
                for hh in range(2):
                    n = TILE[f"cmp_hid{i}"] + hh
                    b = open_tile(n)
                    for m in range(16):
                        last = mm(b[:, 0:60], w[:, m, hh * P:(hh + 1) * P], B_bl[:, i, m, :],
                                  start=(m == 0), stop=(m == 15))
                    last.then_inc(filled, 1)
            wait_evac(pe, TILE["cmp_hid1"] + 1)
            b = open_tile(TILE["cmp_kv"])
            w2k = V("w2k").rearrange("p (k n) -> p k n", k=2)
            w2v = V("w2v").rearrange("p (k n) -> p k n", k=2)
            for k in range(2):
                last = mm(b[:, 0:60], w2k[:, k, :], B_hid[:, 0, k, :], start=(k == 0), stop=(k == 1))
            last.then_inc(filled, 1)
            b = open_tile(TILE["cmp_kv"] + 1)
            for g in range(4):
                for k in range(2):
                    last = mm(b[0:CMP_N, g * HD:(g + 1) * HD], B_hid[:, 1, k, g * CMP_N:(g + 1) * CMP_N],
                              w2v[:, k, :], start=(k == 0), stop=(k == 1))
            last.then_inc(filled, 1)
            ada(10, 14)

            def nsa_ready():
                pe.wait_ge(sig("ada_done"), 14)
                wait_evac(pe, TILE["cmp_kv"] + 1)
                pe.wait_ge(sig("kswap_in"), 32)

            fence(pe, "pe", ("act", "dve", "pool"), 3)
            attention(*NSA_U, B_P, B_PT, nsa_ready, lambda i: ())
            merge("B", B_y, lambda: pe.wait_ge(sig("att_out"), NSA_U[1]))
            ada(14, 18)
            wait_evac(pe, TILE["mergeB3"] + 3)
            for c in range(2):
                feature_tiles(f"w_out{c}", w3(f"w_out{c}"), range(0, 512, P), lambda k: zT[:, k, S:TOK], S)
            fence(pe, "pe", ("act", "dve", "pool"), 4)
            norm(1, S)
            norm(2, S)
            ffn(0, S, 2)
            norm(3, S)

            norm(4, TOK)
            ffn(1, TOK, 4)
            norm(5, TOK)
            fence(pe, "pe", ("act", "dve", "pool"), 5)
            feature_tiles("ev_q", w3("ev_q"), range(0, 512, P), lambda k: zT[:, k, :], TOK, first=normed(5))
            wkv = w3("ev_k")
            feature_tiles("ev_k", wkv, (0,), lambda k: zT[:, k, :], TOK)
            tok = lambda k, j: zT[:, k, j * P:(j + 1) * P]
            token_tiles("ev_v", wkv, tok, 4, P, P)
            token_tiles("ev_bv", w3("ev_bv"), tok, 4, 0, 512)
            feature_tiles("ev_bu", w3("ev_bu"), range(0, 512, P), lambda k: zT[:, k, :], TOK)
            ada(18, 22)
            for j in range(5):
                b = open_tile(TILE["ev_qn"] + j)
                pe.wait_ge(sig("head_sq"), j + 1)
                mm(b[:, :], C("blk64"), E_rt[:, j, :], start=True, stop=True).then_inc(filled, 1)
            for j in range(5):
                b = open_tile(TILE["ev_rope"] + j)
                pe.wait_ge(sig("head_n"), j + 1)
                mm(b[:, 0:S], C("rope_r"), E_qk[:, j, 0:S], start=True, stop=True).then_inc(filled, 1)
            pe.wait_ge(sig("ev_small_in"), 16)
            pe.wait_ge(sig("ev_vv"), 4)
            wsT = E_w[:, 1024:2048].rearrange("p (g i) -> p g i", g=8)
            for jp in range(4):
                b = open_tile(TILE["ev_mix"] + jp)
                for a in range(2):
                    g = 2 * jp + a
                    for t in range(4):
                        last = mm(b[64 * a:64 * a + 64, t * P:(t + 1) * P], E_bv[:, t, g * HD:(g + 1) * HD],
                                  wsT[:, g, :], start=True, stop=True)
                last.then_inc(filled, 1)

            def ev_ready():
                pe.wait_ge(sig("ada_done"), 22)
                pe.wait_ge(sig("ekswap_in"), 32)
                wait_evac(pe, TILE["ev_rope"] + 4)
                wait_evac(pe, TILE["ev_mix"] + 3)
                wait_evac(pe, TILE["ev_v"] + 3)

            attention(*EV_U, E_P, E_PT, ev_ready, lambda i: ADA_EV[i])
            pe.wait_ge(sig("att_out"), EV_U[1])
            pe.wait_ge(sig("mix_y"), 4)
            fence(pe, "pe", ("act", "dve", "pool"), 6)
            for c in range(2):
                feature_tiles(f"ev_out{c}", w3(f"ev_out{c}"), range(0, 512, P), lambda k: E_y[:, k, :], TOK)
            norm(6, TOK)
            ffn(2, TOK, 6)

            norm(7, TOK)
            ffn(3, TOK, 7)
            norm(8, TOK)
            fence(pe, "pe", ("act", "dve", "pool"), 7)
            feature_tiles("od_q", w3("od_q"), range(0, 512, P), hrhs, S, first=normed(8))
            feature_tiles("od_k", w3("od_k"), range(0, 512, P), lambda k: zT[:, k, :], TOK)
            token_tiles("od_v", w3("od_v"), tok, 4, 0, 512)
            feature_tiles("od_xp", w3("od_xp"), range(0, 512, P), hrhs, S)
            for j in range(8):
                b = open_tile(TILE["od_qn"] + j)
                nt = S if j < 4 else TOK
                pe.wait_ge(sig("head_sq"), 5 + j + 1)
                mm(b[:, 0:nt], C("blk64"), O_tmp[:, j % 2, 0:nt], start=True, stop=True).then_inc(filled, 1)
            pe.wait_ge(sig("rpb_stage"), 16 * 16)
            for i in range(8):
                b = open_tile(TILE["od_flip"] + i)
                mm(b[:, :], C("flip"), area(8384 + i * BANK, BANK), start=True, stop=True).then_inc(filled, 1)
            pe.wait_ge(sig("pool_w_in"), 16)
            for g in range(4):
                b = open_tile(TILE["od_pool"] + g)
                pe.wait_ge(sig("pooled"), g + 1)
                mm(b[:, 0:S], O_wp[:, g * P:(g + 1) * P], O_s1[:, g, 0:S], start=True, stop=True)\
                    .then_inc(filled, 1)

            def od_ready():
                pe.wait_ge(sig("head_n"), 13)
                wait_evac(pe, TILE["od_pool"] + 3)
                wait_evac(pe, TILE["od_v"] + 3)

            fence(pe, "pe", ("act", "dve", "pool"), 8)
            attention(*OD_U, O_P, O_PT, od_ready, lambda i: ())
            pe.wait_ge(sig("att_out"), OD_U[1])
            fence(pe, "pe", ("act", "dve", "pool"), 9)
            for c in range(2):
                feature_tiles(f"od_out{c}", w3(f"od_out{c}"), range(0, 512, P), lambda k: O_y[:, k, :], S)
            norm(9, S)
            ffn(4, S, 9)

        @block.scalar
        def _(act):
            A = nc.scalar.activation
            steps = [0]

            def link(ins):
                steps[0] += 1
                ins.then_inc(sig("act_step"), 1)
                act.wait_ge(sig("act_step"), steps[0])

            def empty(n):
                act.wait_ge(filled, n + 1)
                return bank(n)

            def copy_tiles(stage, n, dst, nt=S, func=ACT.Identity, rows=P, scale=1.0, pre=None):
                for j in range(n):
                    b = empty(TILE[stage] + j)
                    if pre is not None:
                        pre(j)
                    A(dst(j), b[0:rows, 0:nt], func, scale=scale).then_inc(evac["A"], 1)

            def w_hi(h):
                if h >= 5 * FFN_HALVES:
                    return
                i = CHUNK_OF[f"ffn{h // FFN_HALVES}_in0_0"] + (h % FFN_HALVES) // 2
                if h % 2 == 0:
                    act.wait_ge(landed[i % NSLOT], 16 * (i // NSLOT + 1))
                if h >= NSPLIT:
                    act.wait_ge(filled, half_first_tile(h - NSPLIT) + 2)
                n = half_width(h)
                at = (i % NSLOT) * SLOT + (h % 2) * n
                A(W_hi[h % NSPLIT][:, 0:n], ring[:, at:at + n], ACT.Identity).then_inc(sig("w_hi"), 1)

            def norm(q, nt, src, ready, prefetch=None):
                for k in range(KT):
                    ready(k)
                    if k == 0 and q > 0:
                        act.wait_ge(sig("norm_recip"), q)
                    A(rr[:, 0:nt] if k == 0 else zT[:, k, 0:nt], src[:, k, 0:nt], ACT.Square)\
                        .then_inc(sig("norm_sq"), 1)
                if prefetch is not None:
                    for h in range(2):
                        w_hi(FFN_HALVES * prefetch + h)
                b = empty(TILE[f"norm{q}"])
                A(rt[:, 0:nt], b[:, 0:nt], ACT.Sqrt, scale=1.0 / D, bias=C("eps")).then_inc(evac["A"], 1)
                for k in range(KT):
                    if q in MODN:
                        j, li = MODN[q][0], 0 if q < 7 else 1
                        act.wait_ge(sig("norm_xr"), norm_xr_before(q) + k + 1)
                        A(zT[:, k, 0:S], zT[:, k, 0:S], ACT.Identity,
                          scale=modA[li][:, 2 * (8 * j + k):2 * (8 * j + k) + 1],
                          bias=mod[li][:, 2 * (24 * j + k):2 * (24 * j + k) + 1]).then_inc(sig("norm_zm"), 1)
                    if q in SPLIT:
                        if q == 2:
                            act.wait_ge(sig("norm_z"), KT + k + 1)
                        else:
                            act.wait_ge(sig("norm_zm"), norm_xr_before(q) + k + 1)
                        if nt == TOK:
                            act.wait_ge(sig("norm_zc"), norm_zc_before(q) + k + 1)
                        A(z_hi(nt)[:, k, :], zT[:, k, 0:nt], ACT.Identity).then_inc(sig("norm_hi"), 1)

            def ffn(f, nt):
                for i, (g, j, second) in enumerate(HALVES):
                    h = FFN_HALVES * f + i
                    if i + 2 < FFN_HALVES:
                        w_hi(h + 2)
                    if not second:
                        n = half_first_tile(h)
                        b = empty(n)
                        m = FT * f + GROUPS[g][0] + j
                        if m - FT * f >= 2:
                            act.wait_ge(sig("a_lo"), m - 1)
                        A((rt, rr)[j % 2][:, 0:nt], b[:, 0:nt], ACT.Silu).then_inc(evac["A"], 1)

            def merge(br, tmp):
                for c in range(4):
                    for j in range(2):
                        n = TILE[f"merge{br}{c}"] + 2 * j
                        b = empty(n)
                        i = 2 * c + j
                        if i >= 2:
                            m = TILE[f"merge{br}{(i - 2) // 2}"] + 2 * (i % 2) + 1
                            wait_evac(act, m)
                        A(tmp[:, i % 2, :], b[:, 0:S], ACT.Sigmoid).then_inc(evac["A"], 1)

            act.wait_ge(sig("vec_in"), 16)
            act.wait_ge(sig("cst_in"), 16)
            act.wait_ge(sig("cs_zero"), 1)
            A(cs[:, :].rearrange("p (k n) -> p k n", k=KT)[:, :, 0:2], V("c").rearrange("p (k s) -> p k s", s=2),
              ACT.Silu).then_inc(sig("cs_ready"), 1)
            link(A(small[:, 0:8], V("lam"), ACT.Abs))
            link(A(small[:, 8:16], small[:, 0:8], ACT.Exp, scale=-1.0))
            A(small[:, 16:24], small[:, 8:16], ACT.Ln, bias=C("one")).then_inc(sig("lru_ln"), 1)
            norm(0, S, xT, lambda k: act.wait_ge(sig("x_in"), 16))
            for c in range(2):
                copy_tiles(f"lru_x{c}", 4, lambda j: A_xp[:, 4 * c + j, 3:S + 3])
            for c in range(2):
                copy_tiles(f"lru_g{c}", 4, lambda j: A_g[:, 4 * c + j, :], func=ACT.Gelu_apprx_tanh)
            wait_evac(act, TILE["lru_x1"] + 3)
            for k in range(KT):
                A(A_xc[:, k, :], A_xp[:, k, 3:S + 3], ACT.Identity, scale=V("conv_w", 24 + k, 1),
                  bias=V("conv_b", k, 1)).then_inc(sig("lru_tap"), 1)
            for k in range(KT):
                for g, dst in enumerate((A_r, A_i)):
                    n = TILE["lru_gates"] + 2 * k + g
                    b = empty(n)
                    A(dst[:, k, :], b[:, 0:S], ACT.Sigmoid, bias=V("b_gates", 8 * g + k, 1)).then_inc(evac["A"], 1)
            act.wait_ge(sig("lru_coef"), 1)
            wait_evac(act, TILE["lru_gates"] + 15)
            for k in range(KT):
                A(A_a[:, k, :], A_r[:, k, :], ACT.Exp, scale=small[:, 32 + k:33 + k]).then_inc(sig("lru_a"), 1)
            for k in range(KT):
                A(A_t[:, k, :], A_r[:, k, :], ACT.Tanh, scale=small[:, 40 + k:41 + k]).then_inc(sig("lru_tanh"), 1)
            copy_tiles("gla_q", 4, lambda j: C_q[:, j, :], scale=float(P) ** -0.5)
            act.wait_ge(sig("lru_v"), 1)
            A(A_t, A_t, ACT.Sqrt, scale=2.0).then_inc(sig("lru_root"), 1)
            copy_tiles("gla_k", 4, lambda j: C_k[:, j, :])
            copy_tiles("gla_lr", 1, lambda j: C_lr[0:16, :], rows=16)
            for h in range(4):
                b = empty(TILE["gla_al"] + h)
                A(C_Y[:, h, :], b[:, 0:S], ACT.Identity, bias=V("gla_ba", h, 1)).then_inc(evac["A"], 1)
            wait_evac(act, TILE["gla_al"] + 3)
            link(A(C_e, C_Y, ACT.Abs))
            link(A(C_e, C_e, ACT.Exp, scale=-1.0))
            A(C_e, C_e, ACT.Ln, bias=C("one")).then_inc(sig("gla_ln"), 1)
            for c in range(2):
                copy_tiles(f"gla_og{c}", 4, lambda j: C_og[:, 4 * c + j, :], func=ACT.Silu)
            act.wait_ge(sig("gla_b"), 1)
            A(C_Y, C_b, ACT.Exp, scale=1.0 / 16).then_inc(sig("gla_eb"), 1)
            A(C_e, C_b, ACT.Exp, scale=-1.0 / 16).then_inc(sig("gla_eb"), 1)
            act.wait_ge(sig("gla_bd"), 1)
            A(C_b, C_b, ACT.Exp, scale=1.0 / 16).then_inc(sig("gla_eb"), 1)
            merge("A", mgA_t)
            fence(act, "act", ("pe", "dve", "pool"), 1)

            for t in range(2):
                b = empty(TILE["gla_t"] + t)
                A(C_kt[:, 4 * t:4 * t + 4, :], b[:, :].rearrange("p (h d) -> p h d", h=4), ACT.Identity)\
                    .then_inc(evac["A"], 1)
            for c in range(2):
                copy_tiles(f"nsa_q{c}", 4, lambda j: B_q[:, 4 * c + j, :], scale=HD ** -0.5)
            copy_tiles("nsa_kvc", 4, lambda j: B_kc[:, j, :])
            copy_tiles("nsa_ksw", 4, lambda j: B_kk[:, j, :])
            copy_tiles("nsa_gate", 2, lambda j: B_gate[:, j, :], nt=48, func=ACT.Sigmoid)
            for j in range(8):
                b = empty(TILE["gla_o"] + j)
                if j == 0:
                    act.wait_ge(sig("gla_state"), 28)
                A(C_o[:, j, :], b[:, 0:S], ACT.Identity).then_inc(evac["A"], 1)
            wait_evac(act, TILE["gla_o"] + 7)
            for j in range(8):
                A(C_st[:, j // 2, (j % 2) * S:(j % 2 + 1) * S], C_o[:, j, :], ACT.Square).then_inc(sig("gla_sq"), 1)
            for h in range(4):
                b = empty(TILE["gla_n"] + h)
                A(C_st[:, h, 2 * S:3 * S], b[:, 0:S], ACT.Sqrt, scale=1.0 / 256, bias=C("eps"))\
                    .then_inc(evac["A"], 1)
            merge("C", mgC_t)
            fence(act, "act", ("pe", "dve", "pool"), 2)

            def att_exp(u, Pb, gate=None):
                kind, g, t = UNITS[u]
                act.wait_ge(sig("att_max"), u + 1)
                act.wait_ge(sig("att_turned"), batches_before(u)) if batches_before(u) else None
                nm, sm = small[:, 0:12], small[:, 16:28]
                if kind == "nsa":
                    nk = P * (t + 1)
                    for i in range(8):
                        A(Pb[:, i * S:i * S + nk], psum[:, i * S:i * S + nk], ACT.Exp,
                          bias=nm[:, i:i + 1], accum_out=sm[:, i:i + 1])
                    for r in range(4):
                        at = r * CMP_N
                        last = A(Pb[:, 2048 + at:2048 + at + CMP_N], psum[:, CMP_AT + at:CMP_AT + at + CMP_N],
                                 ACT.Exp, bias=nm[:, 8 + r:9 + r], accum_out=sm[:, 8 + r:9 + r])
                else:
                    k0 = S if t >= 2 else 0
                    if kind == "ev":
                        A(small[:, 32:36], small[:, 28:32], ACT.Exp)
                    for r in range(4):
                        last = A(Pb[:, r * BANK + k0:(r + 1) * BANK], psum[:, r * BANK + k0:(r + 1) * BANK],
                                 ACT.Exp, bias=nm[:, r:r + 1], accum_out=sm[:, r:r + 1])
                last.then_inc(sig("att_exp"), 1)

            def att_copies(u, PT):
                bs, gb0 = batches(u), batches_before(u)
                for i, (seg, _) in enumerate(bs):
                    gb = gb0 + i
                    act.wait_ge(sig("att_turned"), gb + 1)
                    if gb >= 3:
                        act.wait_ge(sig("att_mult"), gb - 2)
                    n = CMP_N if seg == 2 else P
                    A(PT[0:n, gb % 3, :], psum[0:n, (5 + gb % 2) * BANK:(6 + gb % 2) * BANK], ACT.Identity)\
                        .then_inc(sig("att_copied"), 1)

            def attention(u0, u1, Pb, PT):
                att_exp(u0, Pb)
                for u in range(u0, u1):
                    att_copies(u, PT)
                    if u + 1 < u1:
                        att_exp(u + 1, Pb)

            for i in range(2):
                copy_tiles(f"cmp_hid{i}", 2, lambda j: B_hid[:, i, j, :], nt=60, func=ACT.Gelu_apprx_tanh)
            fence(act, "act", ("pe", "dve", "pool"), 3)
            attention(*NSA_U, B_P, B_PT)
            merge("B", mgB_t)
            for c in range(2):
                copy_tiles(f"w_out{c}", 4, lambda j: Y_y[:, 4 * c + j, :])
            fence(act, "act", ("pe", "dve", "pool"), 4)
            norm(1, S, Y_y, lambda k: wait_evac(act, TILE["w_out1"] + 3))
            norm(2, S, xT, lambda k: act.wait_ge(sig("norm_x"), k + 1), prefetch=0)
            ffn(0, S)
            norm(3, S, Y_y, lambda k: wait_evac(act, TILE["ffn0_out2_0"] + k))

            def ready4(k):
                act.wait_ge(sig("norm_x"), KT + k + 1)
                act.wait_ge(sig("ctx_in"), 16)
                act.wait_ge(sig("mod_ready"), 1)

            norm(4, TOK, xT, ready4, prefetch=1)
            ffn(1, TOK)
            norm(5, TOK, xT, lambda k: wait_evac(act, TILE["ffn1_out2_0"] + k))
            fence(act, "act", ("pe", "dve", "pool"), 5)
            copy_tiles("ev_q", 4, lambda j: E_qk[:, j, :], nt=TOK)
            copy_tiles("ev_k", 1, lambda j: E_qk[:, 4, :], nt=TOK)
            copy_tiles("ev_bv", 4, lambda j: E_bv[:, j, :], nt=TOK, func=ACT.Gelu_apprx_tanh)
            copy_tiles("ev_bu", 4, lambda j: E_u[:, j, :], nt=TOK, func=ACT.Gelu_apprx_tanh)
            wait_evac(act, TILE["ev_bu"] + 3)
            for j in range(5):
                A(E_rt[:, j, :], E_qk[:, j, :], ACT.Square).then_inc(sig("head_sq"), 1)
            for j in range(5):
                b = empty(TILE["ev_qn"] + j)
                A(E_rt[:, j, :], b[:, :], ACT.Sqrt, scale=1.0 / HD, bias=C("eps")).then_inc(evac["A"], 1)
            act.wait_ge(sig("ev_vsum"), 1)
            A(small[:, 96:128], small[:, 64:96], ACT.Sqrt, scale=1.0 / HD, bias=C("eps")).then_inc(sig("ev_vrt"), 1)
            attention(*EV_U, E_P, E_PT)
            fence(act, "act", ("pe", "dve", "pool"), 6)
            norm(6, TOK, xT, lambda k: wait_evac(act, TILE["ev_out0"] + k), prefetch=2)
            ffn(2, TOK)

            norm(7, TOK, xT, lambda k: wait_evac(act, TILE["ffn2_out2_0"] + k), prefetch=3)
            ffn(3, TOK)
            norm(8, TOK, xT, lambda k: wait_evac(act, TILE["ffn3_out2_0"] + k))
            fence(act, "act", ("pe", "dve", "pool"), 7)
            copy_tiles("od_q", 4, lambda j: O_q[:, j, :])
            copy_tiles("od_k", 4, lambda j: O_k[:, j, :], nt=TOK)
            copy_tiles("od_xp", 4, lambda j: O_xp[:, j, 8:S + 8])
            wait_evac(act, TILE["od_xp"] + 3)
            for j in range(8):
                nt = S if j < 4 else TOK
                src = O_q[:, j, :] if j < 4 else O_k[:, j - 4, :]
                if j >= 2:
                    act.wait_ge(sig("head_n"), 5 + j - 1)
                A(O_tmp[:, j % 2, 0:nt], src, ACT.Square).then_inc(sig("head_sq"), 1)
                b = empty(TILE["od_qn"] + j)
                A(O_tmp[:, j % 2, 0:nt], b[:, 0:nt], ACT.Sqrt, scale=1.0 / HD, bias=C("eps")).then_inc(evac["A"], 1)
            wait_evac(act, TILE["od_flip"] + 7)
            for g in range(4):
                b = empty(TILE["od_pool"] + g)
                A(O_y[:, g, :], b[:, 0:S], ACT.Copy, scale=V("c_scale", g, 1)).then_inc(evac["A"], 1)
            fence(act, "act", ("pe", "dve", "pool"), 8)
            attention(*OD_U, O_P, O_PT)
            fence(act, "act", ("pe", "dve", "pool"), 9)
            norm(9, S, xT, lambda k: wait_evac(act, TILE["od_out0"] + k), prefetch=4)
            ffn(4, S)

        @block.vector
        def _(dve):
            v = nc.vector
            steps = [0]

            def link(ins):
                steps[0] += 1
                ins.then_inc(sig("dve_step"), 1)
                dve.wait_ge(sig("dve_step"), steps[0])

            def empty(n):
                dve.wait_ge(filled, n + 1)
                return bank(n)

            def w_lo(h):
                if h >= 5 * FFN_HALVES:
                    return
                i = CHUNK_OF[f"ffn{h // FFN_HALVES}_in0_0"] + (h % FFN_HALVES) // 2
                dve.wait_ge(sig("w_hi"), h + 1)
                n = half_width(h)
                at = (i % NSLOT) * SLOT + (h % 2) * n
                v.tensor_tensor(out=W_lo[h % NSPLIT][:, 0:n], in0=ring[:, at:at + n],
                                in1=W_hi[h % NSPLIT][:, 0:n].bitcast(f32), op=ALU.subtract).then_inc(sig("w_lo"), 1)

            def add_square(q, nt, k):
                dve.wait_ge(sig("norm_sq"), KT * q + k + 1)
                ins = v.tensor_tensor(out=rr[:, 0:nt], in0=rr[:, 0:nt], in1=zT[:, k, 0:nt], op=ALU.add)
                if k == KT - 1:
                    ins.then_inc(sig("norm_sum"), 1)
                else:
                    link(ins)

            def norm(q, nt, src, gain=None, summed=1, prefetch=None):
                for k in range(summed, KT):
                    add_square(q, nt, k)
                if prefetch is not None:
                    for h in range(2):
                        w_lo(FFN_HALVES * prefetch + h)
                wait_evac(dve, TILE[f"norm{q}"])
                v.reciprocal(rr[:, 0:nt], rt[:, 0:nt]).then_inc(sig("norm_rr"), 1)
                dve.wait_ge(sig("norm_rr"), q + 1)
                for k in range(KT + 2):
                    if k < KT:
                        if q in MODN:
                            v.tensor_tensor(out=zT[:, k, 0:nt], in0=src[:, k, 0:nt], in1=rr[:, 0:nt], op=ALU.mult)\
                                .then_inc(sig("norm_xr"), 1)
                        elif q in (0, 2):
                            v.scalar_tensor_tensor(out=zT[:, k, 0:nt], in0=src[:, k, 0:nt], scalar=gain(k),
                                                   in1=rr[:, 0:nt], op0=ALU.mult, op1=ALU.mult)\
                                .then_inc(sig("norm_z"), 1)
                        else:
                            link(v.scalar_tensor_tensor(out=src[:, k, 0:nt], in0=src[:, k, 0:nt], scalar=gain(k),
                                                        in1=rr[:, 0:nt], op0=ALU.mult, op1=ALU.mult))
                            v.tensor_tensor(out=xT[:, k, 0:nt], in0=src[:, k, 0:nt], in1=xT[:, k, 0:nt], op=ALU.add)\
                                .then_inc(sig("norm_x"), 1)
                    if q in SPLIT and k >= 2:
                        j = k - 2
                        dve.wait_ge(sig("norm_hi"), norm_hi_before(q) + j + 1)
                        v.tensor_tensor(out=z_lo[:, j, 0:nt],
                                        in0=zT[:, j, 0:nt], in1=z_hi(nt)[:, j, :].bitcast(f32), op=ALU.subtract)\
                            .then_inc(sig("norm_lo"), 1)
                dve.engine_nop().then_inc(sig("norm_recip"), 1)

            def ada(a, b_, lag=1):
                def done(c):
                    dve.wait_ge(sig("ada_cols"), c + 1)
                    li, j, at = c // 18, c % 18, ada_banks(c)[1] * BANK
                    v.tensor_tensor(out=mod[li][:, 8 * j:8 * j + 8].rearrange("p (j s) -> p j s", s=2),
                                    in0=psum[:, at:at + 8].rearrange("p (j s) -> p j s", s=2),
                                    in1=rep(V("ada_b", 4 * c, 4), 2), op=ALU.add).then_inc(sig("ada_done"), 1)

                for c in range(a, b_):
                    dve.wait_ge(sig("ada_rows"), c + 1)
                    if c >= 2:
                        dve.wait_ge(sig("ada_cols"), c - 1)
                    at = ada_banks(c)[0] * BANK
                    v.tensor_copy(ab[:, (c % 2) * BANK:(c % 2 + 1) * BANK], psum[:, at:at + BANK])\
                        .then_inc(sig("ada_copied"), 1)
                    if lag == 0:
                        done(c)
                    elif c > a:
                        done(c - 1)
                if lag:
                    done(b_ - 1)

            def mods(li):
                dve.wait_ge(sig("ada_done"), 18 * (li + 1))
                for j in range(3):
                    g = rep(V("norm_g2", 24 * li + 8 * j, 8), 2)
                    last = v.scalar_tensor_tensor(
                        out=modA[li][:, 16 * j:16 * j + 16].rearrange("p (k s) -> p k s", s=2),
                        in0=mod[li][:, 16 * (3 * j + 1):16 * (3 * j + 2)].rearrange("p (k s) -> p k s", s=2),
                        scalar=1.0, in1=g, op0=ALU.add, op1=ALU.mult)
                for j in range(2):
                    last = v.tensor_scalar(out=gates_h[li][:, 16 * j:16 * j + 16],
                                           in0=mod[li][:, 16 * (6 * j + 2):16 * (6 * j + 3)],
                                           scalar1=0.5, scalar2=None, op0=ALU.mult)
                last.then_inc(sig("mod_ready"), 1)
                dve.wait_ge(sig("mod_ready"), li + 1)

            def residual(n, k, nt, gate):
                b = empty(n)
                for s in range(nt // S):
                    last = v.scalar_tensor_tensor(out=xT[:, k, s * S:(s + 1) * S], in0=b[:, s * S:(s + 1) * S],
                                                  scalar=gate(k, s), in1=xT[:, k, s * S:(s + 1) * S],
                                                  op0=ALU.mult, op1=ALU.add)
                last.then_inc(evac["V"], 1)

            def ffn(f, nt, li=None, which=None, q=None):
                for i, (g, j, second) in enumerate(HALVES):
                    h = FFN_HALVES * f + i
                    if i + 2 < FFN_HALVES:
                        w_lo(h + 2)
                    n = half_first_tile(h)
                    if not second:
                        b = empty(n + 1)
                        wait_evac(dve, n)
                        a = (rt, rr)[j % 2][:, 0:nt]
                        v.tensor_tensor(out=a, in0=b[:, 0:nt], in1=a, op=ALU.mult).then_inc(evac["V"], 1)
                        continue
                    for c in range(2):
                        k = 2 * j + c
                        if which is not None:
                            residual(n + c, k, nt, lambda k, s: gates_h[li][:, 16 * which + 2 * k + s:
                                                                            16 * which + 2 * k + s + 1])
                        elif g == 0:
                            b = empty(n + c)
                            v.tensor_copy(Y_y[:, k, :], b[:, 0:S]).then_inc(evac["V"], 1)
                        else:
                            b = empty(n + c)
                            v.tensor_tensor(out=Y_y[:, k, :], in0=b[:, 0:S], in1=Y_y[:, k, :], op=ALU.add)\
                                .then_inc(evac["V"], 1)
                        if g == 2 and q is not None and k >= 2:
                            add_square(q, nt, k - 1)

            def merge(br, tmp):
                for c in range(4):
                    for j in range(2):
                        i = 2 * c + j
                        n = TILE[f"merge{br}{c}"] + 2 * j + 1
                        b = empty(n)
                        wait_evac(dve, n - 1)
                        m = zT[:, i, S:TOK]
                        if br == "A":
                            v.tensor_tensor(out=m, in0=b[:, 0:S], in1=tmp[:, i % 2, :], op=ALU.mult)\
                                .then_inc(evac["V"], 1)
                        else:
                            link(v.tensor_tensor(out=tmp[:, i % 2, :], in0=b[:, 0:S], in1=tmp[:, i % 2, :],
                                                 op=ALU.mult))
                            v.tensor_tensor(out=m, in0=m, in1=tmp[:, i % 2, :], op=ALU.add).then_inc(evac["V"], 1)

            dve.wait_ge(sig("vec_in"), 16)
            dve.wait_ge(sig("cst_in"), 16)
            link(v.memset(A_xp[:, :, 0:3], 0.0))
            ada(0, 2)
            dve.wait_ge(sig("x_in"), 16)
            norm(0, S, xT, lambda k: V("norm_g", k, 1))
            b = empty(TILE["strip"])
            v.tensor_copy(K_strip[0:16, :], b[0:16, 0:384]).then_inc(evac["V"], 1)
            b = empty(TILE["cbias"])
            v.tensor_copy(K_C.rearrange("p (t h c) -> p t c h", t=2, h=16),
                          b[:, 0:480].rearrange("p (t c h) -> p t c h", t=2, c=CMP_N)).then_inc(evac["V"], 1)
            for k in range(KT):
                dve.wait_ge(sig("lru_tap"), k + 1)
                for i in range(3):
                    ins = v.scalar_tensor_tensor(out=A_xc[:, k, :], in0=A_xp[:, k, i:i + S],
                                                 scalar=V("conv_w", 8 * i + k, 1), in1=A_xc[:, k, :],
                                                 op0=ALU.mult, op1=ALU.add)
                    if i < 2:
                        link(ins)
                    else:
                        ins.then_inc(sig("lru_xc"), 1)
            link(v.tensor_scalar(out=small[:, 48:56], in0=V("lam"), scalar1=-1.0, scalar2=0.0,
                                 op0=ALU.mult, op1=ALU.max))
            dve.wait_ge(sig("lru_ln"), 1)
            link(v.tensor_tensor(out=small[:, 48:56], in0=small[:, 48:56], in1=small[:, 16:24], op=ALU.add))
            v.tensor_scalar(out=small[:, 32:40], in0=small[:, 48:56], scalar1=-8.0, scalar2=None, op0=ALU.mult)
            v.tensor_scalar(out=small[:, 40:48], in0=small[:, 48:56], scalar1=8.0, scalar2=None, op0=ALU.mult)\
                .then_inc(sig("lru_coef"), 1)
            wait_evac(dve, TILE["lru_gates"] + 15)
            dve.wait_ge(sig("lru_xc"), KT)
            link(v.tensor_tensor(out=A_i, in0=A_i, in1=A_xc, op=ALU.mult))
            dve.wait_ge(sig("lru_tanh"), KT)
            link(v.tensor_scalar(out=A_r, in0=A_t, scalar1=1.0, scalar2=None, op0=ALU.add))
            link(v.reciprocal(A_r, A_r))
            v.tensor_tensor(out=A_t, in0=A_t, in1=A_r, op=ALU.mult).then_inc(sig("lru_v"), 1)
            dve.wait_ge(sig("lru_root"), 1)
            dve.wait_ge(sig("lru_a"), KT)
            link(v.tensor_tensor(out=A_i, in0=A_i, in1=A_t, op=ALU.mult))
            for k in range(KT):
                last = v.tensor_tensor_scan(out=A_r[:, k, :], data0=A_a[:, k, :], data1=A_i[:, k, :], initial=0.0,
                                            op0=ALU.mult, op1=ALU.add)
            link(last)
            for k in range(KT):
                v.tensor_tensor(out=A_y[:, k, :], in0=A_r[:, k, :], in1=A_g[:, k, :], op=ALU.mult)\
                    .then_inc(sig("lru_y"), 1)
            dve.wait_ge(sig("gla_ln"), 1)
            link(v.tensor_scalar(out=C_Y, in0=C_Y, scalar1=0.0, scalar2=None, op0=ALU.min))
            link(v.tensor_tensor(out=C_Y, in0=C_Y, in1=C_e, op=ALU.subtract))
            for h in range(4):
                last = v.tensor_tensor_scan(out=C_b[:, h, :], data0=C("scan_mask"), data1=C_Y[:, h, :], initial=0.0,
                                            op0=ALU.mult, op1=ALU.add)
            last.then_inc(sig("gla_b"), 1)
            dve.wait_ge(sig("gla_b"), 1)
            for c in range(2):
                for t in range(2):
                    b = empty(TILE[f"gla_v{c}"] + t)
                    v.tensor_copy(C_v[:, t, c * 512:(c + 1) * 512], b[:, :]).then_inc(evac["V"], 1)
            dve.wait_ge(sig("gla_eb"), 2)
            blast = small[:, 128:160]
            link(v.tensor_copy(blast, arena[:, 18456 + 31:18456 + 1024:32]))
            v.tensor_tensor(out=arena[:, 18456:19480].rearrange("p (c i) -> p c i", i=32), in0=rep(blast, 32),
                            in1=arena[:, 18456:19480].rearrange("p (c i) -> p c i", i=32), op=ALU.subtract)\
                .then_inc(sig("gla_bd"), 1)
            v.tensor_copy(small[:, 96:128], arena[:, 16408 + 31:16408 + 1024:32])
            wait_evac(dve, TILE["gla_k"] + 3)
            v.tensor_tensor(out=C_q, in0=C_q, in1=C_Y, op=ALU.mult)
            dve.wait_ge(sig("gla_eb"), 3)
            link(v.tensor_tensor(out=C_b, in0=C_b, in1=C_k, op=ALU.mult))
            link(v.tensor_tensor(out=C_k, in0=C_k, in1=C_e, op=ALU.mult))
            v.tensor_copy(C_e, C_b).then_inc(sig("gla_kend"), 1)
            merge("A", mgA_t)
            ada(2, 6)
            fence(dve, "dve", ("pe", "act", "pool"), 1)

            link(v.memset(C_at, 0.0))
            mask = C("gla_mask").bitcast(mybir.dt.uint32)
            for t in range(2):
                b = empty(TILE["gla_att"] + t)
                for h in range(4):
                    last = v.copy_predicated(C_at[:, 4 * t + h, :], mask, b[:, h * P:(h + 1) * P])
                last.then_inc(evac["V"], 1)
            for c in range(7):
                for h in range(4):
                    dve.wait_ge(sig("gla_upd"), 4 * c + h + 1)
                    upd = psum[:, (4 + h) * BANK:(4 + h) * BANK + S]
                    dst = C_st[:, h, c * S:(c + 1) * S]
                    if c == 0:
                        v.tensor_copy(dst, upd).then_inc(sig("gla_state"), 1)
                    else:
                        dve.wait_ge(sig("gla_state"), 4 * (c - 1) + h + 1)
                        v.scalar_tensor_tensor(out=dst, in0=C_st[:, h, (c - 1) * S:c * S],
                                               scalar=small[:, 96 + 8 * h + c:96 + 8 * h + c + 1], in1=upd,
                                               op0=ALU.mult, op1=ALU.add).then_inc(sig("gla_state"), 1)
                if c == 5:
                    for t in range(2):
                        b = empty(TILE["nsa_vsw"] + t)
                        v.tensor_copy(B_v[:, t, :], b[:, :]).then_inc(evac["V"], 1)
            for h in range(4):
                wait_evac(dve, TILE["gla_n"] + h)
                r = C_st[:, h, 2 * S:3 * S]
                link(v.reciprocal(r, r))
                for e in range(2):
                    o = C_o[:, 2 * h + e, :]
                    link(v.scalar_tensor_tensor(out=o, in0=o, scalar=V("gla_norm", e, 1), in1=r,
                                                op0=ALU.mult, op1=ALU.mult))
                    v.tensor_tensor(out=C_og[:, 2 * h + e, :], in0=C_og[:, 2 * h + e, :], in1=o, op=ALU.mult)\
                        .then_inc(sig("gla_y"), 1)
            ada(6, 10)
            merge("C", mgC_t)
            fence(dve, "dve", ("pe", "act", "pool"), 2)

            def att_max(u):
                kind, g, t = UNITS[u]
                nm = small[:, 0:12]
                dve.wait_ge(sig("att_score"), u + 1)
                if kind == "nsa":
                    nk = P * (t + 1)
                    j0 = P if t == 0 else 0
                    for a in range(2):
                        s_ = psum[:, 4 * a * S:4 * (a + 1) * S].rearrange("p (s j k) -> p s j k", s=2, j=2)
                        s_ = s_[:, :, :, 0:nk]
                        bias = B_T[:, 4 * g + 2 * a:4 * g + 2 * a + 2, j0:j0 + nk].unsqueeze(1)\
                            .to_broadcast([P, 2, 2, nk])
                        v.tensor_tensor(out=s_, in0=s_, in1=bias, op=ALU.add)
                    sc = psum[:, CMP_AT:CMP_AT + 4 * CMP_N].rearrange("p (r c) -> p r c", r=4)
                    link(v.tensor_tensor(out=sc, in0=sc, in1=B_C[:, t, 4 * g:4 * g + 4, :], op=ALU.add))
                    v.reduce_max(nm[:, 0:8], psum[:, 0:8 * S].rearrange("p (r k) -> p r k", r=8)[:, :, 0:nk],
                                 AX, negate=True)
                    v.reduce_max(nm[:, 8:12], sc, AX, negate=True).then_inc(sig("att_max"), 1)
                    return
                k0 = S if t >= 2 else 0
                s_ = psum[:, 0:4 * BANK].rearrange("p (r k) -> p r k", r=4)
                if k0 == 0:
                    if kind == "ev":
                        wm = C("win_mask").rearrange("p (t k) -> p t k", t=2)[:, t, :]
                        m = b3(wm, 4, S)
                    else:
                        m = O_nb[:, 8 * t + 4 * g:8 * t + 4 * g + 4, :]
                    link(v.tensor_tensor(out=s_[:, :, 0:S], in0=s_[:, :, 0:S], in1=m, op=ALU.add))
                ins = v.reduce_max(nm[:, 0:4], s_[:, :, k0:BANK], AX, negate=True)
                if kind == "ev":
                    link(ins)
                    sink = V("sink", 4 * g, 4)
                    link(v.scalar_tensor_tensor(out=nm[:, 0:4], in0=sink, scalar=-1.0, in1=nm[:, 0:4],
                                                op0=ALU.mult, op1=ALU.min))
                    ins = v.tensor_tensor(out=small[:, 28:32], in0=sink, in1=nm[:, 0:4], op=ALU.add)
                ins.then_inc(sig("att_max"), 1)

            def att_norm(u, Pb):
                kind, g, t = UNITS[u]
                sm = small[:, 16:28]
                dve.wait_ge(sig("att_exp"), u + 1)
                if kind == "nsa":
                    nk = P * (t + 1)
                    link(v.reciprocal(sm, sm))
                    for seg, br in enumerate((1, 2, 0)):
                        gate = B_gate[:, t, 16 * br + 4 * g:16 * br + 4 * g + 4]
                        if seg == 2:
                            ins = v.tensor_tensor(out=small[:, 44:48], in0=sm[:, 8:12], in1=gate, op=ALU.mult)
                        else:
                            out = small[:, 36:44].rearrange("p (a s j) -> p a s j", a=2, s=2)[:, :, seg, :]
                            si = sm[:, 0:8].rearrange("p (a s j) -> p a s j", a=2, s=2)[:, :, seg, :]
                            v.tensor_tensor(out=out, in0=si, in1=gate.rearrange("p (a j) -> p a j", a=2), op=ALU.mult)
                    link(ins)
                    p_ = Pb[:, 0:2048].rearrange("p (r k) -> p r k", r=8)[:, :, 0:nk]
                    v.tensor_tensor(out=p_, in0=p_, in1=rep(small[:, 36:44], nk), op=ALU.mult)
                    pc = Pb[:, 2048:2108].rearrange("p (r c) -> p r c", r=4)
                    link(v.tensor_tensor(out=pc, in0=pc, in1=rep(small[:, 44:48], CMP_N), op=ALU.mult))
                    va = C("valid_c").rearrange("p (t c) -> p t c", t=2)[:, t, :]
                    v.tensor_tensor(out=pc, in0=pc, in1=b3(va, 4, CMP_N), op=ALU.mult).then_inc(sig("att_p"), 1)
                    return
                k0 = S if t >= 2 else 0
                if kind == "ev":
                    link(v.tensor_tensor(out=sm[:, 0:4], in0=sm[:, 0:4], in1=small[:, 32:36], op=ALU.add))
                link(v.reciprocal(small[:, 36:40], sm[:, 0:4]))
                p_ = Pb[:, 0:2048].rearrange("p (r k) -> p r k", r=4)[:, :, k0:BANK]
                v.tensor_tensor(out=p_, in0=p_, in1=rep(small[:, 36:40], BANK - k0), op=ALU.mult)\
                    .then_inc(sig("att_p"), 1)

            def att_done(u, y):
                kind, g, t = UNITS[u]
                dve.wait_ge(sig("att_mult"), batches_before(u + 1))
                if kind == "od":
                    k = 4 + 2 * g
                else:
                    k = 2 * g
                v.tensor_copy(y[:, k:k + 2, t * P:(t + 1) * P],
                              psum[:, 7 * BANK:7 * BANK + 2 * P].rearrange("p (j t) -> p j t", j=2))\
                    .then_inc(sig("att_out"), 1)

            def attention(u0, u1, Pb, y, extra):
                att_max(u0)
                for u in range(u0, u1):
                    for c in extra(u - u0):
                        ada(c, c + 1, lag=0)
                    att_norm(u, Pb)
                    if u + 1 < u1:
                        att_max(u + 1)
                    att_done(u, y)

            for i in range(8):
                b = empty(TILE["flip"] + i)
                v.tensor_copy(area(14360 + i * BANK, BANK), b[:, :]).then_inc(evac["V"], 1)
            for i in range(2):
                pos = V("pos_k" if i == 0 else "pos_v")
                dve.wait_ge(sig("stack_in"), 16 * 16)
                for g in range(4):
                    st = (4 * i + g) * S
                    for half in range(2):
                        at = st + 16 * half
                        src = arena[:, at:at + 240].rearrange("p (c m two) -> p m c two", m=8, two=2)[:, :, :, 0]
                        last = v.tensor_tensor(out=B_bl[:, i, 8 * half:8 * half + 8, g * CMP_N:(g + 1) * CMP_N],
                                               in0=src, in1=rep(pos[:, 8 * half:8 * half + 8], CMP_N), op=ALU.add)
                    last.then_inc(sig("cmp_blocks"), 1)
            b = empty(TILE["cmp_kv"])
            v.tensor_copy(B_kcT, b[:, 0:60]).then_inc(evac["V"], 1)
            b = empty(TILE["cmp_kv"] + 1)
            v.tensor_copy(B_vc[0:CMP_N, :, :], b[0:CMP_N, 0:256].rearrange("p (g d) -> p g d", g=4))\
                .then_inc(evac["V"], 1)
            ada(10, 14)
            fence(dve, "dve", ("pe", "act", "pool"), 3)
            attention(*NSA_U, B_P, B_y, lambda i: ())
            merge("B", mgB_t)
            ada(14, 18)
            mods(0)
            fence(dve, "dve", ("pe", "act", "pool"), 4)
            norm(1, S, Y_y, lambda k: V("norm_g", 8 + k, 1))
            norm(2, S, xT, lambda k: V("norm_g", 16 + k, 1), prefetch=0)
            ffn(0, S, q=3)
            norm(3, S, Y_y, lambda k: V("norm_g", 24 + k, 1), summed=KT - 1)

            norm(4, TOK, xT, prefetch=1)
            ffn(1, TOK, 0, 0, q=5)
            norm(5, TOK, xT, summed=KT - 1)
            fence(dve, "dve", ("pe", "act", "pool"), 5)
            for t in range(4):
                b = empty(TILE["ev_v"] + t)
                v.tensor_copy(E_v[:, t, :], b[:, 0:P]).then_inc(evac["V"], 1)
            wait_evac(dve, TILE["ev_bv"] + 3)
            link(v.tensor_tensor(out=E_sq, in0=E_bv, in1=E_bv, op=ALU.mult))
            v.tensor_reduce(out=small[:, 64:96], in_=E_sq.rearrange("p t (g d) -> p (t g) d", d=HD), axis=AX,
                            op=ALU.add).then_inc(sig("ev_vsum"), 1)

            def head_norm(stage, j, x, rtile, gain, scale, last_sig=True):
                wait_evac(dve, TILE[stage] + j)
                link(v.reciprocal(rtile, rtile))
                if scale != 1.0:
                    link(v.tensor_scalar(out=x, in0=x, scalar1=scale, scalar2=None, op0=ALU.mult))
                v.scalar_tensor_tensor(out=x, in0=x, scalar=gain, in1=rtile, op0=ALU.mult, op1=ALU.mult)\
                    .then_inc(sig("head_n"), 1)

            ada(18, 22)
            for j in range(5):
                head_norm("ev_qn", j, E_qk[:, j, :], E_rt[:, j, :], V("qg_ev") if j < 4 else V("kg_ev"),
                          HD ** -0.5 if j < 4 else 1.0)
            for j in range(5):
                b = empty(TILE["ev_rope"] + j)
                link(v.tensor_tensor(out=E_rt[:, j, 0:S], in0=b[:, 0:S], in1=C("rope_s"), op=ALU.mult))
                link(v.tensor_tensor(out=E_qk[:, j, 0:S], in0=E_qk[:, j, 0:S], in1=C("rope_c"), op=ALU.mult))
                v.tensor_tensor(out=E_qk[:, j, 0:S], in0=E_qk[:, j, 0:S], in1=E_rt[:, j, 0:S], op=ALU.add)\
                    .then_inc(evac["V"], 1)
            dve.wait_ge(sig("ev_vrt"), 1)
            link(v.reciprocal(small[:, 96:128], small[:, 96:128]))
            bv = E_bv.rearrange("p t (g d) -> p (t g) d", d=HD)
            link(v.tensor_tensor(out=bv, in0=bv, in1=rep(small[:, 96:128], HD), op=ALU.mult))
            dve.wait_ge(sig("ev_small_in"), 16)
            for t in range(4):
                v.tensor_tensor(out=E_bv[:, t, :], in0=E_bv[:, t, :], in1=E_w[:, 0:512], op=ALU.mult)\
                    .then_inc(sig("ev_vv"), 1)
            for jp in range(4):
                b = empty(TILE["ev_mix"] + jp)
                mixed = E_y[:, 4 + jp, :]
                wait_evac(dve, TILE["ev_bu"] + 3)
                v.tensor_tensor(out=mixed.rearrange("p (t i) -> p t i", t=4),
                                in0=b[:, :].rearrange("p (t i) -> p t i", t=4),
                                in1=b3(E_w[:, 512 + jp * P:512 + (jp + 1) * P], 4, P), op=ALU.add)\
                    .then_inc(evac["V"], 1)
                wait_evac(dve, TILE["ev_mix"] + jp)
                v.tensor_tensor(out=mixed, in0=mixed, in1=E_u[:, jp, :], op=ALU.mult).then_inc(sig("mix_y"), 1)
            attention(*EV_U, E_P, E_y, lambda i: ADA_EV[i])
            mods(1)
            fence(dve, "dve", ("pe", "act", "pool"), 6)

            def mixer_residual(stage, li, nt, q):
                for k in range(KT):
                    residual(TILE[stage] + k, k, nt, lambda k, s: mod[li][:, 80 + 2 * k + s:80 + 2 * k + s + 1])
                    if k >= 2:
                        add_square(q, nt, k - 1)

            mixer_residual("ev_out0", 0, TOK, 6)
            norm(6, TOK, xT, summed=KT - 1, prefetch=2)
            ffn(2, TOK, 0, 1, q=7)

            norm(7, TOK, xT, summed=KT - 1, prefetch=3)
            ffn(3, TOK, 1, 0, q=8)
            norm(8, TOK, xT, summed=KT - 1)
            fence(dve, "dve", ("pe", "act", "pool"), 7)
            v.memset(O_xp[:, :, 0:8], 0.0)
            link(v.memset(O_xp[:, :, S + 8:S + 16], 0.0))
            for t in range(4):
                b = empty(TILE["od_v"] + t)
                v.tensor_copy(O_v[:, t, :], b[:, :]).then_inc(evac["V"], 1)
            for j in range(8):
                x = O_q[:, j, :] if j < 4 else O_k[:, j - 4, :]
                head_norm("od_qn", j, x, O_tmp[:, j % 2, 0:S if j < 4 else TOK],
                          V("qg_od") if j < 4 else V("kg_od"), HD ** -0.5 if j < 4 else 1.0)
            for i in range(8):
                b = empty(TILE["od_flip"] + i)
                t = i // 4
                if i == 0:
                    dve.wait_ge(sig("cst_od_in"), 16)
                na = O_na[:, t, :]
                v.tensor_tensor(out=O_nb[:, 2 * i:2 * i + 2, :], in0=b[:, :].rearrange("p (h k) -> p h k", h=2),
                                in1=b3(na, 2, S), op=ALU.add).then_inc(evac["V"], 1)
            for g, w in enumerate((2, 4, 8, 16)):
                wait_evac(dve, TILE["od_xp"] + g)
                src, dst, n, step = O_xp[:, g, :], O_s1[:, g, :], S + 16, 1
                other = O_s2[:, g, :]
                while step < w:
                    n -= step
                    link(v.tensor_tensor(out=dst[:, 0:n], in0=src[:, 0:n], in1=src[:, step:step + n], op=ALU.add))
                    src, dst, other = dst, other, dst
                    step *= 2
                at = 8 - w // 2
                link(v.tensor_tensor(out=dst[:, 0:S], in0=src[:, at:at + S], in1=O_ic[:, g, :], op=ALU.mult))
                link(v.tensor_tensor(out=src[:, 0:S], in0=dst[:, 0:S], in1=O_xp[:, g, 8:S + 8], op=ALU.subtract))
                v.tensor_copy(O_s1[:, g, 0:S], src[:, 0:S]).then_inc(sig("pooled"), 1)
            fence(dve, "dve", ("pe", "act", "pool"), 8)
            attention(*OD_U, O_P, O_y, lambda i: ())
            fence(dve, "dve", ("pe", "act", "pool"), 9)
            mixer_residual("od_out0", 1, S, 9)
            norm(9, S, xT, summed=KT - 1, prefetch=4)
            ffn(4, S, 1, 1)


def col(a):
    return np.ascontiguousarray(a.reshape(-1, P).T)


def pack(w):
    k, n = w.shape
    return w.reshape(k // P, P, n).transpose(1, 0, 2).reshape(P, -1)


def kernel(**inputs):
    import concourse.bacc as _bacc
    from concourse.bass_utils import run_bass_kernel_spmd as _run

    x = {k: np.asarray(v) for k, v in inputs.items()}
    w_in = x["w_in"][0]
    cat = np.concatenate

    def cols(a, b):
        return w_in[:, a:b]

    o_q, o_kv, o_gate, o_gq = 2048, 3072, 4608, 4656
    o_gv, o_og, o_lr, o_merge = 5680, 6704, 7728, 7744
    kv = [cols(o_kv + 256 * i, o_kv + 256 * (i + 1)) for i in range(6)]
    ch = [cols(0, 512), cols(512, 1024), cols(1024, 1536), cols(1536, 2048)]

    def merges(i):
        return [cat([cols(o_merge + D * i + 256 * c, o_merge + D * i + 256 * (c + 1)),
                     x["w_branch"][0, i][:, 256 * c:256 * (c + 1)]], axis=1) for c in range(4)]

    ch += merges(0)
    ch += [cols(o_gq, o_gq + 512), cols(o_gq + 512, o_gq + 1024), cols(o_gv, o_gv + 512),
           cols(o_gv + 512, o_gv + 1024), cols(o_og, o_og + 512), cols(o_og + 512, o_og + 1024)]
    ch += merges(2)
    ch += [cols(o_q, o_q + 512), cols(o_q + 512, o_q + 1024), cat([kv[0], kv[1]], 1), cat([kv[2], kv[4]], 1),
           cat([kv[3], kv[5]], 1)]
    chunks = [pack(w) for w in ch]
    chunks += [pack(x["cmp_w1"][0, i]) for i in range(2)]
    chunks += [pack(w) for w in merges(1)]
    chunks += [pack(x["w_out"][0][:, 512 * c:512 * (c + 1)]) for c in range(2)]
    ffs = [(x["w_ffn_in"][0], x["w_ffn_out"][0])] + [(x["ffn_w_gu_2"][l, i], x["ffn_w_down_2"][l, i])
                                                     for l in range(2) for i in range(2)]
    wf = np.zeros((5 * FFN_CHUNKS, P, W8), np.float32)
    c = 0
    for gu, dn in ffs:
        for k0, nf in GROUPS:
            for i in range(nf):
                a = (k0 + i) * P
                wf[c + i // 2, :, (i % 2) * HALF:(i % 2 + 1) * HALF] = pack(cat([gu[:, a:a + P],
                                                                             gu[:, FF + a:FF + a + P]], 1))
            c += nf // 2
            for i in range(4):
                w = nf * 256
                wf[c + i // 2, :, (i % 2) * w:(i % 2 + 1) * w] = pack(dn[k0 * P:(k0 + nf) * P, 256 * i:256 * (i + 1)])
            c += 2
    for l in range(2):
        chunks += [pack(x["ada_w_2"][l][:, 512 * c:512 * (c + 1)]) for c in range(18)]
    ev = x["ev_w_in_2"][0]
    chunks += [pack(ev[:, 0:512]), pack(ev[:, 1280:1792]), pack(ev[:, 768:1280])]
    chunks += [pack(x["ev_w_out_2"][0][:, 512 * c:512 * (c + 1)]) for c in range(2)]
    od = x["od_w_in_2"][0]
    chunks += [pack(od[:, 512 * c:512 * (c + 1)]) for c in (1, 2, 3, 0)]
    chunks += [pack(x["od_w_out_2"][0][:, 512 * c:512 * (c + 1)]) for c in range(2)]
    assert len(chunks) == W8_N, (len(chunks), W8_N)
    d = {"w8": np.stack(chunks)}
    d["wf"] = wf
    d["w4"] = np.stack([x["lru_w_gates"][0].transpose(2, 0, 1, 3).reshape(P, 2048), pack(ev[:, 512:768])])
    vec = np.zeros((P, VN), np.float32)

    def put(name, a):
        at, n = VOFF[name]
        a = np.asarray(a)
        vec[:a.shape[0], at:at + n] = a.reshape(a.shape[0], n)

    put("norm_g", col(x["norm_g"][0]))
    put("conv_w", col(x["conv_w"][0]))
    put("conv_b", col(x["conv_b"][0]))
    put("b_gates", col(x["lru_b_gates"][0]))
    put("lam", col(x["lru_lambda"][0]))
    put("gla_ba", col(x["gla_ba"][0]))
    put("gla_norm", col(x["gla_norm"][0]))
    put("c", np.stack([col(x["c_2"][0]), col(x["c_ctx_2"])], axis=2))
    put("ada_b", col(x["ada_b_2"]))
    put("norm_g2", col(x["norm_g_2"]))
    for name, src in (("qg_ev", "a_q_gain_2"), ("kg_ev", "a_k_gain_2"), ("qg_od", "d_q_gain_2"),
                      ("kg_od", "d_k_gain_2")):
        put(name, np.tile(x[src][0], 2)[:, None])
    put("c_scale", col(x["c_scale_2"][0]))
    put("sink", np.broadcast_to(x["a_sink_2"][0][None, :], (P, 8)))
    put("pos_k", col(x["cmp_pos"][0, 0]))
    put("pos_v", col(x["cmp_pos"][0, 1]))
    put("w2k", pack(np.tile(x["cmp_w2"][0, 0], (1, 2))))
    put("w2v", pack(x["cmp_w2"][0, 1]))
    order = np.arange(16).reshape(4, 2, 2).transpose(0, 2, 1).ravel()
    gate = cols(o_gate, o_gate + 48).reshape(D, 3, 16)[:, :, order].reshape(D, 48)
    put("w_small", pack(cat([gate, cols(o_lr, o_lr + 16)], 1)))
    put("wa2", x["gla_wa2"][0])
    d["vec"] = vec
    d["cst"], d["cst_od"] = constants()
    d["tbl"] = x["rel_table"][:, order]
    d["rpb"] = x["d_rpb_2"][0].reshape(120, 31)
    d["ev_small"] = cat([np.broadcast_to(x["b_v_gain_2"], (P, 512)),
                         np.repeat(x["b_bias_2"][0].reshape(4, 2, 128), 64, axis=1).transpose(1, 0, 2).reshape(P, 512),
                         x["b_ws_2"][0].transpose(2, 0, 1).reshape(P, 1024)], axis=1)
    d["pool_w"] = x["c_w_pool_2"][0].transpose(1, 0, 2).reshape(P, 512)
    d["x"] = x["x"][0].T.reshape(KT, P, S)
    d["ctx"] = x["ctx_2"][0].T.reshape(KT, P, CL)
    d = {k: np.ascontiguousarray(v) for k, v in d.items()}

    nc = _bacc.Bacc("TRN2", target_bir_lowering=False, num_devices=1)
    f32 = mybir.dt.float32
    aps = {k: nc.dram_tensor(f"in_{k}", v.shape, f32, kind="ExternalInput").ap() for k, v in d.items()}
    out = nc.dram_tensor("out_x", (KT, P, S), f32, kind="ExternalOutput").ap()
    build(nc, aps, out)
    r = _run(nc, [{f"in_{k}": v for k, v in d.items()}], core_ids=[0])
    y = np.asarray(r.results[0]["out_x"])
    return np.ascontiguousarray(y.reshape(D, S).T)[None]
```

```python
import math
from contextlib import ExitStack

import numpy as np
import concourse.bass as bass
from concourse import mybir

P = 128
D = 1024
KT = D // P
S = 256
CL = 256
TOK = S + CL
FF = 2816
FT = FF // P
GROUPS = ((0, 8), (8, 8), (16, 6))
FFN_CHUNKS = 17
FFN_HALVES = 2 * FFN_CHUNKS
LRU, NSAW, GKW, GVW = 1024, 1024, 512, 1024
HD = 64
CMP_N = S // 16 - 1
NEG = -1e30
EPS = 1e-6
NSLOT = 3
W8 = KT * 512
SLOT = W8
HALF = W8 // 2
NSPLIT = 3
BANK = 512
NG = 4

VEC = [("norm_g", 32), ("conv_w", 32), ("conv_b", 8), ("b_gates", 16), ("lam", 8), ("gla_ba", 4),
       ("gla_norm", 2), ("c", 16), ("ada_b", 144), ("norm_g2", 48), ("qg_ev", 1), ("kg_ev", 1),
       ("qg_od", 1), ("kg_od", 1), ("c_scale", 4), ("sink", 8), ("pos_k", 16), ("pos_v", 16),
       ("w2k", 256), ("w2v", 128), ("w_small", 512), ("wa2", 512), ("tbl", 16)]
CST = [("ones", 128), ("eps", 1), ("one", 1), ("ada_sel", 2), ("ident", 128), ("blk64", 128), ("flip", 128), ("rope_r", 128),
       ("oh_fwd", 512), ("oh_rev", 384), ("valid_c", 2 * CMP_N), ("gla_mask", 128), ("scan_mask", S),
       ("win_mask", 2 * S), ("rope_c", S), ("rope_s", S)]
CST_FIRST = 132
CST_OD = [("na_mask", 2 * S), ("inv_count", 4 * S)]


def offsets(table):
    at, out = 0, {}
    for name, n in table:
        out[name] = (at, n)
        at += n
    return out, at


VOFF, VN = offsets(VEC)
COFF, CN = offsets(CST)


def constants():
    c = np.zeros((P, CN), np.float32)

    def put(name, a):
        at, n = COFF[name]
        a = np.asarray(a, np.float32)
        c[:a.shape[0], at:at + n] = a.reshape(a.shape[0], n)

    put("ident", np.eye(P))
    put("ones", np.ones((P, P)))
    put("blk64", np.kron(np.eye(2), np.ones((64, 64))))
    put("flip", np.eye(P)[::-1])
    r = np.zeros((P, P))
    for i in range(P):
        if i % 32 < 16:
            r[i + 16, i] = -1.0
        else:
            r[i - 16, i] = 1.0
    put("rope_r", r)
    n = np.arange(0, 512)
    nf = np.maximum(n, 16).astype(np.float32)
    large = 16 + (np.log(nf / np.float32(16)) / np.float32(math.log(128 / 16)) * np.float32(16)).astype(np.int32)
    bucket = np.where(n < 16, n, np.minimum(large, 31))

    def onehot(dist):
        out = np.zeros((33, len(dist)), np.float32)
        for i, d in enumerate(dist):
            out[bucket[d] if d >= 0 else 32, i] = 1.0
        return out

    put("oh_fwd", onehot(np.arange(512) - 271))
    put("oh_rev", onehot(255 - np.arange(384)))
    t = np.arange(S)
    valid = (16 * np.arange(CMP_N) + 31)[None, :] <= t[:, None]
    put("valid_c", valid.reshape(2, P, CMP_N).transpose(1, 0, 2))
    s_, c_ = np.arange(P)[:, None], np.arange(P)[None, :]
    put("gla_mask", (s_ // 32 == c_ // 32) & (s_ <= c_))
    put("scan_mask", np.broadcast_to((t % 32 != 0), (P, S)))
    win = np.where(np.abs(t[:, None] - t[None, :]) <= 128, 0.0, NEG)
    put("win_mask", win.reshape(2, P, S).transpose(1, 0, 2))
    qc, kc = t[:, None] % 64, t[None, :] % 64
    start = np.clip(qc - 8, 0, 48)
    na = np.where((kc >= start) & (kc < start + 16), 0.0, NEG)
    inv = (1.0 / (np.float32(10000.0) ** (np.arange(16, dtype=np.float32) / np.float32(16)))).astype(np.float32)
    row, col = (t // 64).astype(np.float32), (t % 64).astype(np.float32)
    f = np.arange(P)
    ang = np.where((f % 64 < 32)[:, None], row[None, :], col[None, :]) * inv[f % 16][:, None]
    put("rope_c", np.cos(ang.astype(np.float32)))
    put("rope_s", np.sin(ang.astype(np.float32)))
    cnt = np.stack([np.clip(t + w - w // 2, 0, S) - np.clip(t - w // 2, 0, S) for w in (2, 4, 8, 16)])
    od = np.concatenate([na.reshape(2, P, S).transpose(1, 0, 2).reshape(P, 2 * S),
                         np.broadcast_to((1.0 / cnt).reshape(1, -1), (P, 4 * S))], axis=1).astype(np.float32)
    sel = np.zeros((P, 2))
    for g in range(4):
        sel[32 * g, 0] = sel[32 * g + 1, 1] = 1.0
    put("ada_sel", sel)
    put("eps", np.full((P, 1), EPS))
    put("one", np.ones((P, 1)))
    return c, od


def w8(i):
    return ("w8", i, W8)


W8_LRU_X, W8_LRU_G, W8_MERGE_A, W8_GQK, W8_GV, W8_OG, W8_MERGE_C = 0, 2, 4, 8, 10, 12, 14
W8_NQ, W8_KVC, W8_KSW, W8_VSW, W8_CW1, W8_MERGE_B, W8_OUT = 18, 20, 21, 22, 23, 25, 29
W8_ADA = 31
W8_EQ = W8_ADA + 36
W8_EO = W8_EQ + 3
W8_OD = W8_EO + 2
W8_OO = W8_OD + 4
W8_N = W8_OO + 2


def make_plan():
    plan = []

    def add(stage, chunk, who, free="tiles"):
        plan.append((stage, chunk, who, free))

    def ada(a, b):
        for c in range(a, b):
            add(f"ada{c}", w8(W8_ADA + c), "", "ada")

    def ffn(f):
        c = 0
        for g, (_, nf) in enumerate(GROUPS):
            for i in range(nf // 2):
                add(f"ffn{f}_in{g}_{2 * i}", ("wf", FFN_CHUNKS * f + c, W8), "AV", "split")
                add(f"ffn{f}_in{g}_{2 * i + 1}", None, "AV")
                c += 1
            for i in range(2):
                add(f"ffn{f}_out{g}_{2 * i}", ("wf", FFN_CHUNKS * f + c, nf * 512), "VV", "split")
                add(f"ffn{f}_out{g}_{2 * i + 1}", None, "VV")
                c += 1

    add("norm0", None, "A")
    for c in range(2):
        add(f"lru_x{c}", w8(W8_LRU_X + c), "AAAA")
    ada(0, 4)
    for c in range(2):
        add(f"lru_g{c}", w8(W8_LRU_G + c), "AAAA")
    add("strip", None, "V")
    add("cbias", None, "V")
    ada(4, 6)
    add("lru_gates", ("w4", 0, 2048), "A" * 16)
    add("gla_q", w8(W8_GQK), "AAAA")
    add("gla_k", w8(W8_GQK + 1), "AAAA")
    add("gla_lr", None, "A")
    add("gla_al", None, "AAAA")
    ada(6, 8)
    for c in range(2):
        add(f"gla_v{c}", w8(W8_GV + c), "VV")
    ada(8, 10)
    for c in range(2):
        add(f"gla_og{c}", w8(W8_OG + c), "AAAA")
    ada(10, 12)
    for c in range(4):
        add(f"mergeA{c}", w8(W8_MERGE_A + c), "AVAV")
    add("gla_t", None, "AA")
    add("gla_att", None, "VV")
    for c in range(2):
        add(f"nsa_q{c}", w8(W8_NQ + c), "AAAA")
    add("nsa_kvc", w8(W8_KVC), "AAAA")
    add("nsa_ksw", w8(W8_KSW), "AAAA")
    add("nsa_vsw", w8(W8_VSW), "VV")
    add("nsa_gate", None, "AA")
    add("gla_o", None, "A" * 8)
    add("gla_n", None, "AAAA")
    ada(12, 14)
    for c in range(4):
        add(f"mergeC{c}", w8(W8_MERGE_C + c), "AVAV")
    ada(14, 16)
    for i in range(2):
        add(f"cmp_hid{i}", w8(W8_CW1 + i), "A")
    add("cmp_turn", None, "AA")
    add("flip", None, "V" * 8)
    add("cmp_kv", None, "VV")
    for c in range(4):
        add(f"mergeB{c}", w8(W8_MERGE_B + c), "AVAV")
    for c in range(2):
        add(f"w_out{c}", w8(W8_OUT + c), "AAAA")
    add("norm1", None, "A")
    ada(16, 18)
    add("norm2", None, "A")
    ffn(0)
    add("norm3", None, "A")
    ada(18, 20)
    add("norm4", None, "A")
    ffn(1)
    add("norm5", None, "A")
    add("ev_q", w8(W8_EQ), "AAAA")
    add("ev_k", ("w4", 1, 2048), "A")
    add("ev_v", None, "VVVV")
    add("ev_qn", None, "A" * 5)
    add("ev_bv", w8(W8_EQ + 1), "AAAA")
    add("ev_rope", None, "V" * 5)
    add("ev_bu", w8(W8_EQ + 2), "AAAA")
    ada(20, 22)
    add("ev_mix", None, "V" * 4)
    ada(22, 36)
    for c in range(2):
        add(f"ev_out{c}", w8(W8_EO + c), "VVVV")
    add("norm6", None, "A")
    ffn(2)
    add("norm7", None, "A")
    ffn(3)
    add("norm8", None, "A")
    add("od_q", w8(W8_OD), "AAAA")
    add("od_k", w8(W8_OD + 1), "AAAA")
    add("od_qn", None, "A" * 8)
    add("od_v", w8(W8_OD + 2), "AAAA")
    add("od_xp", w8(W8_OD + 3), "AAAA")
    add("od_flip", None, "V" * 8)
    add("od_pool", None, "A" * 4)
    for c in range(2):
        add(f"od_out{c}", w8(W8_OO + c), "VVVV")
    add("norm9", None, "A")
    ffn(4)
    return plan


PLAN = make_plan()
TILE, WHO, CHUNKS, CHUNK_OF = {}, "", [], {}
_adas = _halves = 0
for _stage, _chunk, _who, _free in PLAN:
    TILE[_stage] = len(WHO)
    WHO += _who
    if _chunk is not None:
        CHUNK_OF[_stage] = len(CHUNKS)
        if _free == "ada":
            _adas += 1
            CHUNKS.append((_chunk, "ada_rows", _adas))
        elif _free == "split":
            _halves += 2
            CHUNKS.append((_chunk, "w_lo", _halves))
        else:
            CHUNKS.append((_chunk, "tiles_filled", len(WHO) + (4 if _stage == "ev_k" else 0)))
NTILES = len(WHO)


def emptied(n):
    return WHO[:n + 1].count(WHO[n])


UNITS = ([("nsa", g, t) for g in range(4) for t in range(2)]
         + [("ev", g, t) for g in range(2) for t in range(4)]
         + [("od", g, t) for g in range(2) for t in range(2)])
NSA_U, EV_U, OD_U = (0, 8), (8, 16), (16, 20)


def batches(u):
    kind, _, t = UNITS[u]
    if kind == "nsa":
        return [(seg, b) for seg in range(2) for b in range(t + 1)] + [(2, 0)]
    if kind == "ev" and t >= 2:
        return [(0, 2), (0, 3)]
    return [(0, b) for b in range(4)]


ADA_EV = [(22 + 2 * i, 23 + 2 * i) if i < 6 else (28 + i,) for i in range(8)]
ADA_BESIDE = range(22, 36)
ADA_LATE = (4, 6, 8, 10, 12)


def place(seg, r):
    return 4 * (r % 2) + 2 * seg + r // 2


def batches_before(u):
    return sum(len(batches(v)) for v in range(u))


def build(nc, d, out_x):
    f32 = mybir.dt.float32
    ACT = mybir.ActivationFunctionType
    ALU = mybir.AluOpType
    AX = mybir.AxisListType.X
    ctx = ExitStack()
    with ctx:
        def sb(name, width):
            return ctx.enter_context(nc.sbuf_tensor(name, [P, width], f32))

        xT_ = sb("xT", KT * TOK)
        zT_at = nc.sbuf_base
        zT_ = sb("zT", KT * TOK)
        cst = sb("cst", CN)
        vec = sb("vec", VN)
        ring = sb("ring", NSLOT * SLOT)
        rt = sb("rt", TOK)
        rr = sb("rr", TOK)
        mod_ = sb("mod", 2 * 144)
        modA_ = sb("modA", 2 * 48)
        gates_h_ = sb("gates_h", 2 * 32)
        mod, modA, gates_h = ([t[:, i * w:(i + 1) * w] for i in range(2)]
                              for t, w in ((mod_, 144), (modA_, 48), (gates_h_, 32)))
        cs = sb("cs", KT * 32)
        ab = sb("ada_partial", 2 * BANK)
        small = sb("small", 168)
        ARENA = 24976
        arena_at = nc.sbuf_base
        arena = sb("arena", ARENA)
        f32r = mybir.dt.float32r
        arena_r = nc.alloc_sbuf_tensor_at("arena_r", [P, ARENA], f32r, offset=arena_at)
        zT_r_ = nc.alloc_sbuf_tensor_at("zT_r", [P, KT * TOK], f32r, offset=zT_at)
        psum = ctx.enter_context(nc.psum_tensor("psum", [P, 8 * BANK], f32))
        strip_dram = nc.dram_tensor("strip_scratch", (16, 384), f32, kind="Internal").ap()
        rpb_dram = nc.dram_tensor("rpb_scratch", (120, 128), f32, kind="Internal").ap()

        xT = xT_[:, :].rearrange("p (k t) -> p k t", k=KT)
        zT = zT_[:, :].rearrange("p (k t) -> p k t", k=KT)
        z_lo = zT_r_[:, :].rearrange("p (k t) -> p k t", k=KT)

        def V(name, a=0, n=None):
            at, w = VOFF[name]
            return vec[:, at + a:at + (w if n is None else a + n)]

        def C(name):
            at, w = COFF[name]
            return cst[:, at:at + w]

        def area(at, *shape):
            n = int(np.prod(shape))
            assert at + n <= ARENA, (at, shape)
            v = arena[:, at:at + n]
            if len(shape) == 2:
                return v.rearrange("p (a b) -> p a b", a=shape[0])
            if len(shape) == 3:
                return v.rearrange("p (a b c) -> p a b c", a=shape[0], b=shape[1])
            return v

        def bank(n, width=BANK):
            return psum[:, (n % NG) * BANK:(n % NG) * BANK + width]

        def b3(ap, n, width):
            return ap.unsqueeze(1).to_broadcast([ap.shape[0], n, width])

        def rep(ap, n):
            return ap.unsqueeze(2).to_broadcast([ap.shape[0], ap.shape[1], n])

        CMP_AT = 4 * BANK

        def ada_banks(c):
            return (4, 4) if c in ADA_BESIDE else (4 + c % 2, 6 + c % 2)

        sems = {}

        def sig(name):
            if name not in sems:
                sems[name] = ctx.enter_context(nc.semaphore(name))
            return sems[name]

        landed = [sig(f"weights_landed{i}") for i in range(NSLOT)]
        filled = sig("tiles_filled")
        evac = {"A": sig("tiles_emptied_by_act"), "V": sig("tiles_emptied_by_dve")}

        def wait_evac(eng, n):
            eng.wait_ge(evac[WHO[n]], emptied(n))

        def fence(eng, name, others, k):
            eng.drain().then_inc(sig(f"fence_{name}"), 1)
            for o in others:
                eng.wait_ge(sig(f"fence_{o}"), k)

        A_xp = area(0, KT, S + 3)
        A_y = area(0, KT, S)
        A_xc = area(2072, KT, S)
        A_g = area(4120, KT, S)
        A_r = area(6168, KT, S)
        A_i = area(8216, KT, S)
        A_a = area(10264, KT, S)
        A_t = area(12312, KT, S)
        mgA_t = area(23576, 2, S)
        C_q = area(14360, 4, S)
        C_k = area(15384, 4, S)
        C_Y = area(16408, 4, S)
        C_e = area(17432, 4, S)
        C_b = area(18456, 4, S)
        C_lr = area(18456, S)
        C_v = area(19480, 2, GVW)
        C_og = area(21528, KT, S)
        C_st = area(0, 4, 7 * S)
        C_kt = area(7168, 8, P)
        C_at = area(8192, 8, P)
        C_o = area(16408, KT, S)
        mgC_t = area(14360, 2, S)
        B_q = area(9216, KT, S)
        B_kk = area(11264, 4, S)
        B_ks = area(12288, 4, S)
        B_v = area(13312, 2, BANK)
        B_kc = area(18456, 4, S)
        B_gate = area(23576, 2, 48)
        B_st = area(7168, 2, 4, S)
        B_bl = area(4224, 2, 16, 60)
        B_hid = area(6144, 2, 2, 60)
        B_stage = area(0, 16, S)
        B_hT = area(6384, 2, 256)
        B_kcT = area(6896, 60)
        B_vc = area(23672, 4, HD)
        B_P = area(0, 2108), area(3644, 2108)
        B_PT = area(2108, 3, BANK)
        B_T = area(14360, 16, S)
        B_y = area(19480, KT, S)
        mgB_t = area(22000, 2, S)
        K_strip = area(24088, 384)
        K_C = area(24472, 480)
        B_C = area(24472, 2, 16, CMP_N)
        K_tbl = area(24952, 16)
        Y_y = area(14336, KT, S)

        def part(at, *shape):
            v = arena_r[:, at:at + int(np.prod(shape))]
            return v.rearrange("p (a b) -> p a b", a=shape[0]) if len(shape) == 2 else v

        W_hi = [part(i * W8, HALF) for i in range(NSPLIT)]
        W_lo = [part(i * W8 + HALF, HALF) for i in range(NSPLIT)]

        def z_hi(nt):
            return part(12288, KT, nt)

        def a_parts(nt):
            return part(16384, KT, nt), part(20480, KT, nt)

        E_qk = area(0, 5, TOK)
        E_ks = area(2560, TOK)
        E_u = area(3072, 4, TOK)
        E_v = area(5120, 4, P)
        E_bv = area(5632, 4, BANK)
        E_y = area(12288, KT, TOK)
        E_P = area(7680, 4 * BANK), area(20992, 4 * BANK)
        E_sq = area(7680, 4, BANK)
        E_PT = area(9728, 3, BANK)
        E_w = area(16384, 2048)
        E_rt = area(18432, 5, TOK)
        O_q = area(0, 4, S)
        O_k = area(1024, 4, TOK)
        O_v = area(3072, 4, BANK)
        O_xp = area(5120, 4, S + 16)
        O_s1 = area(6208, 4, S + 16)
        O_s2 = area(7296, 4, S + 16)
        O_y = area(21568, KT, S)
        O_P = area(10432, 4 * BANK), area(8384, 4 * BANK)
        O_stage = area(8384, 2 * 8, S)
        O_PT = area(12480, 3, BANK)
        O_nb = area(14016, 2 * 8, S)
        O_wp = area(18112, 4 * P)
        O_rt = [area(12480 + j * S, S) for j in range(4)] + [area(22592 + j * TOK, TOK) for j in range(4)]
        PAD = area(19900, 128)
        O_cst = area(20028, 6 * S)
        O_na = area(20028, 2, S)
        O_ic = area(20540, 4, S)

        MODN = {4: (0, TOK), 5: (1, TOK), 6: (2, TOK), 7: (0, TOK), 8: (1, TOK), 9: (2, S)}

        def norm_xr_before(q):
            return KT * sum(1 for p in MODN if p < q)

        SPLIT = (2, 4, 6, 7, 9)

        PE_SUM = (0, 1, 2, 4)

        def norm_sum_before(q):
            return sum(1 for p in range(q) if p not in PE_SUM)

        def norm_hi_before(q):
            return KT * sum(1 for p in SPLIT if p < q)

        def prefetched(f):
            return f == 2

        def halves(f):
            out = []
            for g, (_, nf) in enumerate(GROUPS):
                out += [(g, i, False) for i in range(nf)] + [(g, i, True) for i in range(4)]
            return out

        def half_first_tile(h):
            f, (g, i, second) = h // FFN_HALVES, HALVES[h % FFN_HALVES]
            return TILE[f"ffn{f}_{'out' if second else 'in'}{g}_{i}"]

        HALVES = halves(0)

        def half_width(h):
            g, _, second = HALVES[h % FFN_HALVES]
            return GROUPS[g][1] * 256 if second else HALF

        def norm_zc_before(q):
            return KT * sum(1 for p, (_, n) in MODN.items() if p < q and n == TOK)

        block = ctx.enter_context(nc.Block())

        @block.sync
        def _(sp):
            sp.dma_start(cst[:, 0:CST_FIRST], d["cst"][:, 0:CST_FIRST]).then_inc(sig("cst_in"), 16)
            sp.dma_start(xT[:, :, 0:S], d["x"].rearrange("k p t -> p k t")).then_inc(sig("x_in"), 16)
            sp.dma_start(vec[:, :], d["vec"]).then_inc(sig("vec_in"), 16)
            for i, ((arr, idx, size), _, _) in enumerate(CHUNKS):
                if i == NSLOT:
                    sp.dma_start(cst[:, CST_FIRST:CN], d["cst"][:, CST_FIRST:CN]).then_inc(sig("cst_rest_in"), 16)
                if i >= NSLOT:
                    _, name, count = CHUNKS[i - NSLOT]
                    sp.wait_ge(sig(name), count)
                slot = i % NSLOT
                sp.dma_start(ring[:, slot * SLOT:slot * SLOT + size], d[arr][idx, :, 0:size])\
                    .then_inc(landed[slot], 16)
            wait_evac(sp, NTILES - 1)
            sp.dma_start(out_x.rearrange("k p t -> p k t"), xT[:, :, 0:S]).then_inc(sig("out_written"), 16)
            sp.wait_ge(sig("out_written"), 16)

        @block.gpsimd
        def _(pool):
            pool.memset(cs[:, :], 0.0).then_inc(sig("cs_zero"), 1)
            pool.wait_ge(sig("cs_zero"), 1)
            pool.memset(K_tbl[32:33, :], NEG).then_inc(sig("tbl_row"), 1)
            pool.dma_start(K_tbl[0:32, :], d["tbl"]).then_inc(sig("tbl_in"), 16)
            pool.wait_ge(sig("x_in"), 16)
            pool.dma_start(xT[:, :, S:TOK], d["ctx"].rearrange("k p t -> p k t")).then_inc(sig("ctx_in"), 16)
            wait_evac(pool, TILE["strip"])
            pool.dma_start(strip_dram, K_strip[0:16, :]).then_inc(sig("strip_out"), 16)
            pool.wait_ge(sig("strip_out"), 16)
            fence(pool, "pool", ("pe", "act", "dve"), 1)
            wait_evac(pool, TILE["nsa_ksw"] + 3)
            pool.dma_start(B_ks[0:64, :, :], B_kk[64:128, :, :]).then_inc(sig("kswap_in"), 16)
            pool.dma_start(B_ks[64:128, :, :], B_kk[0:64, :, :]).then_inc(sig("kswap_in"), 16)
            wait_evac(pool, TILE["gla_o"] + 7)
            for c in range(2):
                n = TILE["nsa_kvc"] + 2 * c + 1
                wait_evac(pool, n)
                for a in range(2):
                    src = B_kc[64 * a:64 * a + 64, 2 * c:2 * c + 2, :]
                    pool.dma_start(B_st[0:64, c, a::2, :], src).then_inc(sig("stack_in"), 16)
                    pool.dma_start(B_st[64:128, c, a::2, 0:S - 1], src[:, :, 1:S]).then_inc(sig("stack_in"), 16)
            fence(pool, "pool", ("pe", "act", "dve"), 2)
            src = bass.AP(tensor=strip_dram.tensor, offset=0, ap=[[1, P], [384, 16], [1, S]])
            pool.dma_start(B_stage, src).then_inc(sig("stage_in"), 16)
            for k in range(3, 5):
                fence(pool, "pool", ("pe", "act", "dve"), k)

            def norm_ctx(q, li, j):
                for k in range(KT):
                    pool.wait_ge(sig("norm_xr"), norm_xr_before(q) + k + 1)
                    pool.tensor_scalar(out=zT[:, k, S:TOK], in0=zT[:, k, S:TOK],
                                       scalar1=modA[li][:, 2 * (8 * j + k) + 1:2 * (8 * j + k) + 2],
                                       scalar2=mod[li][:, 2 * (24 * j + k) + 1:2 * (24 * j + k) + 2],
                                       op0=ALU.mult, op1=ALU.add).then_inc(sig("norm_zc"), 1)

            def ffn_parts(f, nt):
                hi, lo = a_parts(nt)
                for g, (k0, nf) in enumerate(GROUPS):
                    if g > 0:
                        pool.wait_ge(filled, TILE[f"ffn{f}_out{g - 1}_3"] + 2)
                    for i in range(nf):
                        a = (rt, rr)[i % 2][:, 0:nt]
                        wait_evac(pool, TILE[f"ffn{f}_in{g}_{i}"] + 1)
                        n = FT * f + k0 + i + 1
                        pool.tensor_copy(hi[:, i, :], a).then_inc(sig("a_hi"), 1)
                        pool.wait_ge(sig("a_hi"), n)
                        pool.tensor_tensor(out=lo[:, i, :], in0=a, in1=hi[:, i, :].bitcast(f32), op=ALU.subtract)\
                            .then_inc(sig("a_lo"), 1)

            ffn_parts(0, S)
            norm_ctx(4, 0, 0)
            ffn_parts(1, TOK)
            fence(pool, "pool", ("pe", "act", "dve"), 5)
            norm_ctx(5, 0, 1)
            pool.dma_start(E_w, d["ev_small"]).then_inc(sig("ev_small_in"), 16)
            wait_evac(pool, TILE["ev_rope"] + 4)
            pool.dma_start(E_ks[0:64, :], E_qk[64:128, 4, :]).then_inc(sig("ekswap_in"), 16)
            pool.dma_start(E_ks[64:128, :], E_qk[0:64, 4, :]).then_inc(sig("ekswap_in"), 16)
            fence(pool, "pool", ("pe", "act", "dve"), 6)
            norm_ctx(6, 0, 2)
            ffn_parts(2, TOK)
            norm_ctx(7, 1, 0)
            ffn_parts(3, TOK)
            fence(pool, "pool", ("pe", "act", "dve"), 7)
            norm_ctx(8, 1, 1)
            pool.dma_start(O_cst, d["cst_od"]).then_inc(sig("cst_od_in"), 16)
            pool.memset(PAD[0:120, :], NEG).then_inc(sig("pad_set"), 1)
            pool.wait_ge(sig("pad_set"), 1)
            pool.dma_start(PAD[0:120, 48:79], d["rpb"]).then_inc(sig("rpb_in"), 16)
            pool.wait_ge(sig("rpb_in"), 16)
            pool.dma_start(rpb_dram, PAD[0:120, :]).then_inc(sig("rpb_out"), 16)
            pool.wait_ge(sig("rpb_out"), 16)
            for t in range(2):
                for r in range(2):
                    for kr in range(4):
                        row = kr - (2 * t + 1 - r) + 7
                        src = bass.AP(tensor=rpb_dram.tensor, offset=row * 128,
                                      ap=[[1, 64], [15 * 128, 8], [1, 64]])
                        pool.dma_start(O_stage[64 * r:64 * r + 64, 8 * t:8 * t + 8, 64 * kr:64 * kr + 64], src)\
                            .then_inc(sig("rpb_stage"), 16)
            pool.dma_start(O_wp, d["pool_w"]).then_inc(sig("pool_w_in"), 16)
            fence(pool, "pool", ("pe", "act", "dve"), 8)
            fence(pool, "pool", ("pe", "act", "dve"), 9)
            ffn_parts(4, S)

        @block.tensor
        def _(pe):
            mm = nc.tensor.matmul

            def get(stage):
                i = CHUNK_OF[stage]
                pe.wait_ge(landed[i % NSLOT], 16 * (i // NSLOT + 1))
                size = CHUNKS[i][0][2]
                return ring[:, (i % NSLOT) * SLOT:(i % NSLOT) * SLOT + size]

            def open_tile(n):
                if n >= NG:
                    wait_evac(pe, n - NG)
                return bank(n)

            def feature_tiles(stage, w, cols, rhs, nt, nk=KT, first=None):
                if first is not None:
                    b = [open_tile(TILE[stage] + j) for j in range(len(cols))]
                    for k in range(nk):
                        first(k)
                        for j, c in enumerate(cols):
                            last = mm(b[j][:, 0:nt], w[:, k, c:c + P], rhs(k), start=(k == 0), stop=(k == nk - 1))
                            if k == nk - 1:
                                last.then_inc(filled, 1)
                    return
                for j, c in enumerate(cols):
                    n = TILE[stage] + j
                    b = open_tile(n)
                    for k in range(nk):
                        last = mm(b[:, 0:nt], w[:, k, c:c + P], rhs(k), start=(k == 0), stop=(k == nk - 1))
                    last.then_inc(filled, 1)

            def token_tiles(stage, w, lhs, ntt, c0, width, nk=KT):
                for j in range(ntt):
                    n = TILE[stage] + j
                    b = open_tile(n)
                    for k in range(nk):
                        last = mm(b[:, 0:width], lhs(k, j), w[:, k, c0:c0 + width],
                                  start=(k == 0), stop=(k == nk - 1))
                    last.then_inc(filled, 1)

            def w3(stage, nk=KT):
                return get(stage).rearrange("p (k n) -> p k n", k=nk)

            def norm(q, nt):
                b = open_tile(TILE[f"norm{q}"])
                if q in PE_SUM:
                    for k in range(KT):
                        pe.wait_ge(sig("norm_sq"), KT * q + k + 1)
                        last = mm(b[:, 0:nt], C("ones"), zT[:, k, 0:nt], start=(k == 0), stop=(k == KT - 1))
                    last.then_inc(filled, 1)
                    return
                pe.wait_ge(sig("norm_sum"), norm_sum_before(q) + 1)
                mm(b[:, 0:nt], C("ones"), rr[:, 0:nt], start=True, stop=True).then_inc(filled, 1)

            def normed(q):
                def first(k):
                    if q in (0, 2):
                        pe.wait_ge(sig("norm_z"), (KT if q == 2 else 0) + k + 1)
                    else:
                        pe.wait_ge(sig("norm_zm"), norm_xr_before(q) + k + 1)
                        if MODN[q][1] == TOK:
                            pe.wait_ge(sig("norm_zc"), norm_zc_before(q) + k + 1)
                return first

            def ada_rows(c):
                w = w3(f"ada{c}")
                if c in ADA_BESIDE:
                    pe.wait_ge(sig("ada_done"), c)
                elif c >= 2:
                    pe.wait_ge(sig("ada_copied"), c - 1)
                at = ada_banks(c)[0] * BANK
                for k in range(KT):
                    g = k % 4
                    last = mm(psum[32 * g:32 * g + 32, at:at + BANK], cs[:, 32 * k:32 * k + 32], w[:, k, :],
                              start=(k < 4), stop=(k >= 4), skip_group_check=True)
                last.then_inc(sig("ada_rows"), 1)

            def ada_cols(c):
                pe.wait_ge(sig("ada_copied"), c + 1)
                if c >= 2:
                    pe.wait_ge(sig("ada_done"), c - 1)
                to = ada_banks(c)[1] * BANK
                for j in range(4):
                    at = (c % 2) * BANK + j * P
                    last = mm(psum[:, to + 2 * j:to + 2 * j + 2], ab[:, at:at + P], C("ada_sel"),
                              start=True, stop=True)
                last.then_inc(sig("ada_cols"), 1)

            def ada(a, b_, cols=True):
                for c in range(a, b_):
                    ada_rows(c)
                    if c > 0 and (c > a or c in ADA_LATE):
                        ada_cols(c - 1)
                if cols:
                    ada_cols(b_ - 1)

            def ffn(f, nt, q):
                hi, lo = a_parts(nt)
                zh = z_hi(nt)
                for i, (g, j, second) in enumerate(HALVES):
                    h = FFN_HALVES * f + i
                    nk = GROUPS[g][1] if second else KT
                    wh = W_hi[h % NSPLIT][:, 0:nk * 256].rearrange("p (k n) -> p k n", k=nk)
                    wl = W_lo[h % NSPLIT][:, 0:nk * 256].rearrange("p (k n) -> p k n", k=nk)
                    pe.wait_ge(sig("w_lo"), h + 1)
                    xh, xl = (hi, lo) if second else (zh, z_lo)
                    b = [open_tile(half_first_tile(h) + c) for c in range(2)]
                    for c, k in ([(c, k) for k in range(nk) for c in range(2)] if i == 0 else
                                 [(c, k) for c in range(2) for k in range(nk)]):
                        if i == 0 and c == 0:
                            pe.wait_ge(sig("norm_lo"), norm_hi_before(q) + k + 1)
                        if second and j == 0 and c == 0:
                            pe.wait_ge(sig("a_lo"), FT * f + GROUPS[g][0] + k + 1)
                        whc, wlc = wh[:, k, c * P:(c + 1) * P], wl[:, k, c * P:(c + 1) * P]
                        mm(b[c][:, 0:nt], whc, xh[:, k, 0:nt], start=(k == 0), stop=False)
                        mm(b[c][:, 0:nt], whc, xl[:, k, 0:nt], start=False, stop=False)
                        last = mm(b[c][:, 0:nt], wlc, xh[:, k, 0:nt], start=False, stop=(k == nk - 1))
                        if k == nk - 1:
                            last.then_inc(filled, 1)

            def merge(br, y, ready):
                for c in range(4):
                    stage = f"merge{br}{c}"
                    w = w3(stage)
                    for j in range(2):
                        for half in range(2):
                            n = TILE[stage] + 2 * j + half
                            b = open_tile(n)
                            if half and c == 0 and j == 0:
                                ready()
                            for k in range(KT):
                                last = mm(b[:, 0:S], w[:, k, 256 * half + P * j:256 * half + P * j + P],
                                          y[:, k, :] if half else zT[:, k, 0:S], start=(k == 0), stop=(k == KT - 1))
                            last.then_inc(filled, 1)

            hrhs = lambda k: zT[:, k, 0:S]

            pe.wait_ge(sig("cst_in"), 16)
            norm(0, S)
            pe.wait_ge(sig("vec_in"), 16)
            for c in range(2):
                feature_tiles(f"lru_x{c}", w3(f"lru_x{c}"), range(0, 512, P), hrhs, S,
                              first=normed(0) if c == 0 else None)
            pe.wait_ge(sig("cs_ready"), 1)
            ada(0, 4, False)
            for c in range(2):
                feature_tiles(f"lru_g{c}", w3(f"lru_g{c}"), range(0, 512, P), hrhs, S)
            pe.wait_ge(sig("cst_rest_in"), 16)
            pe.wait_ge(sig("tbl_in"), 16)
            pe.wait_ge(sig("tbl_row"), 1)
            oh = C("oh_rev")
            b = open_tile(TILE["strip"])
            mm(b[0:16, 0:384], K_tbl[0:33, :], oh[0:33, :], start=True, stop=True).then_inc(filled, 1)
            oh = C("oh_fwd")
            b = open_tile(TILE["cbias"])
            for t in range(2):
                for c in range(CMP_N):
                    at = P * t - 16 * c - 31 + 271
                    col = (t * CMP_N + c) * 16
                    last = mm(b[:, col:col + 16], oh[0:33, at:at + P], K_tbl[0:33, :], start=True, stop=True)
            last.then_inc(filled, 1)
            ada(4, 6, False)
            w = get("lru_gates").rearrange("p (g n e) -> p g n e", g=2, n=8)
            for k in range(KT):
                pe.wait_ge(sig("lru_xc"), k + 1)
                for g in range(2):
                    n = TILE["lru_gates"] + 2 * k + g
                    b = open_tile(n)
                    mm(b[:, 0:S], w[:, g, k, :], A_xc[:, k, :], start=True, stop=True).then_inc(filled, 1)
            feature_tiles("gla_q", w3("gla_q"), range(0, 512, P), hrhs, S)
            feature_tiles("gla_k", w3("gla_k"), range(0, 512, P), hrhs, S)
            wsm = V("w_small").rearrange("p (k n) -> p k n", k=KT)
            b = open_tile(TILE["gla_lr"])
            for k in range(KT):
                last = mm(b[0:16, 0:S], wsm[:, k, 48:64], zT[:, k, 0:S], start=(k == 0), stop=(k == KT - 1))
            last.then_inc(filled, 1)
            wait_evac(pe, TILE["gla_lr"])
            for h in range(4):
                b = open_tile(TILE["gla_al"] + h)
                mm(b[:, 0:S], V("wa2", h * P, P)[0:16, :], C_lr[0:16, :], start=True, stop=True).then_inc(filled, 1)
            ada(6, 8, False)
            for c in range(2):
                token_tiles(f"gla_v{c}", w3(f"gla_v{c}"), lambda k, j: zT[:, k, j * P:(j + 1) * P], 2, 0, 512)
            ada(8, 10, False)
            for c in range(2):
                feature_tiles(f"gla_og{c}", w3(f"gla_og{c}"), range(0, 512, P), hrhs, S)
            ada(10, 12, False)
            merge("A", A_y, lambda: pe.wait_ge(sig("lru_y"), KT))
            ada_cols(11)
            fence(pe, "pe", ("act", "dve", "pool"), 1)

            pe.wait_ge(sig("gla_kend"), 1)
            for t in range(2):
                b = open_tile(TILE["gla_t"] + t)
                for h in range(4):
                    last = nc.tensor.transpose(b[:, h * P:(h + 1) * P], C_e[:, h, t * P:(t + 1) * P], C("ident"))
                last.then_inc(filled, 1)
            for t in range(2):
                b = open_tile(TILE["gla_att"] + t)
                for h in range(4):
                    last = mm(b[:, h * P:(h + 1) * P], C_k[:, h, t * P:(t + 1) * P], C_q[:, h, t * P:(t + 1) * P],
                              start=True, stop=True)
                last.then_inc(filled, 1)
            wait_evac(pe, TILE["gla_t"] + 1)
            between = [lambda: feature_tiles("nsa_q0", w3("nsa_q0"), range(0, 512, P), hrhs, S),
                       lambda: feature_tiles("nsa_q1", w3("nsa_q1"), range(0, 512, P), hrhs, S),
                       lambda: feature_tiles("nsa_kvc", w3("nsa_kvc"), range(0, 512, P), hrhs, S),
                       lambda: feature_tiles("nsa_ksw", w3("nsa_ksw"), range(0, 512, P), hrhs, S),
                       lambda: token_tiles("nsa_vsw", w3("nsa_vsw"), lambda k, j: zT[:, k, j * P:(j + 1) * P],
                                           2, 0, 512),
                       lambda: token_tiles("nsa_gate", wsm, lambda k, j: zT[:, k, j * P:(j + 1) * P], 2, 0, 48)]
            for c in range(7):
                for h in range(4):
                    if c >= 1:
                        pe.wait_ge(sig("gla_state"), 4 * (c - 1) + h + 1)
                    rows = slice(32 * (c % 4), 32 * (c % 4) + 32)
                    mm(psum[:, (4 + h) * BANK:(4 + h) * BANK + S], C_kt[rows, 4 * (c // 4) + h, :],
                       C_v[rows, c // 4, h * S:(h + 1) * S], start=True, stop=True,
                       tile_position=(32 * (c % 4), 0)).then_inc(sig("gla_upd"), 1)
                if c < len(between):
                    between[c]()
            wait_evac(pe, TILE["gla_att"] + 1)
            pe.wait_ge(sig("gla_state"), 28)
            for h in range(4):
                for e in range(2):
                    n = TILE["gla_o"] + 2 * h + e
                    b = open_tile(n)
                    for t in range(2):
                        mm(b[:, t * P:(t + 1) * P], C_v[:, t, h * S + e * P:h * S + (e + 1) * P],
                           C_at[:, 4 * t + h, :], start=(t == 0), stop=False, skip_group_check=True)
                    for c in range(1, 8):
                        st = C_st[:, h, (c - 1) * S + e * P:(c - 1) * S + (e + 1) * P]
                        last = mm(b[:, 32 * c:32 * c + 32], st, C_q[:, h, 32 * c:32 * c + 32],
                                  start=False, stop=(c == 7), skip_group_check=True)
                    last.then_inc(filled, 1)
            for h in range(4):
                b = open_tile(TILE["gla_n"] + h)
                pe.wait_ge(sig("gla_sq"), 2 * h + 2)
                for e in range(2):
                    last = mm(b[:, 0:S], C("ones"), C_st[:, h, e * S:(e + 1) * S], start=(e == 0), stop=(e == 1))
                last.then_inc(filled, 1)
            ada_rows(12)
            ada_rows(13)
            merge("C", C_og, lambda: pe.wait_ge(sig("gla_y"), KT))
            ada_cols(12)
            ada_cols(13)
            fence(pe, "pe", ("act", "dve", "pool"), 2)

            def scores(u):
                kind, g, t = UNITS[u]

                def free(b):
                    if u > 0:
                        pe.wait_ge(sig("att_exp"), 4 * (u - 1) + b + 1)

                if kind == "nsa":
                    nk = P * (t + 1)

                    def compressed(a):
                        half = slice(64 * a, 64 * a + 64)
                        for j in range(2):
                            at = CMP_AT + (2 * a + j) * CMP_N
                            last = mm(psum[:, at:at + CMP_N], B_q[half, 2 * g + j, t * P:(t + 1) * P],
                                      B_kcT[half, g * CMP_N:(g + 1) * CMP_N], start=True, stop=True)
                        return last

                    for r in range(4):
                        half = slice(64 * (r % 2), 64 * (r % 2) + 64)
                        if r < 2:
                            free(1 + 2 * r)
                        if r == 2:
                            compressed(0).then_inc(sig("cmp_even"), 1)
                        for seg in range(2):
                            kk = (B_kk if g % 2 == r % 2 else B_ks)[half, 2 * seg + g // 2, 0:nk]
                            at = place(seg, r) * S
                            last = mm(psum[:, at:at + nk], B_q[half, 2 * g + r // 2, t * P:(t + 1) * P], kk,
                                      start=True, stop=True)
                        if r == 2:
                            last.then_inc(sig("att_score"), 1)
                    pe.wait_ge(sig("cmp_even"), u + 1)
                    last = compressed(1)
                else:
                    ev = kind == "ev"
                    k0 = S if t >= 2 else 0
                    for r in range(4):
                        h = 4 * g + r
                        half = slice(64 * (r % 2), 64 * (r % 2) + 64)
                        free(r)
                        if ev:
                            q = E_qk[half, h // 2, t * P:(t + 1) * P]
                            kk = (E_qk[half, 4, k0:TOK] if g == r % 2 else E_ks[half, k0:TOK])
                        else:
                            q = O_q[half, h // 2, t * P:(t + 1) * P]
                            kk = O_k[half, h // 2, 0:TOK]
                        last = mm(psum[:, r * BANK + k0:(r + 1) * BANK], q, kk, start=True, stop=True)
                        if r == 1:
                            last.then_inc(sig("att_score"), 1)
                last.then_inc(sig("att_score"), 1)

            def att_out(u, Pb, PT):
                kind, g, t = UNITS[u]
                Pb = Pb[u % 2]
                bs = batches(u)
                gb0 = batches_before(u)

                def keys(i):
                    return CMP_N if bs[i][0] == 2 else P

                def turn(i):
                    seg, blk = bs[i]
                    gb = gb0 + i
                    if gb >= 2:
                        pe.wait_ge(sig("att_copied"), gb - 1)
                    pt = psum[:, (5 + gb % 2) * BANK:(6 + gb % 2) * BANK]
                    for r in range(4):
                        if kind == "nsa":
                            at = 2048 + (2 * (r % 2) + r // 2) * CMP_N if seg == 2 else place(seg, r) * S + blk * P
                        else:
                            at = r * BANK + blk * P
                        last = nc.tensor.transpose(pt[0:keys(i), r * P:(r + 1) * P], Pb[:, at:at + keys(i)],
                                                   C("ident"))
                    last.then_inc(sig("att_turned"), 1)

                def multiply(i):
                    seg, blk = bs[i]
                    gb = gb0 + i
                    pe.wait_ge(sig("att_copied"), gb + 1)
                    if i == 0 and u > 0:
                        pe.wait_ge(sig("att_out"), u)
                    pt = PT[0:keys(i), gb % 3, :].rearrange("p (j a t) -> p a j t", j=2, a=2)
                    for a in range(2):
                        o = psum[64 * a:64 * a + 64, 7 * BANK:7 * BANK + 2 * P]
                        if kind == "od":
                            for j in range(2):
                                h = 4 * g + 2 * j + a
                                last = mm(o[:, j * P:(j + 1) * P], O_v[:, blk, h * HD:(h + 1) * HD], pt[:, a, j, :],
                                          start=(i == 0 and j == 0), stop=(i == len(bs) - 1 and j == 1),
                                          skip_group_check=True)
                        else:
                            if kind == "ev":
                                v = E_v[:, blk, g * HD:(g + 1) * HD]
                            elif seg == 2:
                                v = B_vc[0:CMP_N, g, :]
                            else:
                                v = B_v[:, blk, seg * S + g * HD:seg * S + (g + 1) * HD]
                            last = mm(o.rearrange("p (j t) -> p j t", j=2), v, pt[:, a, :, :],
                                      start=(i == 0), stop=(i == len(bs) - 1), skip_group_check=True)
                    last.then_inc(sig("att_mult"), 1)

                pe.wait_ge(sig("att_p"), u + 1)
                for i in range(len(bs)):
                    turn(i)
                    if i >= 1:
                        multiply(i - 1)
                multiply(len(bs) - 1)

            def attention(u0, u1, Pb, PT, ready, extra):
                ready()
                scores(u0)
                late = None
                for u in range(u0, u1):
                    beside = extra(u - u0)
                    if late is not None:
                        ada_cols(late)
                        late = None
                    if beside:
                        ada_rows(beside[0])
                    if u + 1 < u1:
                        scores(u + 1)
                    if beside:
                        ada_cols(beside[0])
                    if len(beside) > 1:
                        late = beside[1]
                        ada_rows(late)
                    att_out(u, Pb, PT)

            ada(14, 16)
            for i in range(2):
                w = w3(f"cmp_hid{i}", 16)
                pe.wait_ge(sig("cmp_blocks"), 4 * i + 4)
                b = open_tile(TILE[f"cmp_hid{i}"])
                for m in range(16):
                    last = mm(b[0:60, 0:256], B_bl[:, i, m, :], w[:, m, :], start=(m == 0), stop=(m == 15))
                last.then_inc(filled, 1)
            for i in range(2):
                wait_evac(pe, TILE[f"cmp_hid{i}"])
                b = open_tile(TILE["cmp_turn"] + i)
                for k in range(2):
                    last = nc.tensor.transpose(b[:, 60 * k:60 * k + 60], B_hT[0:60, i, k * P:(k + 1) * P],
                                               C("ident")[0:60, 0:60])
                last.then_inc(filled, 1)
            pe.wait_ge(sig("stage_in"), 16)
            for i in range(8):
                b = open_tile(TILE["flip"] + i)
                mm(b[:, :], C("flip"), area(i * BANK, BANK), start=True, stop=True).then_inc(filled, 1)
            wait_evac(pe, TILE["cmp_turn"] + 1)
            b = open_tile(TILE["cmp_kv"])
            w2k = V("w2k").rearrange("p (k n) -> p k n", k=2)
            w2v = V("w2v").rearrange("p (k n) -> p k n", k=2)
            for k in range(2):
                last = mm(b[:, 0:60], w2k[:, k, :], B_hid[:, 0, k, :], start=(k == 0), stop=(k == 1))
            last.then_inc(filled, 1)
            b = open_tile(TILE["cmp_kv"] + 1)
            for g in range(4):
                for k in range(2):
                    last = mm(b[0:CMP_N, g * HD:(g + 1) * HD], B_hid[:, 1, k, g * CMP_N:(g + 1) * CMP_N],
                              w2v[:, k, :], start=(k == 0), stop=(k == 1))
            last.then_inc(filled, 1)

            def nsa_ready():
                pe.wait_ge(sig("ada_done"), 16)
                wait_evac(pe, TILE["cmp_kv"] + 1)
                pe.wait_ge(sig("kswap_in"), 32)

            fence(pe, "pe", ("act", "dve", "pool"), 3)
            attention(*NSA_U, B_P, B_PT, nsa_ready, lambda i: ())
            merge("B", B_y, lambda: pe.wait_ge(sig("att_out"), NSA_U[1]))
            wait_evac(pe, TILE["mergeB3"] + 3)
            for c in range(2):
                feature_tiles(f"w_out{c}", w3(f"w_out{c}"), range(0, 512, P), lambda k: zT[:, k, S:TOK], S)
            fence(pe, "pe", ("act", "dve", "pool"), 4)
            norm(1, S)
            ada_rows(16)
            ada_rows(17)
            norm(2, S)
            ada_cols(16)
            ada_cols(17)
            ffn(0, S, 2)
            norm(3, S)
            ada_rows(18)
            ada_rows(19)

            norm(4, TOK)
            ada_cols(18)
            ada_cols(19)
            ffn(1, TOK, 4)
            norm(5, TOK)
            fence(pe, "pe", ("act", "dve", "pool"), 5)
            feature_tiles("ev_q", w3("ev_q"), range(0, 512, P), lambda k: zT[:, k, :], TOK, first=normed(5))
            wkv = w3("ev_k")
            feature_tiles("ev_k", wkv, (0,), lambda k: zT[:, k, :], TOK)
            tok = lambda k, j: zT[:, k, j * P:(j + 1) * P]
            token_tiles("ev_v", wkv, tok, 4, P, P)
            for j in range(5):
                b = open_tile(TILE["ev_qn"] + j)
                pe.wait_ge(sig("head_sq"), j + 1)
                mm(b[:, :], C("blk64"), E_rt[:, j, :], start=True, stop=True).then_inc(filled, 1)
            token_tiles("ev_bv", w3("ev_bv"), tok, 4, 0, 512)
            for j in range(5):
                b = open_tile(TILE["ev_rope"] + j)
                pe.wait_ge(sig("head_n"), j + 1)
                mm(b[:, 0:S], C("rope_r"), E_qk[:, j, 0:S], start=True, stop=True).then_inc(filled, 1)
            feature_tiles("ev_bu", w3("ev_bu"), range(0, 512, P), lambda k: zT[:, k, :], TOK)
            ada(20, 22)
            pe.wait_ge(sig("ev_small_in"), 16)
            pe.wait_ge(sig("ev_vv"), 4)
            wsT = E_w[:, 1024:2048].rearrange("p (g i) -> p g i", g=8)
            for jp in range(4):
                b = open_tile(TILE["ev_mix"] + jp)
                for a in range(2):
                    g = 2 * jp + a
                    for t in range(4):
                        last = mm(b[64 * a:64 * a + 64, t * P:(t + 1) * P], E_bv[:, t, g * HD:(g + 1) * HD],
                                  wsT[:, g, :], start=True, stop=True)
                last.then_inc(filled, 1)

            def ev_ready():
                pe.wait_ge(sig("ada_done"), 22)
                pe.wait_ge(sig("ekswap_in"), 32)
                wait_evac(pe, TILE["ev_rope"] + 4)
                wait_evac(pe, TILE["ev_mix"] + 3)
                wait_evac(pe, TILE["ev_v"] + 3)

            attention(*EV_U, E_P, E_PT, ev_ready, lambda i: ADA_EV[i])
            pe.wait_ge(sig("att_out"), EV_U[1])
            pe.wait_ge(sig("mix_y"), 4)
            fence(pe, "pe", ("act", "dve", "pool"), 6)
            for c in range(2):
                feature_tiles(f"ev_out{c}", w3(f"ev_out{c}"), range(0, 512, P), lambda k: E_y[:, k, :], TOK)
            norm(6, TOK)
            ffn(2, TOK, 6)

            norm(7, TOK)
            ffn(3, TOK, 7)
            norm(8, TOK)
            fence(pe, "pe", ("act", "dve", "pool"), 7)
            feature_tiles("od_q", w3("od_q"), range(0, 512, P), hrhs, S, first=normed(8))
            feature_tiles("od_k", w3("od_k"), range(0, 512, P), lambda k: zT[:, k, :], TOK)
            for j in range(8):
                b = open_tile(TILE["od_qn"] + j)
                nt = S if j < 4 else TOK
                pe.wait_ge(sig("head_sq"), 5 + j + 1)
                mm(b[:, 0:nt], C("blk64"), O_rt[j], start=True, stop=True).then_inc(filled, 1)
            token_tiles("od_v", w3("od_v"), tok, 4, 0, 512)
            feature_tiles("od_xp", w3("od_xp"), range(0, 512, P), hrhs, S)
            pe.wait_ge(sig("rpb_stage"), 16 * 16)
            for i in range(8):
                b = open_tile(TILE["od_flip"] + i)
                mm(b[:, :], C("flip"), area(8384 + i * BANK, BANK), start=True, stop=True).then_inc(filled, 1)
            pe.wait_ge(sig("pool_w_in"), 16)
            for g in range(4):
                b = open_tile(TILE["od_pool"] + g)
                pe.wait_ge(sig("pooled"), g + 1)
                mm(b[:, 0:S], O_wp[:, g * P:(g + 1) * P], O_s1[:, g, 0:S], start=True, stop=True)\
                    .then_inc(filled, 1)

            def od_ready():
                pe.wait_ge(sig("head_n"), 13)
                wait_evac(pe, TILE["od_pool"] + 3)
                wait_evac(pe, TILE["od_v"] + 3)

            fence(pe, "pe", ("act", "dve", "pool"), 8)
            attention(*OD_U, O_P, O_PT, od_ready, lambda i: ())
            pe.wait_ge(sig("att_out"), OD_U[1])
            fence(pe, "pe", ("act", "dve", "pool"), 9)
            for c in range(2):
                feature_tiles(f"od_out{c}", w3(f"od_out{c}"), range(0, 512, P), lambda k: O_y[:, k, :], S)
            norm(9, S)
            ffn(4, S, 9)

        @block.scalar
        def _(act):
            A = nc.scalar.activation
            steps = [0]

            def link(ins):
                steps[0] += 1
                ins.then_inc(sig("act_step"), 1)
                act.wait_ge(sig("act_step"), steps[0])

            def empty(n):
                act.wait_ge(filled, n + 1)
                return bank(n)

            def copy_tiles(stage, n, dst, nt=S, func=ACT.Identity, rows=P, scale=1.0, pre=None):
                for j in range(n):
                    b = empty(TILE[stage] + j)
                    if pre is not None:
                        pre(j)
                    A(dst(j), b[0:rows, 0:nt], func, scale=scale).then_inc(evac["A"], 1)

            def w_hi(h):
                if h >= 5 * FFN_HALVES:
                    return
                i = CHUNK_OF[f"ffn{h // FFN_HALVES}_in0_0"] + (h % FFN_HALVES) // 2
                if h % 2 == 0:
                    act.wait_ge(landed[i % NSLOT], 16 * (i // NSLOT + 1))
                if h >= NSPLIT:
                    act.wait_ge(filled, half_first_tile(h - NSPLIT) + 2)
                n = half_width(h)
                at = (i % NSLOT) * SLOT + (h % 2) * n
                A(W_hi[h % NSPLIT][:, 0:n], ring[:, at:at + n], ACT.Identity).then_inc(sig("w_hi"), 1)

            def first_w_hi(f):
                for h in range(2):
                    w_hi(FFN_HALVES * f + h)

            def squares(q, nt, src, ready, k0, k1):
                for k in range(k0, k1):
                    ready(k)
                    if k == 0 and q > 0 and q not in PE_SUM:
                        act.wait_ge(sig("norm_recip"), q)
                    A(rr[:, 0:nt] if k == 0 and q not in PE_SUM else zT[:, k, 0:nt], src[:, k, 0:nt], ACT.Square)\
                        .then_inc(sig("norm_sq"), 1)

            def norm(q, nt, src, ready, squared=0, middle=None):
                A(small[:, 160:161], C("one"), ACT.Sqrt)
                squares(q, nt, src, ready, squared, KT)
                b = empty(TILE[f"norm{q}"])
                A(rt[:, 0:nt], b[:, 0:nt], ACT.Sqrt, scale=1.0 / D, bias=C("eps")).then_inc(evac["A"], 1)
                if middle is not None:
                    middle()
                for k in range(KT):
                    if q in MODN:
                        j, li = MODN[q][0], 0 if q < 7 else 1
                        act.wait_ge(sig("norm_xr"), norm_xr_before(q) + k + 1)
                        A(zT[:, k, 0:S], zT[:, k, 0:S], ACT.Identity,
                          scale=modA[li][:, 2 * (8 * j + k):2 * (8 * j + k) + 1],
                          bias=mod[li][:, 2 * (24 * j + k):2 * (24 * j + k) + 1]).then_inc(sig("norm_zm"), 1)
                    if q in SPLIT:
                        if q == 2:
                            act.wait_ge(sig("norm_z"), KT + k + 1)
                        else:
                            act.wait_ge(sig("norm_zm"), norm_xr_before(q) + k + 1)
                        if nt == TOK:
                            act.wait_ge(sig("norm_zc"), norm_zc_before(q) + k + 1)
                        A(z_hi(nt)[:, k, :], zT[:, k, 0:nt], ACT.Identity).then_inc(sig("norm_hi"), 1)

            def ffn(f, nt, square=None):
                for i, (g, j, second) in enumerate(HALVES):
                    h = FFN_HALVES * f + i
                    if i + 2 < FFN_HALVES or prefetched(f):
                        w_hi(h + 2)
                    if not second:
                        n = half_first_tile(h)
                        b = empty(n)
                        m = FT * f + GROUPS[g][0] + j
                        if m - FT * f >= 2:
                            act.wait_ge(sig("a_lo"), m - 1)
                        A((rt, rr)[j % 2][:, 0:nt], b[:, 0:nt], ACT.Silu).then_inc(evac["A"], 1)
                    elif g == 2 and j > 0 and square is not None:
                        square(2 * j - 2, 2 * j)

            def merge(br, tmp):
                for c in range(4):
                    for j in range(2):
                        n = TILE[f"merge{br}{c}"] + 2 * j
                        b = empty(n)
                        i = 2 * c + j
                        if i >= 2:
                            m = TILE[f"merge{br}{(i - 2) // 2}"] + 2 * (i % 2) + 1
                            wait_evac(act, m)
                        A(tmp[:, i % 2, :], b[:, 0:S], ACT.Sigmoid).then_inc(evac["A"], 1)

            act.wait_ge(sig("cst_in"), 16)
            norm(0, S, xT, lambda k: act.wait_ge(sig("x_in"), 16))
            act.wait_ge(sig("vec_in"), 16)
            act.wait_ge(sig("cs_zero"), 1)
            A(cs[:, :].rearrange("p (k n) -> p k n", k=KT)[:, :, 0:2], V("c").rearrange("p (k s) -> p k s", s=2),
              ACT.Silu).then_inc(sig("cs_ready"), 1)
            link(A(small[:, 0:8], V("lam"), ACT.Abs))
            link(A(small[:, 8:16], small[:, 0:8], ACT.Exp, scale=-1.0))
            A(small[:, 16:24], small[:, 8:16], ACT.Ln, bias=C("one")).then_inc(sig("lru_ln"), 1)
            for c in range(2):
                copy_tiles(f"lru_x{c}", 4, lambda j: A_xp[:, 4 * c + j, 3:S + 3])
            for c in range(2):
                copy_tiles(f"lru_g{c}", 4, lambda j: A_g[:, 4 * c + j, :], func=ACT.Gelu_apprx_tanh)
            wait_evac(act, TILE["lru_x1"] + 3)
            for k in range(KT):
                A(A_xc[:, k, :], A_xp[:, k, 3:S + 3], ACT.Identity, scale=V("conv_w", 24 + k, 1),
                  bias=V("conv_b", k, 1)).then_inc(sig("lru_tap"), 1)
            for k in range(KT):
                for g, dst in enumerate((A_r, A_i)):
                    n = TILE["lru_gates"] + 2 * k + g
                    b = empty(n)
                    A(dst[:, k, :], b[:, 0:S], ACT.Sigmoid, bias=V("b_gates", 8 * g + k, 1)).then_inc(evac["A"], 1)
            act.wait_ge(sig("lru_coef"), 1)
            wait_evac(act, TILE["lru_gates"] + 15)
            for k in range(KT):
                A(A_a[:, k, :], A_r[:, k, :], ACT.Exp, scale=small[:, 32 + k:33 + k]).then_inc(sig("lru_a"), 1)
            for k in range(KT):
                A(A_t[:, k, :], A_r[:, k, :], ACT.Tanh, scale=small[:, 40 + k:41 + k]).then_inc(sig("lru_tanh"), 1)
            copy_tiles("gla_q", 4, lambda j: C_q[:, j, :], scale=float(P) ** -0.5)
            act.wait_ge(sig("lru_v"), 1)
            A(A_t, A_t, ACT.Sqrt, scale=2.0).then_inc(sig("lru_root"), 1)
            copy_tiles("gla_k", 4, lambda j: C_k[:, j, :])
            copy_tiles("gla_lr", 1, lambda j: C_lr[0:16, :], rows=16)
            for h in range(4):
                b = empty(TILE["gla_al"] + h)
                A(C_Y[:, h, :], b[:, 0:S], ACT.Identity, bias=V("gla_ba", h, 1)).then_inc(evac["A"], 1)
            wait_evac(act, TILE["gla_al"] + 3)
            link(A(C_e, C_Y, ACT.Abs))
            link(A(C_e, C_e, ACT.Exp, scale=-1.0))
            A(C_e, C_e, ACT.Ln, bias=C("one")).then_inc(sig("gla_ln"), 1)
            for c in range(2):
                copy_tiles(f"gla_og{c}", 4, lambda j: C_og[:, 4 * c + j, :], func=ACT.Silu)
            act.wait_ge(sig("gla_b"), 1)
            A(C_Y, C_b, ACT.Exp, scale=1.0 / 16).then_inc(sig("gla_eb"), 1)
            A(C_e, C_b, ACT.Exp, scale=-1.0 / 16).then_inc(sig("gla_eb"), 1)
            act.wait_ge(sig("gla_bd"), 1)
            A(C_b, C_b, ACT.Exp, scale=1.0 / 16).then_inc(sig("gla_eb"), 1)
            merge("A", mgA_t)
            fence(act, "act", ("pe", "dve", "pool"), 1)

            for t in range(2):
                b = empty(TILE["gla_t"] + t)
                A(C_kt[:, 4 * t:4 * t + 4, :], b[:, :].rearrange("p (h d) -> p h d", h=4), ACT.Identity)\
                    .then_inc(evac["A"], 1)
            for c in range(2):
                copy_tiles(f"nsa_q{c}", 4, lambda j: B_q[:, 4 * c + j, :], scale=HD ** -0.5)
            copy_tiles("nsa_kvc", 4, lambda j: B_kc[:, j, :])
            copy_tiles("nsa_ksw", 4, lambda j: B_kk[:, j, :])
            copy_tiles("nsa_gate", 2, lambda j: B_gate[:, j, :], nt=48, func=ACT.Sigmoid)
            for j in range(8):
                b = empty(TILE["gla_o"] + j)
                if j == 0:
                    act.wait_ge(sig("gla_state"), 28)
                A(C_o[:, j, :], b[:, 0:S], ACT.Identity).then_inc(evac["A"], 1)
            wait_evac(act, TILE["gla_o"] + 7)
            for j in range(8):
                A(C_st[:, j // 2, (j % 2) * S:(j % 2 + 1) * S], C_o[:, j, :], ACT.Square).then_inc(sig("gla_sq"), 1)
            for h in range(4):
                b = empty(TILE["gla_n"] + h)
                A(C_st[:, h, 2 * S:3 * S], b[:, 0:S], ACT.Sqrt, scale=1.0 / 256, bias=C("eps"))\
                    .then_inc(evac["A"], 1)
            merge("C", mgC_t)
            fence(act, "act", ("pe", "dve", "pool"), 2)

            def att_exp(u, Pb, part):
                kind, g, t = UNITS[u]
                Pb = Pb[u % 2]
                nm, sm = small[:, 0:12], small[:, 16:28]
                if part % 2 == 0:
                    act.wait_ge(sig("att_max"), 2 * u + part // 2 + 1)
                if part == 0:
                    if u >= 2:
                        act.wait_ge(sig("att_turned"), batches_before(u - 1))
                if kind == "nsa":
                    nk = P * (t + 1)
                    for i in (2 * part, 2 * part + 1):
                        last = A(Pb[:, i * S:i * S + nk], psum[:, i * S:i * S + nk], ACT.Exp,
                                 bias=nm[:, i:i + 1], accum_out=sm[:, i:i + 1])
                    if part == 3:
                        for r in range(4):
                            at = r * CMP_N
                            last = A(Pb[:, 2048 + at:2048 + at + CMP_N], psum[:, CMP_AT + at:CMP_AT + at + CMP_N],
                                     ACT.Exp, bias=nm[:, 8 + r:9 + r], accum_out=sm[:, 8 + r:9 + r])
                else:
                    k0 = S if t >= 2 else 0
                    if kind == "ev" and part % 2 == 0:
                        A(small[:, 32 + part:34 + part], small[:, 28 + part:30 + part], ACT.Exp)
                    r = part
                    last = A(Pb[:, r * BANK + k0:(r + 1) * BANK], psum[:, r * BANK + k0:(r + 1) * BANK],
                             ACT.Exp, bias=nm[:, r:r + 1], accum_out=sm[:, r:r + 1])
                last.then_inc(sig("att_exp"), 1)

            def att_copy(u, PT, i):
                seg, gb = batches(u)[i][0], batches_before(u) + i
                act.wait_ge(sig("att_turned"), gb + 1)
                if gb >= 3:
                    act.wait_ge(sig("att_mult"), gb - 2)
                n = CMP_N if seg == 2 else P
                A(PT[0:n, gb % 3, :], psum[0:n, (5 + gb % 2) * BANK:(6 + gb % 2) * BANK], ACT.Identity)\
                    .then_inc(sig("att_copied"), 1)

            def attention(u0, u1, Pb, PT):
                for part in range(4):
                    att_exp(u0, Pb, part)
                for u in range(u0, u1):
                    for i in range(5):
                        if i < len(batches(u)):
                            att_copy(u, PT, i)
                        if i >= 1 and u + 1 < u1:
                            att_exp(u + 1, Pb, i - 1)

            for i in range(2):
                copy_tiles(f"cmp_hid{i}", 1, lambda j: B_hT[0:60, i, :], nt=256, rows=60, func=ACT.Gelu_apprx_tanh)
            copy_tiles("cmp_turn", 2, lambda i: area(6144 + 120 * i, 120), nt=120)
            fence(act, "act", ("pe", "dve", "pool"), 3)
            attention(*NSA_U, B_P, B_PT)
            merge("B", mgB_t)
            for c in range(2):
                copy_tiles(f"w_out{c}", 4, lambda j: Y_y[:, 4 * c + j, :])
            fence(act, "act", ("pe", "dve", "pool"), 4)
            norm(1, S, Y_y, lambda k: wait_evac(act, TILE["w_out0"] + k))
            first_w_hi(0)
            norm(2, S, xT, lambda k: act.wait_ge(sig("norm_x"), k + 1))
            after0 = S, Y_y, lambda k: wait_evac(act, TILE["ffn0_out2_0"] + k)
            ffn(0, S, lambda a, b: squares(3, *after0, a, b))
            norm(3, *after0, squared=6)

            def ready4(k):
                act.wait_ge(sig("norm_x"), KT + k + 1)
                act.wait_ge(sig("ctx_in"), 16)
                act.wait_ge(sig("mod_ready"), 1)

            first_w_hi(1)
            norm(4, TOK, xT, ready4)
            after1 = TOK, xT, lambda k: wait_evac(act, TILE["ffn1_out2_0"] + k)
            ffn(1, TOK, lambda a, b: squares(5, *after1, a, b))
            norm(5, *after1, squared=6,
                 middle=lambda: fence(act, "act", ("pe", "dve", "pool"), 5))
            copy_tiles("ev_q", 4, lambda j: E_qk[:, j, :], nt=TOK)
            copy_tiles("ev_k", 1, lambda j: E_qk[:, 4, :], nt=TOK)
            wait_evac(act, TILE["ev_k"])
            for j in range(5):
                A(E_rt[:, j, :], E_qk[:, j, :], ACT.Square).then_inc(sig("head_sq"), 1)
            for j in range(5):
                b = empty(TILE["ev_qn"] + j)
                A(E_rt[:, j, :], b[:, :], ACT.Sqrt, scale=1.0 / HD, bias=C("eps")).then_inc(evac["A"], 1)
            copy_tiles("ev_bv", 4, lambda j: E_bv[:, j, :], nt=TOK, func=ACT.Gelu_apprx_tanh)
            copy_tiles("ev_bu", 4, lambda j: E_u[:, j, :], nt=TOK, func=ACT.Gelu_apprx_tanh)
            act.wait_ge(sig("ev_vsum"), 1)
            A(small[:, 96:128], small[:, 64:96], ACT.Sqrt, scale=1.0 / HD, bias=C("eps")).then_inc(sig("ev_vrt"), 1)
            attention(*EV_U, E_P, E_PT)
            fence(act, "act", ("pe", "dve", "pool"), 6)
            first_w_hi(2)
            norm(6, TOK, xT, lambda k: wait_evac(act, TILE["ev_out0"] + k))
            after2 = TOK, xT, lambda k: wait_evac(act, TILE["ffn2_out2_0"] + k)
            ffn(2, TOK, lambda a, b: squares(7, *after2, a, b))

            norm(7, *after2, squared=6)
            after3 = TOK, xT, lambda k: wait_evac(act, TILE["ffn3_out2_0"] + k)
            ffn(3, TOK, lambda a, b: squares(8, *after3, a, b))
            norm(8, *after3, squared=6,
                 middle=lambda: fence(act, "act", ("pe", "dve", "pool"), 7))
            copy_tiles("od_q", 4, lambda j: O_q[:, j, :])
            copy_tiles("od_k", 4, lambda j: O_k[:, j, :], nt=TOK)
            wait_evac(act, TILE["od_k"] + 3)
            for j in range(8):
                src = O_q[:, j, :] if j < 4 else O_k[:, j - 4, :]
                A(O_rt[j], src, ACT.Square).then_inc(sig("head_sq"), 1)
            for j in range(8):
                nt = S if j < 4 else TOK
                b = empty(TILE["od_qn"] + j)
                A(O_rt[j], b[:, 0:nt], ACT.Sqrt, scale=1.0 / HD, bias=C("eps")).then_inc(evac["A"], 1)
            copy_tiles("od_v", 4, lambda t: O_v[:, t, :], nt=BANK)
            copy_tiles("od_xp", 4, lambda j: O_xp[:, j, 8:S + 8])
            wait_evac(act, TILE["od_flip"] + 7)
            for g in range(4):
                b = empty(TILE["od_pool"] + g)
                A(O_y[:, g, :], b[:, 0:S], ACT.Copy, scale=V("c_scale", g, 1)).then_inc(evac["A"], 1)
            fence(act, "act", ("pe", "dve", "pool"), 8)
            attention(*OD_U, O_P, O_PT)
            fence(act, "act", ("pe", "dve", "pool"), 9)
            first_w_hi(4)
            norm(9, S, xT, lambda k: wait_evac(act, TILE["od_out0"] + k))
            ffn(4, S)

        @block.vector
        def _(dve):
            v = nc.vector
            steps = [0]

            def link(ins):
                steps[0] += 1
                ins.then_inc(sig("dve_step"), 1)
                dve.wait_ge(sig("dve_step"), steps[0])

            def empty(n):
                dve.wait_ge(filled, n + 1)
                return bank(n)

            def w_lo(h):
                if h >= 5 * FFN_HALVES:
                    return
                i = CHUNK_OF[f"ffn{h // FFN_HALVES}_in0_0"] + (h % FFN_HALVES) // 2
                dve.wait_ge(sig("w_hi"), h + 1)
                n = half_width(h)
                at = (i % NSLOT) * SLOT + (h % 2) * n
                v.tensor_tensor(out=W_lo[h % NSPLIT][:, 0:n], in0=ring[:, at:at + n],
                                in1=W_hi[h % NSPLIT][:, 0:n].bitcast(f32), op=ALU.subtract).then_inc(sig("w_lo"), 1)

            def add_square(q, nt, k):
                dve.wait_ge(sig("norm_sq"), KT * q + k + 1)
                ins = v.tensor_tensor(out=rr[:, 0:nt], in0=rr[:, 0:nt], in1=zT[:, k, 0:nt], op=ALU.add)
                if k == KT - 1:
                    ins.then_inc(sig("norm_sum"), 1)
                else:
                    link(ins)

            def first_w_lo(f):
                for h in range(2):
                    w_lo(FFN_HALVES * f + h)

            def norm(q, nt, src, gain=None, summed=1, middle=None):
                if q not in PE_SUM:
                    for k in range(summed, KT):
                        add_square(q, nt, k)
                wait_evac(dve, TILE[f"norm{q}"])
                v.reciprocal(rr[:, 0:nt], rt[:, 0:nt]).then_inc(sig("norm_rr"), 1)
                dve.wait_ge(sig("norm_rr"), q + 1)
                if middle is not None:
                    middle()
                for k in range(KT + 2):
                    if k < KT:
                        if q in MODN:
                            v.tensor_tensor(out=zT[:, k, 0:nt], in0=src[:, k, 0:nt], in1=rr[:, 0:nt], op=ALU.mult)\
                                .then_inc(sig("norm_xr"), 1)
                        elif q in (0, 2):
                            v.scalar_tensor_tensor(out=zT[:, k, 0:nt], in0=src[:, k, 0:nt], scalar=gain(k),
                                                   in1=rr[:, 0:nt], op0=ALU.mult, op1=ALU.mult)\
                                .then_inc(sig("norm_z"), 1)
                        else:
                            link(v.scalar_tensor_tensor(out=src[:, k, 0:nt], in0=src[:, k, 0:nt], scalar=gain(k),
                                                        in1=rr[:, 0:nt], op0=ALU.mult, op1=ALU.mult))
                            v.tensor_tensor(out=xT[:, k, 0:nt], in0=src[:, k, 0:nt], in1=xT[:, k, 0:nt], op=ALU.add)\
                                .then_inc(sig("norm_x"), 1)
                    if q in SPLIT and k >= 2:
                        j = k - 2
                        dve.wait_ge(sig("norm_hi"), norm_hi_before(q) + j + 1)
                        v.tensor_tensor(out=z_lo[:, j, 0:nt],
                                        in0=zT[:, j, 0:nt], in1=z_hi(nt)[:, j, :].bitcast(f32), op=ALU.subtract)\
                            .then_inc(sig("norm_lo"), 1)
                dve.engine_nop().then_inc(sig("norm_recip"), 1)

            def ada_copy(c):
                dve.wait_ge(sig("ada_rows"), c + 1)
                if c >= 2:
                    dve.wait_ge(sig("ada_cols"), c - 1)
                at = ada_banks(c)[0] * BANK
                v.tensor_copy(ab[:, (c % 2) * BANK:(c % 2 + 1) * BANK], psum[:, at:at + BANK])\
                    .then_inc(sig("ada_copied"), 1)

            def ada_bias(c):
                dve.wait_ge(sig("ada_cols"), c + 1)
                li, j, at = c // 18, c % 18, ada_banks(c)[1] * BANK
                v.tensor_tensor(out=mod[li][:, 8 * j:8 * j + 8].rearrange("p (j s) -> p j s", s=2),
                                in0=psum[:, at:at + 8].rearrange("p (j s) -> p j s", s=2),
                                in1=rep(V("ada_b", 4 * c, 4), 2), op=ALU.add).then_inc(sig("ada_done"), 1)

            def ada(a, b_, cols=True):
                for c in range(a, b_):
                    ada_copy(c)
                    if c > 0 and (c > a or c in ADA_LATE):
                        ada_bias(c - 1)
                if cols:
                    ada_bias(b_ - 1)

            def mods(li):
                dve.wait_ge(sig("ada_done"), 18 * (li + 1))
                for j in range(3):
                    g = rep(V("norm_g2", 24 * li + 8 * j, 8), 2)
                    last = v.scalar_tensor_tensor(
                        out=modA[li][:, 16 * j:16 * j + 16].rearrange("p (k s) -> p k s", s=2),
                        in0=mod[li][:, 16 * (3 * j + 1):16 * (3 * j + 2)].rearrange("p (k s) -> p k s", s=2),
                        scalar=1.0, in1=g, op0=ALU.add, op1=ALU.mult)
                for j in range(2):
                    last = v.tensor_scalar(out=gates_h[li][:, 16 * j:16 * j + 16],
                                           in0=mod[li][:, 16 * (6 * j + 2):16 * (6 * j + 3)],
                                           scalar1=0.5, scalar2=None, op0=ALU.mult)
                last.then_inc(sig("mod_ready"), 1)
                dve.wait_ge(sig("mod_ready"), li + 1)

            def residual(n, k, nt, gate):
                b = empty(n)
                for s in range(nt // S):
                    last = v.scalar_tensor_tensor(out=xT[:, k, s * S:(s + 1) * S], in0=b[:, s * S:(s + 1) * S],
                                                  scalar=gate(k, s), in1=xT[:, k, s * S:(s + 1) * S],
                                                  op0=ALU.mult, op1=ALU.add)
                last.then_inc(evac["V"], 1)

            def ffn(f, nt, li=None, which=None, q=None):
                for i, (g, j, second) in enumerate(HALVES):
                    h = FFN_HALVES * f + i
                    if i + 2 < FFN_HALVES or prefetched(f):
                        w_lo(h + 2)
                    n = half_first_tile(h)
                    if not second:
                        b = empty(n + 1)
                        wait_evac(dve, n)
                        a = (rt, rr)[j % 2][:, 0:nt]
                        v.tensor_tensor(out=a, in0=b[:, 0:nt], in1=a, op=ALU.mult).then_inc(evac["V"], 1)
                        continue
                    for c in range(2):
                        k = 2 * j + c
                        if which is not None:
                            residual(n + c, k, nt, lambda k, s: gates_h[li][:, 16 * which + 2 * k + s:
                                                                            16 * which + 2 * k + s + 1])
                        elif g == 0:
                            b = empty(n + c)
                            v.tensor_copy(Y_y[:, k, :], b[:, 0:S]).then_inc(evac["V"], 1)
                        else:
                            b = empty(n + c)
                            v.tensor_tensor(out=Y_y[:, k, :], in0=b[:, 0:S], in1=Y_y[:, k, :], op=ALU.add)\
                                .then_inc(evac["V"], 1)
                        if g == 2 and q is not None and k >= 2:
                            add_square(q, nt, k - 1)

            def merge(br, tmp):
                for c in range(4):
                    for j in range(2):
                        i = 2 * c + j
                        n = TILE[f"merge{br}{c}"] + 2 * j + 1
                        b = empty(n)
                        wait_evac(dve, n - 1)
                        m = zT[:, i, S:TOK]
                        if br == "A":
                            v.tensor_tensor(out=m, in0=b[:, 0:S], in1=tmp[:, i % 2, :], op=ALU.mult)\
                                .then_inc(evac["V"], 1)
                        else:
                            link(v.tensor_tensor(out=tmp[:, i % 2, :], in0=b[:, 0:S], in1=tmp[:, i % 2, :],
                                                 op=ALU.mult))
                            v.tensor_tensor(out=m, in0=m, in1=tmp[:, i % 2, :], op=ALU.add).then_inc(evac["V"], 1)

            dve.wait_ge(sig("vec_in"), 16)
            dve.wait_ge(sig("cst_in"), 16)
            link(v.memset(A_xp[:, :, 0:3], 0.0))
            dve.wait_ge(sig("x_in"), 16)
            norm(0, S, xT, lambda k: V("norm_g", k, 1))
            ada(0, 4, False)
            dve.wait_ge(sig("cst_rest_in"), 16)
            b = empty(TILE["strip"])
            v.tensor_copy(K_strip[0:16, :], b[0:16, 0:384]).then_inc(evac["V"], 1)
            b = empty(TILE["cbias"])
            v.tensor_copy(K_C.rearrange("p (t h c) -> p t c h", t=2, h=16),
                          b[:, 0:480].rearrange("p (t c h) -> p t c h", t=2, c=CMP_N)).then_inc(evac["V"], 1)
            ada(4, 6, False)
            for k in range(KT):
                dve.wait_ge(sig("lru_tap"), k + 1)
                for i in range(3):
                    ins = v.scalar_tensor_tensor(out=A_xc[:, k, :], in0=A_xp[:, k, i:i + S],
                                                 scalar=V("conv_w", 8 * i + k, 1), in1=A_xc[:, k, :],
                                                 op0=ALU.mult, op1=ALU.add)
                    if i < 2:
                        link(ins)
                    else:
                        ins.then_inc(sig("lru_xc"), 1)
            link(v.tensor_scalar(out=small[:, 48:56], in0=V("lam"), scalar1=-1.0, scalar2=0.0,
                                 op0=ALU.mult, op1=ALU.max))
            dve.wait_ge(sig("lru_ln"), 1)
            link(v.tensor_tensor(out=small[:, 48:56], in0=small[:, 48:56], in1=small[:, 16:24], op=ALU.add))
            v.tensor_scalar(out=small[:, 32:40], in0=small[:, 48:56], scalar1=-8.0, scalar2=None, op0=ALU.mult)
            v.tensor_scalar(out=small[:, 40:48], in0=small[:, 48:56], scalar1=8.0, scalar2=None, op0=ALU.mult)\
                .then_inc(sig("lru_coef"), 1)
            wait_evac(dve, TILE["lru_gates"] + 15)
            dve.wait_ge(sig("lru_xc"), KT)
            link(v.tensor_tensor(out=A_i, in0=A_i, in1=A_xc, op=ALU.mult))
            dve.wait_ge(sig("lru_tanh"), KT)
            link(v.tensor_scalar(out=A_r, in0=A_t, scalar1=1.0, scalar2=None, op0=ALU.add))
            link(v.reciprocal(A_r, A_r))
            v.tensor_tensor(out=A_t, in0=A_t, in1=A_r, op=ALU.mult).then_inc(sig("lru_v"), 1)
            dve.wait_ge(sig("lru_root"), 1)
            dve.wait_ge(sig("lru_a"), KT)
            link(v.tensor_tensor(out=A_i, in0=A_i, in1=A_t, op=ALU.mult))
            for k in range(KT):
                last = v.tensor_tensor_scan(out=A_r[:, k, :], data0=A_a[:, k, :], data1=A_i[:, k, :], initial=0.0,
                                            op0=ALU.mult, op1=ALU.add)
            link(last)
            for k in range(KT):
                v.tensor_tensor(out=A_y[:, k, :], in0=A_r[:, k, :], in1=A_g[:, k, :], op=ALU.mult)\
                    .then_inc(sig("lru_y"), 1)
            ada(6, 8, False)
            dve.wait_ge(sig("gla_ln"), 1)
            link(v.tensor_scalar(out=C_Y, in0=C_Y, scalar1=0.0, scalar2=None, op0=ALU.min))
            link(v.tensor_tensor(out=C_Y, in0=C_Y, in1=C_e, op=ALU.subtract))
            for h in range(4):
                last = v.tensor_tensor_scan(out=C_b[:, h, :], data0=C("scan_mask"), data1=C_Y[:, h, :], initial=0.0,
                                            op0=ALU.mult, op1=ALU.add)
            last.then_inc(sig("gla_b"), 1)
            dve.wait_ge(sig("gla_b"), 1)
            for c in range(2):
                for t in range(2):
                    b = empty(TILE[f"gla_v{c}"] + t)
                    v.tensor_copy(C_v[:, t, c * 512:(c + 1) * 512], b[:, :]).then_inc(evac["V"], 1)
            ada(8, 10, False)
            dve.wait_ge(sig("gla_eb"), 2)
            blast = small[:, 128:160]
            link(v.tensor_copy(blast, arena[:, 18456 + 31:18456 + 1024:32]))
            v.tensor_tensor(out=arena[:, 18456:19480].rearrange("p (c i) -> p c i", i=32), in0=rep(blast, 32),
                            in1=arena[:, 18456:19480].rearrange("p (c i) -> p c i", i=32), op=ALU.subtract)\
                .then_inc(sig("gla_bd"), 1)
            v.tensor_copy(small[:, 96:128], arena[:, 16408 + 31:16408 + 1024:32])
            wait_evac(dve, TILE["gla_k"] + 3)
            v.tensor_tensor(out=C_q, in0=C_q, in1=C_Y, op=ALU.mult)
            dve.wait_ge(sig("gla_eb"), 3)
            link(v.tensor_tensor(out=C_b, in0=C_b, in1=C_k, op=ALU.mult))
            link(v.tensor_tensor(out=C_k, in0=C_k, in1=C_e, op=ALU.mult))
            v.tensor_copy(C_e, C_b).then_inc(sig("gla_kend"), 1)
            ada(10, 12, False)
            merge("A", mgA_t)
            ada_bias(11)
            fence(dve, "dve", ("pe", "act", "pool"), 1)

            link(v.memset(C_at, 0.0))
            mask = C("gla_mask").bitcast(mybir.dt.uint32)
            for t in range(2):
                b = empty(TILE["gla_att"] + t)
                for h in range(4):
                    last = v.copy_predicated(C_at[:, 4 * t + h, :], mask, b[:, h * P:(h + 1) * P])
                last.then_inc(evac["V"], 1)
            for c in range(7):
                for h in range(4):
                    dve.wait_ge(sig("gla_upd"), 4 * c + h + 1)
                    upd = psum[:, (4 + h) * BANK:(4 + h) * BANK + S]
                    dst = C_st[:, h, c * S:(c + 1) * S]
                    if c == 0:
                        v.tensor_copy(dst, upd).then_inc(sig("gla_state"), 1)
                    else:
                        dve.wait_ge(sig("gla_state"), 4 * (c - 1) + h + 1)
                        v.scalar_tensor_tensor(out=dst, in0=C_st[:, h, (c - 1) * S:c * S],
                                               scalar=small[:, 96 + 8 * h + c:96 + 8 * h + c + 1], in1=upd,
                                               op0=ALU.mult, op1=ALU.add).then_inc(sig("gla_state"), 1)
                if c == 5:
                    for t in range(2):
                        b = empty(TILE["nsa_vsw"] + t)
                        v.tensor_copy(B_v[:, t, :], b[:, :]).then_inc(evac["V"], 1)
            for h in range(4):
                wait_evac(dve, TILE["gla_n"] + h)
                r = C_st[:, h, 2 * S:3 * S]
                link(v.reciprocal(r, r))
                for e in range(2):
                    o = C_o[:, 2 * h + e, :]
                    link(v.scalar_tensor_tensor(out=o, in0=o, scalar=V("gla_norm", e, 1), in1=r,
                                                op0=ALU.mult, op1=ALU.mult))
                    v.tensor_tensor(out=C_og[:, 2 * h + e, :], in0=C_og[:, 2 * h + e, :], in1=o, op=ALU.mult)\
                        .then_inc(sig("gla_y"), 1)
            ada_copy(12)
            ada_copy(13)
            merge("C", mgC_t)
            ada_bias(12)
            ada_bias(13)
            fence(dve, "dve", ("pe", "act", "pool"), 2)

            def att_max(u):
                kind, g, t = UNITS[u]
                nm = small[:, 0:12]
                for a in range(2):
                    dve.wait_ge(sig("att_score"), 2 * u + a + 1)
                    if kind == "nsa":
                        nk = P * (t + 1)
                        j0 = P if t == 0 else 0
                        s_ = psum[:, 4 * a * S:4 * (a + 1) * S].rearrange("p (s j k) -> p s j k", s=2, j=2)
                        s_ = s_[:, :, :, 0:nk]
                        bias = B_T[:, 4 * g + 2 * a:4 * g + 2 * a + 2, j0:j0 + nk].unsqueeze(1)\
                            .to_broadcast([P, 2, 2, nk])
                        link(v.tensor_tensor(out=s_, in0=s_, in1=bias, op=ALU.add))
                        ins = v.reduce_max(nm[:, 4 * a:4 * a + 4],
                                           psum[:, 4 * a * S:4 * (a + 1) * S].rearrange("p (r k) -> p r k", r=4)
                                           [:, :, 0:nk], AX, negate=True)
                        if a == 1:
                            sc = psum[:, CMP_AT:CMP_AT + 4 * CMP_N].rearrange("p (r c) -> p r c", r=4)
                            link(v.tensor_tensor(out=sc, in0=sc, in1=B_C[:, t, 4 * g:4 * g + 4, :], op=ALU.add))
                            ins = v.reduce_max(nm[:, 8:12], sc, AX, negate=True)
                        ins.then_inc(sig("att_max"), 1)
                        continue
                    k0 = S if t >= 2 else 0
                    s_ = psum[:, 2 * a * BANK:2 * (a + 1) * BANK].rearrange("p (r k) -> p r k", r=2)
                    if k0 == 0:
                        if kind == "ev":
                            m = b3(C("win_mask").rearrange("p (t k) -> p t k", t=2)[:, t, :], 2, S)
                        else:
                            r0 = 8 * t + 4 * g + 2 * a
                            m = O_nb[:, r0:r0 + 2, :]
                        link(v.tensor_tensor(out=s_[:, :, 0:S], in0=s_[:, :, 0:S], in1=m, op=ALU.add))
                    nma = nm[:, 2 * a:2 * a + 2]
                    ins = v.reduce_max(nma, s_[:, :, k0:BANK], AX, negate=True)
                    if kind == "ev":
                        link(ins)
                        sink = V("sink", 4 * g + 2 * a, 2)
                        link(v.scalar_tensor_tensor(out=nma, in0=sink, scalar=-1.0, in1=nma,
                                                    op0=ALU.mult, op1=ALU.min))
                        ins = v.tensor_tensor(out=small[:, 28 + 2 * a:30 + 2 * a], in0=sink, in1=nma, op=ALU.add)
                    ins.then_inc(sig("att_max"), 1)

            def att_norm(u, Pb):
                kind, g, t = UNITS[u]
                sm = small[:, 16:28]
                Pb = Pb[u % 2]
                dve.wait_ge(sig("att_exp"), 4 * (u + 1))
                if kind == "nsa":
                    nk = P * (t + 1)
                    link(v.reciprocal(sm, sm))
                    for seg, br in enumerate((1, 2, 0)):
                        gate = B_gate[:, t, 16 * br + 4 * g:16 * br + 4 * g + 4]
                        if seg == 2:
                            ins = v.tensor_tensor(out=small[:, 44:48], in0=sm[:, 8:12], in1=gate, op=ALU.mult)
                        else:
                            out = small[:, 36:44].rearrange("p (a s j) -> p a s j", a=2, s=2)[:, :, seg, :]
                            si = sm[:, 0:8].rearrange("p (a s j) -> p a s j", a=2, s=2)[:, :, seg, :]
                            v.tensor_tensor(out=out, in0=si, in1=gate.rearrange("p (a j) -> p a j", a=2), op=ALU.mult)
                    link(ins)
                    p_ = Pb[:, 0:2048].rearrange("p (r k) -> p r k", r=8)[:, :, 0:nk]
                    v.tensor_tensor(out=p_, in0=p_, in1=rep(small[:, 36:44], nk), op=ALU.mult)
                    pc = Pb[:, 2048:2108].rearrange("p (r c) -> p r c", r=4)
                    link(v.tensor_tensor(out=pc, in0=pc, in1=rep(small[:, 44:48], CMP_N), op=ALU.mult))
                    va = C("valid_c").rearrange("p (t c) -> p t c", t=2)[:, t, :]
                    v.tensor_tensor(out=pc, in0=pc, in1=b3(va, 4, CMP_N), op=ALU.mult).then_inc(sig("att_p"), 1)
                    return
                k0 = S if t >= 2 else 0
                if kind == "ev":
                    link(v.tensor_tensor(out=sm[:, 0:4], in0=sm[:, 0:4], in1=small[:, 32:36], op=ALU.add))
                link(v.reciprocal(small[:, 36:40], sm[:, 0:4]))
                p_ = Pb[:, 0:2048].rearrange("p (r k) -> p r k", r=4)[:, :, k0:BANK]
                v.tensor_tensor(out=p_, in0=p_, in1=rep(small[:, 36:40], BANK - k0), op=ALU.mult)\
                    .then_inc(sig("att_p"), 1)

            def att_done(u, y):
                kind, g, t = UNITS[u]
                dve.wait_ge(sig("att_mult"), batches_before(u + 1))
                if kind == "od":
                    k = 4 + 2 * g
                else:
                    k = 2 * g
                v.tensor_copy(y[:, k:k + 2, t * P:(t + 1) * P],
                              psum[:, 7 * BANK:7 * BANK + 2 * P].rearrange("p (j t) -> p j t", j=2))\
                    .then_inc(sig("att_out"), 1)

            def attention(u0, u1, Pb, y, extra):
                att_max(u0)
                late = None
                for u in range(u0, u1):
                    beside = extra(u - u0)
                    if late is not None:
                        ada_bias(late)
                        late = None
                    att_norm(u, Pb)
                    if beside:
                        ada_copy(beside[0])
                        ada_bias(beside[0])
                    if u + 1 < u1:
                        att_max(u + 1)
                    if len(beside) > 1:
                        late = beside[1]
                        ada_copy(late)
                    att_done(u, y)

            ada(14, 16)
            for i in range(2):
                pos = V("pos_k" if i == 0 else "pos_v")
                dve.wait_ge(sig("stack_in"), 8 * 16)
                for g in range(4):
                    st = 7168 + (4 * i + g) * S
                    for half in range(2):
                        at = st + 16 * half
                        src = arena[:, at:at + 240].rearrange("p (c m two) -> p m c two", m=8, two=2)[:, :, :, 0]
                        last = v.tensor_tensor(out=B_bl[:, i, 8 * half:8 * half + 8, g * CMP_N:(g + 1) * CMP_N],
                                               in0=src, in1=rep(pos[:, 8 * half:8 * half + 8], CMP_N), op=ALU.add)
                    last.then_inc(sig("cmp_blocks"), 1)
            for i in range(8):
                b = empty(TILE["flip"] + i)
                v.tensor_copy(area(14360 + i * BANK, BANK), b[:, :]).then_inc(evac["V"], 1)
            b = empty(TILE["cmp_kv"])
            v.tensor_copy(B_kcT, b[:, 0:60]).then_inc(evac["V"], 1)
            b = empty(TILE["cmp_kv"] + 1)
            v.tensor_copy(B_vc[0:CMP_N, :, :], b[0:CMP_N, 0:256].rearrange("p (g d) -> p g d", g=4))\
                .then_inc(evac["V"], 1)
            fence(dve, "dve", ("pe", "act", "pool"), 3)
            attention(*NSA_U, B_P, B_y, lambda i: ())
            merge("B", mgB_t)
            fence(dve, "dve", ("pe", "act", "pool"), 4)
            norm(1, S, Y_y, lambda k: V("norm_g", 8 + k, 1))
            ada_copy(16)
            ada_copy(17)
            w_lo(0)
            norm(2, S, xT, lambda k: V("norm_g", 16 + k, 1))
            ada_bias(16)
            ada_bias(17)
            w_lo(1)
            mods(0)
            ffn(0, S, q=3)
            norm(3, S, Y_y, lambda k: V("norm_g", 24 + k, 1), summed=KT - 1)

            ada_copy(18)
            ada_copy(19)
            w_lo(FFN_HALVES)
            norm(4, TOK, xT)
            ada_bias(18)
            ada_bias(19)
            w_lo(FFN_HALVES + 1)
            ffn(1, TOK, 0, 0, q=5)
            norm(5, TOK, xT, summed=KT - 1, middle=lambda: fence(dve, "dve", ("pe", "act", "pool"), 5))
            for t in range(4):
                b = empty(TILE["ev_v"] + t)
                v.tensor_copy(E_v[:, t, :], b[:, 0:P]).then_inc(evac["V"], 1)
            def head_norm(stage, j, x, rtile, gain, scale, last_sig=True):
                wait_evac(dve, TILE[stage] + j)
                link(v.reciprocal(rtile, rtile))
                if scale != 1.0:
                    link(v.tensor_scalar(out=x, in0=x, scalar1=scale, scalar2=None, op0=ALU.mult))
                v.scalar_tensor_tensor(out=x, in0=x, scalar=gain, in1=rtile, op0=ALU.mult, op1=ALU.mult)\
                    .then_inc(sig("head_n"), 1)

            for j in range(5):
                head_norm("ev_qn", j, E_qk[:, j, :], E_rt[:, j, :], V("qg_ev") if j < 4 else V("kg_ev"),
                          HD ** -0.5 if j < 4 else 1.0)
            for j in range(5):
                b = empty(TILE["ev_rope"] + j)
                link(v.tensor_tensor(out=E_rt[:, j, 0:S], in0=b[:, 0:S], in1=C("rope_s"), op=ALU.mult))
                link(v.tensor_tensor(out=E_qk[:, j, 0:S], in0=E_qk[:, j, 0:S], in1=C("rope_c"), op=ALU.mult))
                v.tensor_tensor(out=E_qk[:, j, 0:S], in0=E_qk[:, j, 0:S], in1=E_rt[:, j, 0:S], op=ALU.add)\
                    .then_inc(evac["V"], 1)
            wait_evac(dve, TILE["ev_bv"] + 3)
            link(v.tensor_tensor(out=E_sq, in0=E_bv, in1=E_bv, op=ALU.mult))
            v.tensor_reduce(out=small[:, 64:96], in_=E_sq.rearrange("p t (g d) -> p (t g) d", d=HD), axis=AX,
                            op=ALU.add).then_inc(sig("ev_vsum"), 1)
            ada(20, 22)
            dve.wait_ge(sig("ev_vrt"), 1)
            link(v.reciprocal(small[:, 96:128], small[:, 96:128]))
            bv = E_bv.rearrange("p t (g d) -> p (t g) d", d=HD)
            link(v.tensor_tensor(out=bv, in0=bv, in1=rep(small[:, 96:128], HD), op=ALU.mult))
            dve.wait_ge(sig("ev_small_in"), 16)
            for t in range(4):
                v.tensor_tensor(out=E_bv[:, t, :], in0=E_bv[:, t, :], in1=E_w[:, 0:512], op=ALU.mult)\
                    .then_inc(sig("ev_vv"), 1)
            for jp in range(4):
                b = empty(TILE["ev_mix"] + jp)
                mixed = E_y[:, 4 + jp, :]
                wait_evac(dve, TILE["ev_bu"] + 3)
                v.tensor_tensor(out=mixed.rearrange("p (t i) -> p t i", t=4),
                                in0=b[:, :].rearrange("p (t i) -> p t i", t=4),
                                in1=b3(E_w[:, 512 + jp * P:512 + (jp + 1) * P], 4, P), op=ALU.add)\
                    .then_inc(evac["V"], 1)
                wait_evac(dve, TILE["ev_mix"] + jp)
                v.tensor_tensor(out=mixed, in0=mixed, in1=E_u[:, jp, :], op=ALU.mult).then_inc(sig("mix_y"), 1)
            attention(*EV_U, E_P, E_y, lambda i: ADA_EV[i])
            mods(1)
            fence(dve, "dve", ("pe", "act", "pool"), 6)

            def mixer_residual(stage, li, nt, q):
                for k in range(KT):
                    residual(TILE[stage] + k, k, nt, lambda k, s: mod[li][:, 80 + 2 * k + s:80 + 2 * k + s + 1])
                    if k >= 2:
                        add_square(q, nt, k - 1)

            first_w_lo(2)
            mixer_residual("ev_out0", 0, TOK, 6)
            norm(6, TOK, xT, summed=KT - 1)
            ffn(2, TOK, 0, 1, q=7)

            norm(7, TOK, xT, summed=KT - 1)
            ffn(3, TOK, 1, 0, q=8)
            norm(8, TOK, xT, summed=KT - 1, middle=lambda: fence(dve, "dve", ("pe", "act", "pool"), 7))
            v.memset(O_xp[:, :, 0:8], 0.0)
            link(v.memset(O_xp[:, :, S + 8:S + 16], 0.0))
            for j in range(8):
                x = O_q[:, j, :] if j < 4 else O_k[:, j - 4, :]
                head_norm("od_qn", j, x, O_rt[j],
                          V("qg_od") if j < 4 else V("kg_od"), HD ** -0.5 if j < 4 else 1.0)
            for i in range(8):
                b = empty(TILE["od_flip"] + i)
                t = i // 4
                if i == 0:
                    dve.wait_ge(sig("cst_od_in"), 16)
                na = O_na[:, t, :]
                v.tensor_tensor(out=O_nb[:, 2 * i:2 * i + 2, :], in0=b[:, :].rearrange("p (h k) -> p h k", h=2),
                                in1=b3(na, 2, S), op=ALU.add).then_inc(evac["V"], 1)
            for g, w in enumerate((2, 4, 8, 16)):
                wait_evac(dve, TILE["od_xp"] + g)
                src, dst, n, step = O_xp[:, g, :], O_s1[:, g, :], S + 16, 1
                other = O_s2[:, g, :]
                while step < w:
                    n -= step
                    link(v.tensor_tensor(out=dst[:, 0:n], in0=src[:, 0:n], in1=src[:, step:step + n], op=ALU.add))
                    src, dst, other = dst, other, dst
                    step *= 2
                at = 8 - w // 2
                link(v.tensor_tensor(out=dst[:, 0:S], in0=src[:, at:at + S], in1=O_ic[:, g, :], op=ALU.mult))
                link(v.tensor_tensor(out=src[:, 0:S], in0=dst[:, 0:S], in1=O_xp[:, g, 8:S + 8], op=ALU.subtract))
                v.tensor_copy(O_s1[:, g, 0:S], src[:, 0:S]).then_inc(sig("pooled"), 1)
            fence(dve, "dve", ("pe", "act", "pool"), 8)
            attention(*OD_U, O_P, O_y, lambda i: ())
            fence(dve, "dve", ("pe", "act", "pool"), 9)
            first_w_lo(4)
            mixer_residual("od_out0", 1, S, 9)
            norm(9, S, xT, summed=KT - 1)
            ffn(4, S, 1, 1)


def col(a):
    return np.ascontiguousarray(a.reshape(-1, P).T)


def pack(w):
    k, n = w.shape
    return w.reshape(k // P, P, n).transpose(1, 0, 2).reshape(P, -1)


def kernel(**inputs):
    import concourse.bacc as _bacc
    from concourse.bass_utils import run_bass_kernel_spmd as _run

    x = {k: np.asarray(v) for k, v in inputs.items()}
    w_in = x["w_in"][0]
    cat = np.concatenate

    def cols(a, b):
        return w_in[:, a:b]

    o_q, o_kv, o_gate, o_gq = 2048, 3072, 4608, 4656
    o_gv, o_og, o_lr, o_merge = 5680, 6704, 7728, 7744
    kv = [cols(o_kv + 256 * i, o_kv + 256 * (i + 1)) for i in range(6)]
    ch = [cols(0, 512), cols(512, 1024), cols(1024, 1536), cols(1536, 2048)]

    def merges(i):
        return [cat([cols(o_merge + D * i + 256 * c, o_merge + D * i + 256 * (c + 1)),
                     x["w_branch"][0, i][:, 256 * c:256 * (c + 1)]], axis=1) for c in range(4)]

    ch += merges(0)
    ch += [cols(o_gq, o_gq + 512), cols(o_gq + 512, o_gq + 1024), cols(o_gv, o_gv + 512),
           cols(o_gv + 512, o_gv + 1024), cols(o_og, o_og + 512), cols(o_og + 512, o_og + 1024)]
    ch += merges(2)
    ch += [cols(o_q, o_q + 512), cols(o_q + 512, o_q + 1024), cat([kv[0], kv[1]], 1), cat([kv[2], kv[4]], 1),
           cat([kv[3], kv[5]], 1)]
    chunks = [pack(w) for w in ch]
    chunks += [pack(x["cmp_w1"][0, i]) for i in range(2)]
    chunks += [pack(w) for w in merges(1)]
    chunks += [pack(x["w_out"][0][:, 512 * c:512 * (c + 1)]) for c in range(2)]
    ffs = [(x["w_ffn_in"][0], x["w_ffn_out"][0])] + [(x["ffn_w_gu_2"][l, i], x["ffn_w_down_2"][l, i])
                                                     for l in range(2) for i in range(2)]
    wf = np.zeros((5 * FFN_CHUNKS, P, W8), np.float32)
    c = 0
    for gu, dn in ffs:
        for k0, nf in GROUPS:
            for i in range(nf):
                a = (k0 + i) * P
                wf[c + i // 2, :, (i % 2) * HALF:(i % 2 + 1) * HALF] = pack(cat([gu[:, a:a + P],
                                                                             gu[:, FF + a:FF + a + P]], 1))
            c += nf // 2
            for i in range(4):
                w = nf * 256
                wf[c + i // 2, :, (i % 2) * w:(i % 2 + 1) * w] = pack(dn[k0 * P:(k0 + nf) * P, 256 * i:256 * (i + 1)])
            c += 2
    for l in range(2):
        chunks += [pack(x["ada_w_2"][l][:, 512 * c:512 * (c + 1)]) for c in range(18)]
    ev = x["ev_w_in_2"][0]
    chunks += [pack(ev[:, 0:512]), pack(ev[:, 1280:1792]), pack(ev[:, 768:1280])]
    chunks += [pack(x["ev_w_out_2"][0][:, 512 * c:512 * (c + 1)]) for c in range(2)]
    od = x["od_w_in_2"][0]
    chunks += [pack(od[:, 512 * c:512 * (c + 1)]) for c in (1, 2, 3, 0)]
    chunks += [pack(x["od_w_out_2"][0][:, 512 * c:512 * (c + 1)]) for c in range(2)]
    assert len(chunks) == W8_N, (len(chunks), W8_N)
    d = {"w8": np.stack(chunks)}
    d["wf"] = wf
    d["w4"] = np.stack([x["lru_w_gates"][0].transpose(2, 0, 1, 3).reshape(P, 2048), pack(ev[:, 512:768])])
    vec = np.zeros((P, VN), np.float32)

    def put(name, a):
        at, n = VOFF[name]
        a = np.asarray(a)
        vec[:a.shape[0], at:at + n] = a.reshape(a.shape[0], n)

    put("norm_g", col(x["norm_g"][0]))
    put("conv_w", col(x["conv_w"][0]))
    put("conv_b", col(x["conv_b"][0]))
    put("b_gates", col(x["lru_b_gates"][0]))
    put("lam", col(x["lru_lambda"][0]))
    put("gla_ba", col(x["gla_ba"][0]))
    put("gla_norm", col(x["gla_norm"][0]))
    put("c", np.stack([col(x["c_2"][0]), col(x["c_ctx_2"])], axis=2))
    put("ada_b", col(x["ada_b_2"]))
    put("norm_g2", col(x["norm_g_2"]))
    for name, src in (("qg_ev", "a_q_gain_2"), ("kg_ev", "a_k_gain_2"), ("qg_od", "d_q_gain_2"),
                      ("kg_od", "d_k_gain_2")):
        put(name, np.tile(x[src][0], 2)[:, None])
    put("c_scale", col(x["c_scale_2"][0]))
    put("sink", np.broadcast_to(x["a_sink_2"][0][None, :], (P, 8)))
    put("pos_k", col(x["cmp_pos"][0, 0]))
    put("pos_v", col(x["cmp_pos"][0, 1]))
    put("w2k", pack(np.tile(x["cmp_w2"][0, 0], (1, 2))))
    put("w2v", pack(x["cmp_w2"][0, 1]))
    order = np.arange(16).reshape(4, 2, 2).transpose(0, 2, 1).ravel()
    gate = cols(o_gate, o_gate + 48).reshape(D, 3, 16)[:, :, order].reshape(D, 48)
    put("w_small", pack(cat([gate, cols(o_lr, o_lr + 16)], 1)))
    put("wa2", x["gla_wa2"][0])
    d["vec"] = vec
    d["cst"], d["cst_od"] = constants()
    d["tbl"] = x["rel_table"][:, order]
    d["rpb"] = x["d_rpb_2"][0].reshape(120, 31)
    d["ev_small"] = cat([np.broadcast_to(x["b_v_gain_2"], (P, 512)),
                         np.repeat(x["b_bias_2"][0].reshape(4, 2, 128), 64, axis=1).transpose(1, 0, 2).reshape(P, 512),
                         x["b_ws_2"][0].transpose(2, 0, 1).reshape(P, 1024)], axis=1)
    d["pool_w"] = x["c_w_pool_2"][0].transpose(1, 0, 2).reshape(P, 512)
    d["x"] = x["x"][0].T.reshape(KT, P, S)
    d["ctx"] = x["ctx_2"][0].T.reshape(KT, P, CL)
    d = {k: np.ascontiguousarray(v) for k, v in d.items()}

    nc = _bacc.Bacc("TRN2", target_bir_lowering=False, num_devices=1)
    f32 = mybir.dt.float32
    aps = {k: nc.dram_tensor(f"in_{k}", v.shape, f32, kind="ExternalInput").ap() for k, v in d.items()}
    out = nc.dram_tensor("out_x", (KT, P, S), f32, kind="ExternalOutput").ap()
    build(nc, aps, out)
    r = _run(nc, [{f"in_{k}": v for k, v in d.items()}], core_ids=[0])
    y = np.asarray(r.results[0]["out_x"])
    return np.ascontiguousarray(y.reshape(D, S).T)[None]
```
